# Optimizing a Trainium2 kernel written in Bass

```python
import jax
import jax.numpy as jnp
from jax import lax
import numpy as np
import math

D_MODEL = 1024
BATCH = 1
SEQ = 256
DEPTH = 2

N_MIXERS = 4
GROUP_WIDTH = D_MODEL // N_MIXERS
HEADS = 4
HEAD_DIM = GROUP_WIDTH // HEADS
CONV_WIDTH = 3
SGU_CHUNK = 128
GLA_KEY_DIM = HEAD_DIM // 2
GLA_GATE_RANK = 16
GLA_GATE_NORMALIZER = 16.0
LA_CHUNK = 16
D_FF = 2816
N_EXPERTS = 8
TOP_K = 2
D_FF_EXPERT = 3584
N_MOD = 6
N_DENSE_LAYERS = (DEPTH + 1) // 2
N_MOE_LAYERS = DEPTH // 2
EPS = 1e-6
PROJ_SIZES = (
    GROUP_WIDTH, GROUP_WIDTH, GROUP_WIDTH,
    GROUP_WIDTH, GROUP_WIDTH,
    HEADS * GLA_KEY_DIM, HEADS * GLA_KEY_DIM, GROUP_WIDTH,
    GLA_GATE_RANK, GROUP_WIDTH,
    GROUP_WIDTH, GROUP_WIDTH, GROUP_WIDTH, GROUP_WIDTH,
)
IN_PROJ_WIDTH = sum(PROJ_SIZES)


def rms_norm(x, g):
    xf = x.astype(jnp.float32)
    y = xf * lax.rsqrt(jnp.mean(xf * xf, axis=-1, keepdims=True) + EPS)
    return y.astype(x.dtype) * g

def causal_depthwise_conv(x, w):
    s = x.shape[1]
    xp = jnp.pad(x, ((0, 0), (CONV_WIDTH - 1, 0), (0, 0)))
    return sum(xp[:, k:k + s] * w[k] for k in range(CONV_WIDTH))

def short_conv_mixer(b_gate, c_gate, x_in, w_conv):
    return b_gate * causal_depthwise_conv(c_gate * x_in, w_conv)

def spatial_gating_mixer(u, v, norm_g, w_s, b_s):
    bn, s, _ = v.shape
    n = s // SGU_CHUNK
    vf = v.astype(jnp.float32)
    mu = jnp.mean(vf, axis=-1, keepdims=True)
    var = jnp.mean(jnp.square(vf - mu), axis=-1, keepdims=True)
    vn = ((vf - mu) * lax.rsqrt(var + EPS)).astype(v.dtype) * norm_g
    vc = vn.reshape(bn, n, SGU_CHUNK, HEADS, HEAD_DIM)
    causal = jnp.tril(jnp.ones((SGU_CHUNK, SGU_CHUNK), dtype=bool))
    ws = jnp.where(causal[None], w_s, 0.0)
    mixed = jnp.einsum('hts,bnshd->bnthd', ws, vc) + b_s.T[None, None, :, :, None]
    return u * mixed.reshape(bn, s, GROUP_WIDTH)

def chunk_gated_linear_attention(q, k, v, log_a):
    bn, s, h, kd = q.shape
    vd = v.shape[-1]
    n = s // LA_CHUNK
    f32 = jnp.float32
    q, k, v, log_a = (t.astype(f32).reshape(bn, n, LA_CHUNK, h, t.shape[-1]) for t in (q, k, v, log_a))
    b = jnp.cumsum(log_a, axis=2)
    mid = LA_CHUNK // 2
    b_ref = b[:, :, mid:mid + 1]
    scores = jnp.einsum('bnihk,bnjhk->bnhij', q * jnp.exp(b - b_ref), k * jnp.exp(b_ref - b))
    causal = jnp.tril(jnp.ones((LA_CHUNK, LA_CHUNK), dtype=bool))
    scores = jnp.where(causal, scores, 0.0)
    o_intra = jnp.einsum('bnhij,bnjhv->bnihv', scores, v)
    b_last = b[:, :, -1:]
    k_upd = k * jnp.exp(b_last - b)
    decay = jnp.exp(b_last[:, :, 0])

    def step(state, xs):
        d, kc, vc = xs
        new_state = d[..., None] * state + jnp.einsum('bjhk,bjhv->bhkv', kc, vc)
        return new_state, state

    s0 = jnp.zeros((bn, h, kd, vd), f32)
    _, s_prev = lax.scan(step, s0, (jnp.moveaxis(decay, 1, 0), jnp.moveaxis(k_upd, 1, 0), jnp.moveaxis(v, 1, 0)))
    o_inter = jnp.einsum('bnihk,nbhkv->bnihv', q * jnp.exp(b), s_prev)
    return (o_intra + o_inter).reshape(bn, s, h, vd)

def gla_mixer(q, k, v, g_lowrank, r, w_gate, b_gate, norm_g):
    bn, s, _ = q.shape
    log_a = jax.nn.log_sigmoid((g_lowrank @ w_gate + b_gate).astype(jnp.float32)) / GLA_GATE_NORMALIZER
    o = chunk_gated_linear_attention(
        q.reshape(bn, s, HEADS, GLA_KEY_DIM) * (GLA_KEY_DIM ** -0.5),
        k.reshape(bn, s, HEADS, GLA_KEY_DIM),
        v.reshape(bn, s, HEADS, HEAD_DIM),
        log_a.reshape(bn, s, HEADS, GLA_KEY_DIM))
    o = rms_norm(o.astype(q.dtype), norm_g)
    return o.reshape(bn, s, GROUP_WIDTH) * jax.nn.silu(r)

def hgrn2_mixer(q, f_logit, i_in, g, lower_bound, norm_g):
    bn, s, _ = q.shape
    f = lower_bound + (1.0 - lower_bound) * jax.nn.sigmoid(f_logit.astype(jnp.float32))
    o = chunk_gated_linear_attention(
        q.reshape(bn, s, HEADS, HEAD_DIM),
        (1.0 - f).reshape(bn, s, HEADS, HEAD_DIM),
        i_in.reshape(bn, s, HEADS, HEAD_DIM),
        jnp.log(f).reshape(bn, s, HEADS, HEAD_DIM))
    o = rms_norm(o.astype(q.dtype), norm_g)
    return o.reshape(bn, s, GROUP_WIDTH) * jax.nn.silu(g)

def swiglu(x, w1, w3, w2):
    return (jax.nn.silu(x @ w1) * (x @ w3)) @ w2

def moe_swiglu(x, w_router, w1, w3, w2):
    bn, s, d = x.shape
    t = x.reshape(bn * s, d)
    logits = (t @ w_router).astype(jnp.float32)
    top_val, top_idx = lax.top_k(logits, TOP_K)
    top_w = jax.nn.softmax(top_val, axis=-1)
    combine = jnp.sum(jax.nn.one_hot(top_idx, N_EXPERTS, dtype=jnp.float32) * top_w[..., None], axis=1)
    out = jnp.zeros_like(t)
    for e in range(N_EXPERTS):
        out = out + combine[:, e:e + 1].astype(t.dtype) * swiglu(t, w1[e], w3[e], w2[e])
    return out.reshape(bn, s, d)

def first_inputs(seed: int = 0) -> dict:
    key = jax.random.key(seed)
    ks = jax.random.split(key, 25)
    f32 = jnp.float32

    def normal(k, shape, scale):
        return scale * jax.random.normal(k, shape, f32)

    def gain(k, shape):
        return 1.0 + normal(k, shape, 0.02)

    L = DEPTH
    return {
        "x": normal(ks[0], (BATCH, SEQ, D_MODEL), 1.0),
        "c": normal(ks[1], (BATCH, D_MODEL), 1.0),
        "norm_mix_g": gain(ks[2], (L, D_MODEL)),
        "norm_ffn_g": gain(ks[3], (L, D_MODEL)),
        "final_norm_g": gain(ks[4], (D_MODEL,)),
        "w_ada": normal(ks[5], (L, D_MODEL, N_MOD * D_MODEL), 0.5 * D_MODEL ** -0.5),
        "b_ada": normal(ks[6], (L, N_MOD * D_MODEL), 0.02),
        "w_in": normal(ks[7], (L, D_MODEL, IN_PROJ_WIDTH), D_MODEL ** -0.5),
        "w_out": normal(ks[8], (L, N_MIXERS * GROUP_WIDTH, D_MODEL), (N_MIXERS * GROUP_WIDTH) ** -0.5),
        "conv_w": normal(ks[9], (L, CONV_WIDTH, GROUP_WIDTH), CONV_WIDTH ** -0.5),
        "sgu_norm_g": gain(ks[10], (L, GROUP_WIDTH)),
        "sgu_w": normal(ks[11], (L, HEADS, SGU_CHUNK, SGU_CHUNK), SGU_CHUNK ** -0.5),
        "sgu_b": gain(ks[12], (L, HEADS, SGU_CHUNK)),
        "gla_w_gate": normal(ks[13], (L, GLA_GATE_RANK, HEADS * GLA_KEY_DIM), GLA_GATE_RANK ** -0.5),
        "gla_b_gate": normal(ks[14], (L, HEADS * GLA_KEY_DIM), 0.1),
        "gla_norm_g": gain(ks[15], (L, HEAD_DIM)),
        "hgrn_lower_bounds": normal(ks[16], (L, GROUP_WIDTH), 0.1),
        "hgrn_norm_g": gain(ks[17], (L, HEAD_DIM)),
        "ffn_w1": normal(ks[18], (N_DENSE_LAYERS, D_MODEL, D_FF), D_MODEL ** -0.5),
        "ffn_w3": normal(ks[19], (N_DENSE_LAYERS, D_MODEL, D_FF), D_MODEL ** -0.5),
        "ffn_w2": normal(ks[20], (N_DENSE_LAYERS, D_FF, D_MODEL), D_FF ** -0.5),
        "moe_router": normal(ks[21], (N_MOE_LAYERS, D_MODEL, N_EXPERTS), D_MODEL ** -0.5),
        "moe_w1": normal(ks[22], (N_MOE_LAYERS, N_EXPERTS, D_MODEL, D_FF_EXPERT), D_MODEL ** -0.5),
        "moe_w3": normal(ks[23], (N_MOE_LAYERS, N_EXPERTS, D_MODEL, D_FF_EXPERT), D_MODEL ** -0.5),
        "moe_w2": normal(ks[24], (N_MOE_LAYERS, N_EXPERTS, D_FF_EXPERT, D_MODEL), D_FF_EXPERT ** -0.5),
    }

def first_block(x, c, norm_mix_g, norm_ffn_g, final_norm_g, w_ada, b_ada, w_in, w_out, conv_w,
              sgu_norm_g, sgu_w, sgu_b, gla_w_gate, gla_b_gate, gla_norm_g, hgrn_lower_bounds,
              hgrn_norm_g, ffn_w1, ffn_w3, ffn_w2, moe_router, moe_w1, moe_w3, moe_w2):
    split_points = np.cumsum(PROJ_SIZES)[:-1].tolist()
    cond = jax.nn.silu(c)
    lb_cum = jnp.cumsum(jax.nn.softmax(hgrn_lower_bounds.astype(jnp.float32), axis=0), axis=0)
    lower_bounds = lb_cum - lb_cum[0]
    for layer in range(DEPTH):
        mod = cond @ w_ada[layer] + b_ada[layer]
        shift_m, scale_m, gate_m, shift_f, scale_f, gate_f = [m[:, None, :] for m in jnp.split(mod, N_MOD, axis=-1)]
        h = rms_norm(x, norm_mix_g[layer]) * (1.0 + scale_m) + shift_m
        (cb, cc, cx, su, sv, aq, ak, av, ag, ar, hq, hf, hi, hg) = jnp.split(h @ w_in[layer], split_points, axis=-1)
        y_conv = short_conv_mixer(cb, cc, cx, conv_w[layer])
        y_sgu = spatial_gating_mixer(su, sv, sgu_norm_g[layer], sgu_w[layer], sgu_b[layer])
        y_gla = gla_mixer(aq, ak, av, ag, ar, gla_w_gate[layer], gla_b_gate[layer], gla_norm_g[layer])
        y_hgrn = hgrn2_mixer(hq, hf, hi, hg, lower_bounds[layer], hgrn_norm_g[layer])
        mixed = jnp.concatenate([y_conv, y_sgu, y_gla, y_hgrn], axis=-1) @ w_out[layer]
        x = x + gate_m * mixed
        h = rms_norm(x, norm_ffn_g[layer]) * (1.0 + scale_f) + shift_f
        idx = layer // 2
        if layer % 2 == 0:
            y = swiglu(h, ffn_w1[idx], ffn_w3[idx], ffn_w2[idx])
        else:
            y = moe_swiglu(h, moe_router[idx], moe_w1[idx], moe_w3[idx], moe_w2[idx])
        x = x + gate_f * y
    return rms_norm(x, final_norm_g)


N_EVEN = (DEPTH + 1) // 2
N_ODD = DEPTH // 2
RMS_EPS = 1e-6

GDN_HEADS = 4
GDN_DK = 128
GDN_DV = 128
GDN_QK_W = GDN_HEADS * GDN_DK
GDN_V_W = GDN_HEADS * GDN_DV
GDN_CONV = 4
GDN_CHUNK = 64

POOL_WINDOWS = (2, 4, 8, 16)
POOL_GROUPS = len(POOL_WINDOWS)
POOL_GROUP_W = 128
POOL_W = POOL_GROUPS * POOL_GROUP_W

EVEN_QKV = 2 * GDN_QK_W + GDN_V_W
EVEN_IN = EVEN_QKV + GDN_V_W + 2 * GDN_HEADS + POOL_W
EVEN_OUT = GDN_V_W + POOL_W

DIL_PATTERNS = ((128, 1), (512, 4), (2048, 16))
ATT_GROUPS = len(DIL_PATTERNS)
ATT_HEADS = 8
ATT_DH = 128
ATT_W = ATT_HEADS * ATT_DH
ODD_IN = ATT_GROUPS * 3 * ATT_W
ATT_BLOCK = 128

FFN_CONV = 3


def rms_norm_2(x, gain):
    xf = x.astype(jnp.float32)
    y = xf * lax.rsqrt(jnp.mean(xf * xf, axis=-1, keepdims=True) + RMS_EPS)
    return (y * gain.astype(jnp.float32)).astype(x.dtype)

def l2_norm(x):
    xf = x.astype(jnp.float32)
    return xf * lax.rsqrt(jnp.sum(xf * xf, axis=-1, keepdims=True) + RMS_EPS)

def causal_dwconv(x, w):
    K, C = w.shape
    return lax.conv_general_dilated(
        x, w[:, None, :].astype(x.dtype), window_strides=(1,), padding=[(K - 1, 0)],
        dimension_numbers=("NWC", "WIO", "NWC"), feature_group_count=C)

def gated_delta_rule(q, k, v, g, beta):
    B, T, H, dk = q.shape
    dv = v.shape[-1]
    C = GDN_CHUNK
    N = T // C
    f32 = jnp.float32

    def chunks(t):
        return t.astype(f32).reshape(B, N, C, H, -1).transpose(0, 3, 1, 2, 4)

    q = chunks(q) * (dk ** -0.5)
    k = chunks(k)
    v = chunks(v)
    g = g.astype(f32).reshape(B, N, C, H).transpose(0, 3, 1, 2)
    beta = beta.astype(f32).reshape(B, N, C, H).transpose(0, 3, 1, 2)
    gc = jnp.cumsum(g, axis=-1)

    idx = jnp.arange(C)
    causal = idx[:, None] >= idx[None, :]
    strict = idx[:, None] > idx[None, :]
    diff = gc[..., :, None] - gc[..., None, :]
    decay = jnp.where(causal, jnp.exp(jnp.where(causal, diff, 0.0)), 0.0)

    kb = k * beta[..., None]
    L = jnp.where(strict, jnp.einsum("bhncd,bhnsd->bhncs", kb, k) * decay, 0.0)
    rhs = jnp.concatenate([v * beta[..., None], kb * jnp.exp(gc)[..., None]], axis=-1)
    uw = lax.linalg.triangular_solve(L, rhs, left_side=True, lower=True,
                                     unit_diagonal=True)
    u, w = uw[..., :dv], uw[..., dv:]

    intra = jnp.where(causal, jnp.einsum("bhncd,bhnsd->bhncs", q, k) * decay, 0.0)
    qg = q * jnp.exp(gc)[..., None]
    kdec = k * jnp.exp(gc[..., -1:] - gc)[..., None]
    glast = jnp.exp(gc[..., -1])

    def step(S, xs):
        qg_i, kdec_i, u_i, w_i, intra_i, gl_i = xs
        v_new = u_i - jnp.einsum("bhck,bhkv->bhcv", w_i, S)
        o_i = (jnp.einsum("bhck,bhkv->bhcv", qg_i, S)
               + jnp.einsum("bhcs,bhsv->bhcv", intra_i, v_new))
        S = S * gl_i[..., None, None] + jnp.einsum("bhck,bhcv->bhkv", kdec_i, v_new)
        return S, o_i

    xs = tuple(jnp.moveaxis(t, 2, 0) for t in (qg, kdec, u, w, intra, glast))
    S0 = jnp.zeros((B, H, dk, dv), f32)
    _, o = lax.scan(step, S0, xs)
    return o.transpose(1, 0, 3, 2, 4).reshape(B, T, H, dv)

def multiscale_pool(p, pool_w, pool_scale):
    B, T, _ = p.shape
    pf = p.astype(jnp.float32).reshape(B, T, POOL_GROUPS, POOL_GROUP_W)
    csum = jnp.cumsum(pf, axis=1)
    t1 = jnp.arange(1, T + 1, dtype=jnp.float32)
    pooled = []
    for gi, win in enumerate(POOL_WINDOWS):
        cg = csum[:, :, gi]
        lag = jnp.pad(cg, ((0, 0), (win, 0), (0, 0)))[:, :T]
        cnt = jnp.minimum(t1, float(win))[None, :, None]
        pooled.append((cg - lag) / cnt)
    pooled = jnp.stack(pooled, axis=2) - pf
    y = jnp.einsum("btgc,gcd->btgd", pooled, pool_w.astype(jnp.float32))
    return (y.reshape(B, T, POOL_W) * pool_scale.astype(jnp.float32)).astype(p.dtype)

def even_mixer(h, w_in, w_out, conv_w, a_log, dt_bias, gdn_norm, pool_w, pool_scale):
    B, T, _ = h.shape
    proj = h @ w_in
    i1 = EVEN_QKV
    i2 = i1 + GDN_V_W
    i3 = i2 + GDN_HEADS
    i4 = i3 + GDN_HEADS
    qkv, z, b_raw, a_raw, pool_in = jnp.split(proj, [i1, i2, i3, i4], axis=-1)

    qkv = jax.nn.silu(causal_dwconv(qkv, conv_w))
    q, k, v = jnp.split(qkv, [GDN_QK_W, 2 * GDN_QK_W], axis=-1)
    q = l2_norm(q.reshape(B, T, GDN_HEADS, GDN_DK))
    k = l2_norm(k.reshape(B, T, GDN_HEADS, GDN_DK))
    v = v.reshape(B, T, GDN_HEADS, GDN_DV)
    beta = jax.nn.sigmoid(b_raw.astype(jnp.float32))
    g = -jnp.exp(a_log.astype(jnp.float32)) * jax.nn.softplus(
        a_raw.astype(jnp.float32) + dt_bias.astype(jnp.float32))
    o = gated_delta_rule(q, k, v, g, beta)
    o = rms_norm_2(o, gdn_norm) * jax.nn.silu(
        z.astype(jnp.float32).reshape(B, T, GDN_HEADS, GDN_DV))
    o_a = o.reshape(B, T, GDN_V_W).astype(h.dtype)

    o_b = multiscale_pool(pool_in, pool_w, pool_scale)
    return jnp.concatenate([o_a, o_b], axis=-1) @ w_out

def alibi_slopes(n_heads):
    return jnp.exp2(-8.0 * jnp.arange(1, n_heads + 1, dtype=jnp.float32) / n_heads)

def dilated_band_attention(q, k, v, dil, n_back, slopes):
    B, T, H, dh = q.shape
    L = T // dil
    nb = -(-L // ATT_BLOCK)
    Lp = nb * ATT_BLOCK

    def to_sub(t):
        t = t.reshape(B, L, dil, H, dh).transpose(0, 2, 3, 1, 4)
        t = jnp.pad(t, ((0, 0), (0, 0), (0, 0), (0, Lp - L), (0, 0)))
        return t.reshape(B, dil, H, nb, ATT_BLOCK, dh)

    def band(t):
        prev = jnp.pad(t, ((0, 0), (0, 0), (0, 0), (1, 0), (0, 0), (0, 0)))[:, :, :, :nb]
        return jnp.concatenate([prev, t], axis=4)

    qb = to_sub(q)
    kb = band(to_sub(k))
    vb = band(to_sub(v))

    a = jnp.arange(ATT_BLOCK)[:, None]
    j = jnp.arange(2 * ATT_BLOCK)[None, :]
    rel = ATT_BLOCK + a - j
    blk = jnp.arange(nb)[:, None, None]
    mask = (rel >= 0) & (rel <= n_back) & ((j >= ATT_BLOCK) | (blk > 0))
    bias = -(slopes * dil)[:, None, None, None] * rel.astype(jnp.float32)

    s = jnp.einsum("brhnqd,brhnkd->brhnqk", qb, kb) + bias
    s = jnp.where(mask, s, -jnp.inf)
    m = jnp.max(s, axis=-1, keepdims=True)
    p = jnp.exp(s - m)
    l = jnp.sum(p, axis=-1, keepdims=True)
    o = jnp.einsum("brhnqk,brhnkd->brhnqd", p, vb) / l
    lse = m + jnp.log(l)

    def from_sub(t):
        t = t.reshape(B, dil, H, Lp, -1)[:, :, :, :L]
        return t.transpose(0, 3, 1, 2, 4).reshape(B, T, H, -1)

    return from_sub(o), from_sub(lse)[..., 0]

def odd_mixer(h, w_in, w_out, q_norm, k_norm):
    B, T, _ = h.shape
    slopes = alibi_slopes(ATT_HEADS)
    outs, lses = [], []
    for gi, (window, dil) in enumerate(DIL_PATTERNS):
        cols = w_in[:, gi * 3 * ATT_W:(gi + 1) * 3 * ATT_W]
        proj = (h @ cols).astype(jnp.float32).reshape(B, T, 3, ATT_HEADS, ATT_DH)
        q = rms_norm_2(proj[:, :, 0], q_norm) * (ATT_DH ** -0.5)
        k = rms_norm_2(proj[:, :, 1], k_norm)
        v = proj[:, :, 2]
        o, lse = dilated_band_attention(q, k, v, dil, window // dil, slopes)
        outs.append(o)
        lses.append(lse)
    wts = jax.nn.softmax(jnp.stack(lses), axis=0)
    o = jnp.sum(wts[..., None] * jnp.stack(outs), axis=0)
    return o.reshape(B, T, ATT_W).astype(h.dtype) @ w_out

def conv_ffn(h, w_up, conv_w, conv_b, w_down):
    up = h @ w_up
    gate, val = jnp.split(up, 2, axis=-1)
    gate = causal_dwconv(gate, conv_w) + conv_b
    return (jax.nn.silu(gate) * val) @ w_down

def second_inputs(seed: int = 0) -> dict:
    key = jax.random.key(seed)
    ks = jax.random.split(key, 24)
    f32 = jnp.float32
    D = D_MODEL

    def nrm(k, shape, s):
        return jax.random.normal(k, shape, f32) * s

    dt = jnp.exp(jax.random.uniform(ks[10], (N_EVEN, GDN_HEADS), f32,
                                    math.log(1e-3), math.log(1e-1)))
    return {
        "x": nrm(ks[0], (BATCH, SEQ, D), 1.0),
        "c": nrm(ks[1], (BATCH, D), 1.0),
        "ada_w": nrm(ks[2], (DEPTH, D, 6 * D), 0.5 * D ** -0.5),
        "ada_b": nrm(ks[3], (DEPTH, 6 * D), 0.01),
        "norm_mix": 1.0 + nrm(ks[4], (DEPTH, D), 0.02),
        "norm_ffn": 1.0 + nrm(ks[5], (DEPTH, D), 0.02),
        "ev_w_in": nrm(ks[6], (N_EVEN, D, EVEN_IN), D ** -0.5),
        "ev_w_out": nrm(ks[7], (N_EVEN, EVEN_OUT, D), EVEN_OUT ** -0.5),
        "gdn_conv_w": nrm(ks[8], (N_EVEN, GDN_CONV, EVEN_QKV), GDN_CONV ** -0.5),
        "gdn_a_log": jnp.log(jax.random.uniform(ks[9], (N_EVEN, GDN_HEADS), f32, 1.0, 16.0)),
        "gdn_dt_bias": dt + jnp.log(-jnp.expm1(-dt)),
        "gdn_norm": 1.0 + nrm(ks[11], (N_EVEN, GDN_DV), 0.02),
        "pool_w": nrm(ks[12], (N_EVEN, POOL_GROUPS, POOL_GROUP_W, POOL_GROUP_W), POOL_GROUP_W ** -0.5),
        "pool_scale": 1.0 + nrm(ks[13], (N_EVEN, POOL_W), 0.1),
        "od_w_in": nrm(ks[14], (N_ODD, D, ODD_IN), D ** -0.5),
        "od_w_out": nrm(ks[15], (N_ODD, ATT_W, D), ATT_W ** -0.5),
        "att_q_norm": 1.0 + nrm(ks[16], (N_ODD, ATT_DH), 0.02),
        "att_k_norm": 1.0 + nrm(ks[17], (N_ODD, ATT_DH), 0.02),
        "ffn_w_up": nrm(ks[18], (DEPTH, D, 2 * D_FF), D ** -0.5),
        "ffn_conv_w": nrm(ks[19], (DEPTH, FFN_CONV, D_FF), FFN_CONV ** -0.5),
        "ffn_conv_b": nrm(ks[20], (DEPTH, D_FF), 0.01),
        "ffn_w_down": nrm(ks[21], (DEPTH, D_FF, D), D_FF ** -0.5),
    }

def second_block(x, c, ada_w, ada_b, norm_mix, norm_ffn, ev_w_in, ev_w_out, gdn_conv_w,
              gdn_a_log, gdn_dt_bias, gdn_norm, pool_w, pool_scale, od_w_in, od_w_out,
              att_q_norm, att_k_norm, ffn_w_up, ffn_conv_w, ffn_conv_b, ffn_w_down):
    cs = jax.nn.silu(c)
    for i in range(DEPTH):
        mod = (cs @ ada_w[i] + ada_b[i])[:, None, :]
        sh_m, sc_m, g_m, sh_f, sc_f, g_f = jnp.split(mod, 6, axis=-1)

        hm = rms_norm_2(x, norm_mix[i]) * (1.0 + sc_m) + sh_m
        if i % 2 == 0:
            e = i // 2
            y = even_mixer(hm, ev_w_in[e], ev_w_out[e], gdn_conv_w[e], gdn_a_log[e],
                           gdn_dt_bias[e], gdn_norm[e], pool_w[e], pool_scale[e])
        else:
            o = i // 2
            y = odd_mixer(hm, od_w_in[o], od_w_out[o], att_q_norm[o], att_k_norm[o])
        x = x + g_m * y

        hf = rms_norm_2(x, norm_ffn[i]) * (1.0 + sc_f) + sh_f
        x = x + g_f * conv_ffn(hf, ffn_w_up[i], ffn_conv_w[i], ffn_conv_b[i], ffn_w_down[i])
    return x


def setup_inputs(seed=0):
    out = dict(first_inputs(seed))
    for name, value in second_inputs(seed + 1).items():
        if name != "x":
            out[name + "_2"] = value
    return out


def reference(
    x, c, norm_mix_g, norm_ffn_g, final_norm_g, w_ada, b_ada, w_in, w_out, conv_w, sgu_norm_g,
    sgu_w, sgu_b, gla_w_gate, gla_b_gate, gla_norm_g, hgrn_lower_bounds, hgrn_norm_g, ffn_w1,
    ffn_w3, ffn_w2, moe_router, moe_w1, moe_w3, moe_w2, c_2, ada_w_2, ada_b_2, norm_mix_2,
    norm_ffn_2, ev_w_in_2, ev_w_out_2, gdn_conv_w_2, gdn_a_log_2, gdn_dt_bias_2, gdn_norm_2,
    pool_w_2, pool_scale_2, od_w_in_2, od_w_out_2, att_q_norm_2, att_k_norm_2, ffn_w_up_2,
    ffn_conv_w_2, ffn_conv_b_2, ffn_w_down_2,
):
    x = first_block(
        x, c, norm_mix_g, norm_ffn_g, final_norm_g, w_ada, b_ada, w_in, w_out, conv_w,
        sgu_norm_g, sgu_w, sgu_b, gla_w_gate, gla_b_gate, gla_norm_g, hgrn_lower_bounds,
        hgrn_norm_g, ffn_w1, ffn_w3, ffn_w2, moe_router, moe_w1, moe_w3, moe_w2,
    )
    return second_block(
        x, c_2, ada_w_2, ada_b_2, norm_mix_2, norm_ffn_2, ev_w_in_2, ev_w_out_2, gdn_conv_w_2,
        gdn_a_log_2, gdn_dt_bias_2, gdn_norm_2, pool_w_2, pool_scale_2, od_w_in_2, od_w_out_2,
        att_q_norm_2, att_k_norm_2, ffn_w_up_2, ffn_conv_w_2, ffn_conv_b_2, ffn_w_down_2,
    )


_drawn_inputs = setup_inputs


def setup_inputs(seed=0):
    import zlib

    import numpy as np

    out = dict(_drawn_inputs(seed))
    spreads = {}
    factors = {'norm_mix_g': 2.978,
     'norm_ffn_g': 3.814,
     'final_norm_g': 2.713,
     'sgu_norm_g': 8.0,
     'sgu_b': 8.0,
     'gla_b_gate': 6.918,
     'gla_norm_g': 8.0,
     'hgrn_lower_bounds': 5.284,
     'hgrn_norm_g': 8.0,
     'ada_b_2': 3.76,
     'norm_mix_2': 8.0,
     'norm_ffn_2': 6.972,
     'gdn_norm_2': 8.0,
     'pool_scale_2': 2.834,
     'att_q_norm_2': 8.0,
     'att_k_norm_2': 21.583,
     'ffn_conv_b_2': 26.535}
    for name, (base, spread) in spreads.items():
        noise = np.random.default_rng([zlib.crc32(name.encode()), seed]).standard_normal(out[name].shape)
        drawn = base * np.exp(spread * noise) if base else spread * noise
        out[name] = jnp.asarray(drawn.astype(out[name].dtype))
    for name, factor in factors.items():
        out[name] = (out[name] * factor).astype(out[name].dtype)
    return out
```

```python
from contextlib import ExitStack

import concourse.bass as bass
import numpy as np
from concourse import mybir

F32 = mybir.dt.float32
ALU = mybir.AluOpType
ACT = mybir.ActivationFunctionType
AX = mybir.AxisListType.X

P = 128
D = 1024
KD = D // P
T = 256
NT = T // P
EPS = 1e-6
SLOT = 2048
COLS = 256
RING = 6
MODS = 6 * KD
D_FF = 2816
D_FFE = 3584
EXPERTS = 8
DENSE_CHUNKS = D_FF // COLS
EXPERT_CHUNKS = D_FFE // COLS
MOE_CHUNKS = EXPERTS * EXPERT_CHUNKS
FF_TILES = D_FF // P
LA = 16
NCH = T // LA
HEADS = 4
ATT_HEADS = 8
ATT_GROUPS = 3
LEVELS = 7
NEG = -1e30

HF, HQ, HI, AQK, AV, SV, SU, CC, CX, CB, HG, AR = range(12)
TOKEN_MAJOR = (HI, AV, SV)
COLUMN_OF = {HF: 2320, HQ: 2064, HI: 2576, AQK: 1280, AV: 1536, SV: 1024, SU: 768, CC: 256, CX: 512, CB: 0,
             HG: 2832, AR: 1808}
GLOW_COLUMN = 1792
GDN_QKV, GDN_Z, GDN_POOL = 6, 2, 2
PLAN = ("first0", "first1", "even", "odd")
LAYER = {"first0": 0, "first1": 1, "even": 0, "odd": 1}


class Steps:

    def __init__(self, sem, names):
        self.sem, self.names, self.count = sem, names.split(), 0

    def step(self, name):
        assert self.names[self.count % len(self.names)] == name, (name, self.names[self.count % len(self.names)])
        self.count += 1
        return self.sem, 1

    def at(self, name, use):
        return self.sem, use * len(self.names) + self.names.index(name) + 1


def ffn_slots(first, chunks):
    def up(c):
        return first + 3 * c - 1

    def down(c):
        return first + 3 * c + 4
    return up, down, first, first + 3 * chunks - 1


def stream_plan(plan):
    at, place = 0, {}

    def put(name, n):
        nonlocal at
        place[name] = at
        at += n
    put("mod0", 2 * KD * P // COLS)
    for n, kind in enumerate(plan):
        mods = (MODS if n + 1 < len(plan) else MODS - 2 * KD) * P // COLS
        if kind.startswith("first"):
            put(f"in{n}", 12)
            put(f"mod{n + 1}", mods)
        elif kind == "even":
            put(f"in{n}", GDN_QKV + GDN_Z + GDN_POOL)
            put(f"mod{n + 1}", mods)
        else:
            put(f"mod{n + 1}", mods)
            put(f"in{n}", ATT_HEADS // 2 * ATT_GROUPS * 3)
        put(f"out{n}", D // COLS)
        put(f"ffn{n}", 3 * (MOE_CHUNKS if kind == "first1" else DENSE_CHUNKS))
    place["end"] = at
    return place


def constant_columns():
    r = np.arange(P)
    row, col = r[:, None], r[None, :]
    out = {
        "ident": (row == col), "ones": np.ones((P, P)), "half_ones": (row // 64 == col // 64),
        "upto": (row <= col), "before": (row < col),
        "same_chunk": (row // LA == col // LA) & (row <= col),
        "restart": np.tile((np.arange(2 * T) % LA != 0), (P, 1)),
        "chunk_of": (row // LA == np.arange(P // LA)[None, :]),
        "levels": np.concatenate([((col >> l) & 1 == 1) & (row >> l == (col >> l) - 1) for l in range(LEVELS)], 1),
    }
    rel = []
    for qt in range(NT):
        for dil in (1, 4, 16):
            d = (qt * P + row) - np.arange((qt + 1) * P)[None, :]
            ok = (d >= 0) & (d % dil == 0) & (d <= P * dil)
            rel.append(np.where(ok, -d.astype(np.float64), NEG))
    out["distance"] = np.concatenate(rel, 1)
    out["per_count"] = np.tile(np.concatenate([1.0 / np.minimum(np.arange(1, T + 1), w) for w in (2, 4, 8, 16)]), (P, 1))
    e = np.arange(EXPERTS)
    out["lower_expert"] = np.tile((e[None, :] < e[:, None]).reshape(-1), (P, 1))
    return {k: np.ascontiguousarray(v, np.float32) for k, v in out.items()}


PARAM_COLUMNS = {
    "c": KD, "c_2": KD, "norm_mix_g": 2 * KD, "norm_ffn_g": 2 * KD, "final_norm_g": KD, "b_mod": 4 * MODS,
    "norm_mix_2": 2 * KD, "norm_ffn_2": 2 * KD, "conv_w": 2 * 6, "sgu_norm_g": 2 * 256,
    "sgu_w": 2 * 512, "sgu_b": 2 * 256, "w_glow": 2 * KD * 16, "gla_w_gate": 2 * P, "gla_b_gate": 2,
    "gla_norm_g": 2, "hgrn_norm_g": 2, "hgrn_lower_bounds": 4, "moe_router": KD * EXPERTS,
    "w_ab": KD * 8, "gdn_conv_w_2": 12 * 4, "gdn_a_log_2": 4, "gdn_dt_bias_2": 4, "gdn_norm_2": 1,
    "pool_w_2": 4 * P, "pool_scale_2": 4, "ffn_conv_w_2": 2 * FF_TILES * 3, "ffn_conv_b_2": 2 * FF_TILES,
    "att_q_norm_2": 1, "att_k_norm_2": 1,
}


def columns_of(widths):
    at, out = 0, {}
    for name, n in widths.items():
        out[name] = (at, n)
        at += n
    return out, at



def build_program(nc, x_in, params_in, consts_in, stream_in, out, plan=PLAN):
    place = stream_plan(plan)
    total_slots = place["end"]
    const_at, const_n = columns_of({k: v.shape[1] for k, v in constant_columns().items()})
    param_at, param_n = columns_of(PARAM_COLUMNS)
    firsts = [n for n, kind in enumerate(plan) if kind.startswith("first")]

    with ExitStack() as ctx:
        def sb(name, shape):
            return ctx.enter_context(nc.sbuf_tensor(name, shape, F32))

        def sem(name):
            return ctx.enter_context(nc.semaphore(name))

        def steps(name, names):
            return Steps(sem(name), names)

        ring = sb("ring", [P, RING, SLOT])
        xT = sb("xT", [P, KD, T])
        hT = sb("hT", [P, KD, T])
        yT = sb("yT", [P, KD, T])
        proj = sb("proj", [P, 12, 2, T])
        pflat = proj[:, :, :, :].rearrange("p a b t -> p (a b t)")
        consts = sb("consts", [P, const_n])
        params = sb("params", [P, param_n])
        mod = sb("mod", [P, 4 * MODS])
        cond = sb("cond", [P, 2, KD])
        rstd = sb("rstd", [P, T])
        gain = sb("gain", [P, KD])
        lbs = sb("lbs", [P, 2, 2, 2])
        lbw = sb("lbw", [P, 5, 2])
        ff_silu = sb("ff_silu", [P, 4, T])
        ff_mid = sb("ff_mid", [P, 4, T])
        ff_hid = sb("ff_hid", [P, 4, T])
        work_n = 16890
        work = sb("work", [P, work_n])

        banks = [ctx.enter_context(nc.psum_tensor(f"bank{i}", [P, 512], F32)) for i in range(6)]
        pair = ctx.enter_context(nc.psum_tensor("bank67", [P, 1024], F32))

        def bank(i, a=0, b=512):
            return banks[i][:, a:b] if i < 6 else pair[:, 512 * (i - 6) + a:512 * (i - 6) + b]

        def const(name):
            a, n = const_at[name]
            return consts[:, a:a + n]

        def param(name, layer=0, layers=1):
            a, n = param_at[name]
            n //= layers
            return params[:, a + layer * n:a + (layer + 1) * n]

        taken = [0]

        def take(n):
            taken[0] += n
            assert taken[0] <= work_n, taken[0]
            return work[:, taken[0] - n:taken[0]]

        gb = take(T)
        ge = take(4 * T).rearrange("p (a t) -> p a t", a=4)
        gz, gt = ge[:, 0, :], ge[:, 1, :]
        gk = take(2 * T).rearrange("p (a t) -> p a t", a=2)
        gdecay = take(NCH)
        gq = take(4 * T).rearrange("p (h t) -> p h t", h=4)
        gqe = take(4 * T).rearrange("p (h t) -> p h t", h=4)
        hb, hkey = take(2 * T), take(2 * T)
        he = take(4 * 2 * T).rearrange("p (a n) -> p a n", a=4)
        hz, hf = he[:, 0, :], he[:, 1, :]
        hk = take(4 * T).rearrange("p (a n) -> p a n", a=2)
        hdecay = take(2 * NCH)
        hq = take(4 * T).rearrange("p (f h t) -> p f h t", f=2, h=2)
        hqe = take(4 * T).rearrange("p (f h t) -> p f h t", f=2, h=2)
        v_chunks = hT[:, :, :].rearrange("p k t -> p (k t)")
        state = take(NCH * T)
        hd = state[:, 0:4 * T].rearrange("p (a n) -> p a n", a=2)
        gd = state[:, 4 * T:6 * T].rearrange("p (a t) -> p a t", a=2)
        ku_tok = take(2 * T)
        glow = ku_tok[:, 0:T]
        sgu_w = take(4 * P).rearrange("p (h t) -> p h t", h=HEADS)
        sgu_s = take(8)
        scores = ff_silu[:, :, :].rearrange("p a t -> p (a t)").rearrange("p (t n) -> p t n", t=NT)
        gates = ff_mid[:, :, :].rearrange("p a t -> p (a t)").rearrange("p (m n) -> p m n", m=2)
        osq = ff_hid[:, 0:2, :].rearrange("p a t -> p (a t)")
        orn = ff_hid[:, 2:4, :].rearrange("p a t -> p (a t)")
        vn = take(2 * T).rearrange("p (t d) -> p t d", t=NT)
        cv = take(2 * T).rearrange("p (f t) -> p f t", f=2)
        cacc = take(2 * T).rearrange("p (f t) -> p f t", f=2)
        used = [taken[0]]
        taken[0] = 0
        logits = take(NT * 8).rearrange("p (t e) -> p t e", t=NT)
        rk_gt = take(64).rearrange("p (a b) -> p a b", a=8)
        rk_eq = take(64).rearrange("p (a b) -> p a b", a=8)
        rank = take(NT * 8).rearrange("p (t e) -> p t e", t=NT)
        top = take(NT)
        den = take(NT)
        comb = take(NT * 8).rearrange("p (t e) -> p t e", t=NT)
        comb_b = take(EXPERTS * NT * P).rearrange("p (e t m) -> p e t m", e=EXPERTS, t=NT)
        comb_row = take(EXPERTS * T).rearrange("p (e t) -> p e t", e=EXPERTS)
        taken[0] = 0
        qkv = take(12 * T).rearrange("p (n t) -> p n t", n=12)
        l2 = take(8 * T)
        ab = take(NT * 8).rearrange("p (t e) -> p t e", t=NT)
        abt = take(NT * 8).rearrange("p (t e) -> p t e", t=NT)
        beta, gdec, anex, gccol, egc, kdf, bege = take(8), take(8), take(4), take(8), take(8), take(8), take(8)
        spread = take(2 * 8 * P).rearrange("p (a n m) -> p a n m", a=2, n=8)
        dec = take(8 * P)
        decs = take(8 * P)
        egrow = take(4 * P)
        qg = take(4 * P)
        kb = take(8 * P).rearrange("p (t n) -> p t n", t=NT)
        LT = take(8 * P).rearrange("p (t n) -> p t n", t=NT)
        PT = take(8 * P).rearrange("p (t n) -> p t n", t=NT)
        vb = take(8 * P)
        kbe, kdec = take(4 * P), take(4 * P)
        poolb = [ff_hid[:, :, :], pflat[:, 5120:6144].rearrange("p (n t) -> p n t", n=4)]
        X = pflat[:, 0:1024].rearrange("p (t n) -> p t n", t=NT)
        XT = pflat[:, 1024:2048].rearrange("p (t n) -> p t n", t=NT)
        Y = pflat[:, 2048:3072].rearrange("p (t n) -> p t n", t=NT)
        poolx = pflat[:, 4096:5120].rearrange("p (n t) -> p n t", n=4)
        MT = ff_silu[:, :, :].rearrange("p a t -> p (a t)").rearrange("p (t n) -> p t n", t=NT)
        vnew = l2[:, 0:1024].rearrange("p (t n) -> p t n", t=NT)
        wTn, S1 = l2[:, 1024:1536], l2[:, 1536:2048]
        zsilu = ff_mid[:, :, :].rearrange("p a t -> p (a t)")
        gosq = spread[:, 0, :, :].rearrange("p n m -> p (n m)")
        gorn = spread[:, 1, :, :].rearrange("p n m -> p (n m)")
        used.append(taken[0])
        taken[0] = 0
        qraw = take(2 * 512).rearrange("p (a n) -> p a n", a=2)
        qsq = take(2 * 512).rearrange("p (a n) -> p a n", a=2)
        qrn = take(2 * 512).rearrange("p (a n) -> p a n", a=2)
        qk = pflat[:, 0:6144].rearrange("p (b a g h t) -> p b a g h t", b=2, a=2, g=3, h=2)
        vtok = take(2 * 3 * 512).rearrange("p (b g t d) -> p b g t d", b=2, g=3, t=2)
        logit = take(2 * 768).rearrange("p (a n) -> p a n", a=2)
        prob = take(2 * 768).rearrange("p (a n) -> p a n", a=2)
        probT = take(2 * 768).rearrange("p (a n m) -> p a n m", a=2, n=6)
        top_q, neg_q, sum_q, inv_q = take(16), take(16), take(16), take(16)
        qgain = take(1)

        weights_here = [sem(f"weights_here{i}") for i in range(RING)]
        weights_used = sem("weights_used")
        x_here, params_here, consts_here, stored = sem("x_here"), sem("params_here"), sem("consts_here"), sem("stored")
        cond_act = steps("cond_act", "cond")
        mod_vec = steps("mod_vec", "mod")
        x_vec = steps("x_vec", "x")
        norm_act = steps("norm_act", "squares root")
        norm_pe = steps("norm_pe", "sum")
        norm_vec = steps("norm_vec", "gain rstd " + " ".join(f"s{k}" for k in range(KD)))
        shift_act = steps("shift_act", " ".join(f"h{k}" for k in range(KD)))
        proj_act = steps("proj_act", "p")
        ffn_half = sem("ffn_half")
        ffn_mid = sem("ffn_mid")
        ffn_silu = sem("ffn_silu")
        ffn_hid = sem("ffn_hid")
        ffn_conv = sem("ffn_conv")
        zero_pool = steps("zero_pool", "zero")
        lb_vec = steps("lb_vec", "max d sum inv lb om")
        lb_act = steps("lb_act", "exp")
        glow_pe = steps("glow_pe", "glow z")
        gla_act = steps("gla_act", "glow t1 ln exps gate")
        gla_vec = steps("gla_vec", "z abs min run dist ku")
        hgrn_act = steps("hgrn_act", "e lnf exps gate")
        hgrn_vec = steps("hgrn_vec", "add sig f key run dist ku")
        v_pool = steps("v_pool", "vg0 vg1 vh0 vh1")
        la_pe = steps("la_pe", " ".join(f"{n}{m}" for m in "gh" for n in ("tr", "sa", "sb", "u0", "u1", "o", "ms")))
        la_act = steps("la_act", " ".join(f"{n}{m}" for m in "gh" for n in ("ku", "osq", "root")))
        la_vec = steps("la_vec", " ".join(f"{n}{m}" for m in "gh" for n in (
            ["sa", "sb"] + [f"st{c}" for c in range(1, NCH)] + ["rn", "on", "y"])))
        sgu_pool = steps("sgu_pool", "w")
        sgu_act = steps("sgu_act", "sq root")
        sgu_vec = steps("sgu_vec", "sum mu d rs vn mix y")
        sgu_pe = steps("sgu_pe", "mix")
        conv_vec = steps("conv_vec", "cv c0 c1 c2 y")
        moe_pe = steps("moe_pe", "logits rows")
        moe_act = steps("moe_act", "exp rows")
        moe_vec = steps("moe_vec", "copy max neg " + " ".join(f"gt{t} eq{t} low{t} sum{t} rk{t}" for t in range(NT)) +
                        " sel pick den inv w spread")
        gdn_pe = steps("gdn_pe", "ab gc grows l2 brows kk0 kk1 tr " +
                       " ".join(f"{s}{l}{t}" for l in range(LEVELS) for s in "yz" for t in range(NT)) +
                       " v0 w s1 v1 o ms pool")
        gdn_act = steps("gdn_act", "e ln dec silu_qk sq silu_v l2root vb " +
                        " ".join(f"y{l}{t}" for l in range(LEVELS) for t in range(NT)) +
                        " vn0 w S1 vn1 osq root zs pool")
        gdn_vec = steps("gdn_vec", "ab adt aabs b1 b2 sp g spread gcc dd dm a0 a1 a2 a3 b0 b4 b5 b6 l2i qkn kb0 kb1 qg "
                        "lp0 lp1 kt " +
                        " ".join(f"{s}{l}{t}" for l in range(LEVELS) for s in "mx" for t in range(NT)) +
                        " rn on y")
        gdn_pool = steps("gdn_pool", "w2 w4 w8 w16 count less ident")
        att_pe = {s: steps(f"att_pe_{s}", s) for s in ("ms", "scores", "turned", "out")}
        att_act = {s: steps(f"att_act_{s}", s) for s in ("sq", "root", "v", "exp", "turned", "out")}
        att_vec = {s: steps(f"att_vec_{s}", s) for s in ("rn", "qk", "logit", "top", "neg", "inv", "prob")}
        gain_vec = steps("gain_vec", "q")

        def slot_k(n):
            return ring[:, n % RING, :].rearrange("p (k n) -> p k n", k=KD)

        def down_k(n):
            return ring[:, n % RING, :].rearrange("p (j n) -> p j n", j=2)

        def ff_slot(first, c):
            return first if isinstance(c, int) and c == 0 else first - 1 + 3 * c

        def ff_down(first, c, chunks):
            return first + 3 * chunks - 1 if isinstance(c, int) and c == chunks - 1 else first + 4 + 3 * c

        def each_chunk(eng, chunks, visit):
            visit(0, 0)
            visit(1, 1)
            with eng.Fori(1, chunks // 2) as i:
                for u in range(2):
                    visit(2 * i + u, u)
            if chunks % 2:
                visit(chunks - 1, 0)

        def chunks_of(kind):
            return MOE_CHUNKS if kind == "first1" else DENSE_CHUNKS

        tiles_before, total = [], 0
        for kind in plan:
            tiles_before.append(total)
            total += 2 * chunks_of(kind)
        mid_before, total = [], 0
        for kind in plan:
            mid_before.append(total)
            total += 0 if kind == "first0" else 2 * chunks_of(kind)
        conv_before = [2 * DENSE_CHUNKS * sum(k in ("even", "odd") for k in plan[:n]) for n in range(len(plan))]
        proj_before = [sum({"first0": 12, "first1": 12, "even": 10, "odd": 0}[k] for k in plan[:n])
                       for n in range(len(plan))]

        def mod_columns(layer, what):
            a = layer * MODS + what * KD
            return mod[:, a:a + KD]

        def mod_group(m):
            if m == 0:
                return 0, 2 * KD
            return (m - 1) * MODS + 2 * KD, min(m * MODS + 2 * KD, len(plan) * MODS)

        norms = []
        for n, kind in enumerate(plan):
            norms += [(n, 0), (n, 1)] + ([(n, 2)] if kind == "first1" else [])

        def x_ready(u):
            if norms[u - 1][1] == 2:
                return norm_vec.at("s7", u - 1)
            return x_vec.at("x", u - 1 - sum(which == 2 for _, which in norms[:u]))

        def norm_gain(n, which):
            kind, layer = plan[n], LAYER[plan[n]]
            if which == 2:
                return param("final_norm_g")
            if kind.startswith("first"):
                return param(("norm_mix_g", "norm_ffn_g")[which], layer, 2)
            return param(("norm_mix_2", "norm_ffn_2")[which], {"even": 0, "odd": 1}[kind], 2)

        block = ctx.enter_context(nc.Block())

        @block.sync
        def _(sp):
            for n in range(RING):
                sp.dma_start(ring[:, n, :], stream_in[n]).then_inc(weights_here[n], 16)
            rounds = total_slots // RING
            with sp.Fori(1, rounds) as i:
                for r in range(RING):
                    sp.wait_ge(weights_used, (i - 1) * RING + r + 1)
                    sp.dma_start(ring[:, r, :], stream_in[bass.ds(i * RING + r, 1)].rearrange("a p n -> p (a n)"))\
                      .then_inc(weights_here[r], 16)
            for n in range(rounds * RING, total_slots):
                sp.wait_ge(weights_used, n - RING + 1)
                sp.dma_start(ring[:, n % RING, :], stream_in[n]).then_inc(weights_here[n % RING], 16)
            sp.wait_ge(*x_ready(len(norms)))
            sp.dma_start(out, xT[:, :, :]).then_inc(stored, 16)
            sp.wait_ge(stored, 16)

        @block.gpsimd
        def _(pool):
            if firsts:
                for buf in (gq, gqe, hq, hqe):
                    last = pool.memset(buf, 0.0)
                last.then_inc(*zero_pool.step("zero"))

            def first_mixers(l):
                n = firsts[l]
                if l == 0:
                    pool.wait_ge(consts_here, 16)
                    pool.wait_ge(params_here, 16)
                else:
                    pool.wait_ge(*x_ready(norms.index((n, 0))))
                pool.tensor_tensor(sgu_w, param("sgu_w", LAYER[plan[firsts[l]]], 2).rearrange("p (h t) -> p h t", h=HEADS),
                                   const("upto").unsqueeze(1).to_broadcast([P, HEADS, P]), ALU.mult)\
                    .then_inc(*sgu_pool.step("w"))
                for m, slot in (("g", AV), ("h", HI)):
                    if m == "g":
                        pool.wait_ge(*proj_act.at("p", proj_before[n] + 11))
                    for tt in range(NT):
                        if m == "g" and tt == 0:
                            pass
                        elif tt == 1:
                            pool.wait_ge(*la_pe.at("u0" + m, l))
                        else:
                            pool.wait_ge(*la_pe.at("u1g", l))
                        pool.tensor_tensor(
                            v_chunks.rearrange("p (c v) -> p c v", c=8),
                            proj[:, slot, tt, :].unsqueeze(1).to_broadcast([P, 8, T]),
                            const("chunk_of").unsqueeze(2).to_broadcast([P, 8, T]), ALU.mult)\
                            .then_inc(*v_pool.step(f"v{m}{tt}"))

            def even_mixers(n):
                pool.wait_ge(*proj_act.at("p", proj_before[n] + 9))
                src = poolx
                for j in range(4):
                    d, lag = poolb[j % 2], 2 ** j
                    if j:
                        pool.wait_ge(*gdn_pool.at(f"w{lag}", 0))
                    pool.tensor_copy(d[:, j:4, 0:lag], src[:, j:4, 0:lag])
                    pool.tensor_tensor(d[:, j:4, lag:T], src[:, j:4, lag:T], src[:, j:4, 0:T - lag], ALU.add)\
                        .then_inc(*gdn_pool.step(f"w{2 * lag}"))
                    src = d
                pool.wait_ge(*gdn_pool.at("w16", 0))
                counts = const("per_count").rearrange("p (g t) -> p g t", g=4)
                for g in range(4):
                    d = poolb[g % 2][:, g, :]
                    last = pool.tensor_tensor(d, d, counts[:, g, :], ALU.mult)
                last.then_inc(*gdn_pool.step("count"))
                pool.wait_ge(*gdn_pool.at("count", 0))
                for g in range(4):
                    d = poolb[g % 2][:, g, :]
                    last = pool.tensor_tensor(d, d, poolx[:, g, :], ALU.subtract)
                last.then_inc(*gdn_pool.step("less"))
                pool.wait_ge(*gdn_vec.at("b6", 0))
                for buf in (X, XT):
                    last = pool.tensor_copy(buf.rearrange("p t (h n) -> p (t h) n", h=HEADS),
                                            const("ident").unsqueeze(1).to_broadcast([P, 8, P]))
                last.then_inc(*gdn_pool.step("ident"))

            for n, kind in enumerate(plan):
                if kind.startswith("first"):
                    first_mixers(firsts.index(n))
                elif kind == "even":
                    even_mixers(n)

        @block.scalar
        def _(act):
            act.dma_start(params[:, :], params_in).then_inc(params_here, 16)
            act.dma_start(xT[:, :, :], x_in).then_inc(x_here, 16)
            act.dma_start(consts[:, :], consts_in).then_inc(consts_here, 16)
            act.wait_ge(params_here, 16)
            act.activation(cond[:, 0, :], param("c"), ACT.Silu)
            act.activation(cond[:, 1, :], param("c_2"), ACT.Silu).then_inc(*cond_act.step("cond"))
            act.wait_ge(*lb_vec.at("d", 0))
            act.activation(lbw[:, 1:3, :], lbw[:, 1:3, :], ACT.Exp).then_inc(*lb_act.step("exp"))

            def norm(n, which):
                u = norms.index((n, which))
                if u == 0:
                    act.wait_ge(x_here, 16)
                else:
                    act.wait_ge(*x_ready(u))
                act.activation(yT[:, :, :], xT[:, :, :], ACT.Square).then_inc(*norm_act.step("squares"))
                act.wait_ge(*norm_pe.at("sum", u))
                act.activation(rstd[:, :], bank(4, 0, T), ACT.Sqrt, bias=EPS, scale=1.0 / D)\
                   .then_inc(*norm_act.step("root"))
                if which == 2:
                    return
                shift = mod_columns(n, 3 * which)
                for k in range(KD):
                    act.wait_ge(*norm_vec.at(f"s{k}", u))
                    act.activation(hT[:, k, :], yT[:, k, :], ACT.Identity, bias=shift[:, k:k + 1])\
                       .then_inc(*shift_act.step(f"h{k}"))

            def evacuate(n, slots):
                for s in slots:
                    act.wait_ge(weights_used, place[f"in{n}"] + s + 1)
                    act.activation(proj[:, s, :, :], bank(s % 4).rearrange("p (a t) -> p a t", a=2), ACT.Copy)\
                       .then_inc(*proj_act.step("p"))

            def exps(l, steps_act, steps_vec, decay, dist, run, e, scale):
                act.wait_ge(*steps_vec.at("dist", l))
                act.activation(e[:, 0, :], dist[:, 0, :], ACT.Exp, scale=scale)
                act.activation(e[:, 1, :], dist[:, 0, :], ACT.Exp, scale=-scale)
                act.activation(e[:, 2, :], dist[:, 1, :], ACT.Exp, scale=scale)
                act.activation(e[:, 3, :], run, ACT.Exp, scale=scale)
                act.activation(decay, run.rearrange("p (c i) -> p c i", i=LA)[:, :, LA - 1], ACT.Exp, scale=scale)\
                   .then_inc(*steps_act.step("exps"))

            def first_mixers(l):
                n = firsts[l]
                act.wait_ge(*glow_pe.at("glow", l))
                act.activation(glow[0:16, :], bank(4, 0, T)[0:16, :], ACT.Copy).then_inc(*gla_act.step("glow"))
                evacuate(n, [HF])
                act.wait_ge(*gla_vec.at("abs", l))
                act.activation(gt, gt, ACT.Exp, scale=-1.0).then_inc(*gla_act.step("t1"))
                act.wait_ge(*proj_act.at("p", proj_before[n] + HF))
                act.activation(hz, proj[:, HF, :, :].rearrange("p a t -> p (a t)"), ACT.Exp, scale=-1.0)\
                   .then_inc(*hgrn_act.step("e"))
                act.wait_ge(*gla_act.at("t1", l))
                act.activation(gt, gt, ACT.Ln, bias=1.0).then_inc(*gla_act.step("ln"))
                exps(l, gla_act, gla_vec, gdecay, gd, gb, ge, 1.0 / 16.0)
                evacuate(n, [HQ])
                act.wait_ge(*hgrn_vec.at("key", l))
                act.activation(hz, hf, ACT.Ln).then_inc(*hgrn_act.step("lnf"))
                evacuate(n, [HI, AQK])
                exps(l, hgrn_act, hgrn_vec, hdecay, hd, hb, he, 1.0)
                evacuate(n, [AV, SV])
                act.wait_ge(*sgu_vec.at("d", l))
                for tt in range(NT):
                    last = act.activation(cacc[:, tt, :], vn[:, tt, :], ACT.Square, accum_out=sgu_s[:, 2 + tt:3 + tt])
                last.then_inc(*sgu_act.step("sq"))
                act.wait_ge(*sgu_act.at("sq", l))
                act.activation(sgu_s[:, 4:6], sgu_s[:, 2:4], ACT.Sqrt, bias=EPS, scale=1.0 / T)\
                   .then_inc(*sgu_act.step("root"))
                evacuate(n, [SU, CC, CX, CB, HG, AR])
                act.wait_ge(*proj_act.at("p", proj_before[n] + AR))
                act.activation(gates[:, 0, :], proj[:, AR, :, :].rearrange("p a t -> p (a t)"), ACT.Silu)\
                   .then_inc(*gla_act.step("gate"))
                act.activation(gates[:, 1, :], proj[:, HG, :, :].rearrange("p a t -> p (a t)"), ACT.Silu)\
                   .then_inc(*hgrn_act.step("gate"))
                for m in "gh":
                    w = 2 * P if m == "g" else 4 * P
                    act.wait_ge(*la_pe.at("tr" + m, l))
                    act.activation(ku_tok[:, 0:w], bank(5, 0, w), ACT.Copy).then_inc(*la_act.step("ku" + m))
                    act.wait_ge(*la_pe.at("o" + m, l))
                    act.activation(osq, bank(5), ACT.Square).then_inc(*la_act.step("osq" + m))
                    act.wait_ge(*la_pe.at("ms" + m, l))
                    act.activation(orn, bank(4), ACT.Sqrt, bias=EPS, scale=1.0 / 64)\
                       .then_inc(*la_act.step("root" + m))

            def router(n):
                act.wait_ge(*moe_vec.at("neg", 0))
                for tt in range(NT):
                    last = act.activation(comb[:, tt, :], logits[:, tt, :], ACT.Exp, bias=top[:, tt:tt + 1])
                last.then_inc(*moe_act.step("exp"))
                act.wait_ge(*moe_pe.at("rows", 0))
                for b in range(4):
                    last = act.activation(comb_row[:, 2 * b:2 * b + 2, :], bank(b).rearrange("p (e t) -> p e t", e=2),
                                          ACT.Copy)
                last.then_inc(*moe_act.step("rows"))

            def even_mixers(n):
                act.wait_ge(*gdn_vec.at("aabs", 0))
                act.activation(beta.rearrange("p (t h) -> p t h", t=NT), ab[:, :, 0:4], ACT.Exp, scale=-1.0)
                act.activation(anex, param("gdn_a_log_2"), ACT.Exp)
                act.activation(abt[:, :, 0:4], abt[:, :, 0:4], ACT.Exp, scale=-1.0).then_inc(*gdn_act.step("e"))
                act.wait_ge(*gdn_act.at("e", 0))
                act.activation(abt[:, :, 0:4], abt[:, :, 0:4], ACT.Ln, bias=1.0).then_inc(*gdn_act.step("ln"))
                act.wait_ge(*gdn_vec.at("dd", 0))
                act.activation(dec, dec, ACT.Exp)
                act.activation(egrow, bank(7), ACT.Exp)
                act.activation(egc, gccol, ACT.Exp)
                act.activation(kdf, kdf, ACT.Exp).then_inc(*gdn_act.step("dec"))
                evacuate(n, range(6))
                act.wait_ge(*gdn_vec.at("a3", 0))
                act.activation(qkv[:, 0:8, :], qkv[:, 0:8, :], ACT.Silu).then_inc(*gdn_act.step("silu_qk"))
                evacuate(n, [6])
                act.wait_ge(*gdn_act.at("silu_qk", 0))
                act.activation(l2.rearrange("p (n t) -> p n t", n=8), qkv[:, 0:8, :], ACT.Square)\
                   .then_inc(*gdn_act.step("sq"))
                evacuate(n, [7])
                act.wait_ge(*gdn_vec.at("b6", 0))
                act.activation(qkv[:, 8:12, :], qkv[:, 8:12, :], ACT.Silu).then_inc(*gdn_act.step("silu_v"))
                evacuate(n, [8, 9])
                act.wait_ge(*gdn_pe.at("l2", 0))
                for b in range(4):
                    last = act.activation(l2[:, 512 * b:512 * b + 512], bank(b), ACT.Sqrt, bias=EPS)
                last.then_inc(*gdn_act.step("l2root"))
                act.wait_ge(*gdn_pe.at("tr", 0))
                for m in range(8):
                    last = act.activation(vb[:, m * P:m * P + P], pair[:, m * P:m * P + P], ACT.Copy,
                                          scale=beta[:, m:m + 1])
                last.then_inc(*gdn_act.step("vb"))
                for l in range(LEVELS):
                    for t in range(NT):
                        act.wait_ge(*gdn_pe.at(f"y{l}{t}", 0))
                        act.activation(Y[:, t, :], bank(t), ACT.Copy).then_inc(*gdn_act.step(f"y{l}{t}"))
                act.wait_ge(*gdn_pe.at("v0", 0))
                act.activation(vnew[:, 0, :], bank(0), ACT.Copy).then_inc(*gdn_act.step("vn0"))
                act.wait_ge(*gdn_pe.at("w", 0))
                act.activation(wTn, bank(1), ACT.Copy, scale=-1.0).then_inc(*gdn_act.step("w"))
                act.wait_ge(*gdn_pe.at("s1", 0))
                act.activation(S1, bank(2), ACT.Copy).then_inc(*gdn_act.step("S1"))
                act.wait_ge(*gdn_pe.at("v1", 0))
                act.activation(vnew[:, 1, :], bank(3), ACT.Copy).then_inc(*gdn_act.step("vn1"))
                act.wait_ge(*gdn_pe.at("o", 0))
                act.activation(gosq, pair[:, :], ACT.Square).then_inc(*gdn_act.step("osq"))
                act.wait_ge(*gdn_pe.at("ms", 0))
                act.activation(gorn[:, 0:512], bank(4), ACT.Sqrt, bias=EPS, scale=1.0 / P)
                act.activation(gorn[:, 512:1024], bank(5), ACT.Sqrt, bias=EPS, scale=1.0 / P)\
                   .then_inc(*gdn_act.step("root"))
                act.activation(zsilu, pflat[:, 3072:4096], ACT.Silu).then_inc(*gdn_act.step("zs"))
                act.wait_ge(*gdn_pe.at("pool", 0))
                for g in range(4):
                    last = act.activation(yT[:, 4 + g, :], bank(2 + g // 2, g % 2 * T, g % 2 * T + T), ACT.Copy,
                                          scale=param("pool_scale_2")[:, g:g + 1])
                last.then_inc(*gdn_act.step("pool"))

            def odd_mixers(n):
                def unit_exp(u):
                    w = ATT_GROUPS * (u % 2 + 1) * P
                    act.wait_ge(*att_vec["neg"].at("neg", u))
                    if u >= 2:
                        act.wait_ge(*att_pe["turned"].at("turned", u - 2))
                    act.activation(prob[:, u % 2, 0:w], logit[:, u % 2, 0:w], ACT.Exp, bias=neg_q[:, u:u + 1],
                                   accum_out=sum_q[:, u:u + 1]).then_inc(*att_act["exp"].step("exp"))

                def unit_turned(u):
                    blocks = ATT_GROUPS * (u % 2 + 1)
                    act.wait_ge(*att_pe["turned"].at("turned", u))
                    if u >= 2:
                        act.wait_ge(*att_pe["out"].at("out", u - 2))
                    a = min(blocks, 4)
                    last = act.activation(probT[:, u % 2, 0:a, :], bank(4, 0, a * P).rearrange("p (n m) -> p n m", n=a),
                                          ACT.Copy)
                    if blocks > 4:
                        last = act.activation(probT[:, u % 2, 4:6, :],
                                              bank(5, 0, 2 * P).rearrange("p (n m) -> p n m", n=2), ACT.Copy)
                    last.then_inc(*att_act["turned"].step("turned"))

                def unit_out(u):
                    act.wait_ge(*att_pe["out"].at("out", u))
                    act.activation(yT[:, u // 2, u % 2 * P:u % 2 * P + P], bank(3, 0, P), ACT.Copy)\
                       .then_inc(*att_act["out"].step("out"))

                for hp in range(5):
                    for s in range(9):
                        if hp < 4:
                            at, g, j = place[f"in{n}"] + hp * 9 + s, s // 3, s % 3
                            q = hp * 6 + g * 2 + j
                            act.wait_ge(weights_used, at + 1)
                            if j < 2:
                                if q >= 2:
                                    act.wait_ge(*att_vec["qk"].at("qk", q - 2))
                                act.activation(qraw[:, q % 2, :], bank((hp * 9 + s) % 2), ACT.Copy)
                                act.activation(qsq[:, q % 2, :], bank((hp * 9 + s) % 2), ACT.Square)\
                                   .then_inc(*att_act["sq"].step("sq"))
                            else:
                                if hp >= 2 and g == 0:
                                    act.wait_ge(*att_pe["out"].at("out", 4 * (hp - 1) - 1))
                                act.activation(vtok[:, hp % 2, g, :, :],
                                               bank((hp * 9 + s) % 2).rearrange("p (t d) -> p t d", t=2), ACT.Copy)\
                                   .then_inc(*att_act["v"].step("v"))
                        if hp >= 1 and s < 8:
                            u = 4 * (hp - 1) + s // 2
                            if s % 2 == 0:
                                unit_exp(u)
                            else:
                                unit_turned(u)
                        if hp >= 1 and s >= 2 and s % 2 == 0:
                            unit_out(4 * (hp - 1) + s // 2 - 1)
                        if hp < 4 and s % 3 < 2:
                            act.wait_ge(*att_pe["ms"].at("ms", q))
                            act.activation(qrn[:, q % 2, :], bank(2), ACT.Sqrt, bias=EPS, scale=1.0 / P)\
                               .then_inc(*att_act["root"].step("root"))

            def feed_forward(n, kind):
                base, first = tiles_before[n], place[f"ffn{n}"]

                def visit(c, odd):
                    for j in range(2):
                        t = base + 2 * c + j
                        b = 2 * odd + j
                        if not isinstance(c, int) or c >= 2:
                            act.wait_ge(ffn_hid, t - 3)
                        if kind in ("even", "odd"):
                            act.wait_ge(ffn_mid, mid_before[n] + 2 * c + j + 1)
                            act.activation(ff_silu[:, b, :], ff_mid[:, b, :], ACT.Silu).then_inc(ffn_silu, 1)
                            continue
                        if j == 0:
                            act.wait_ge(ffn_half, base // 2 + c + 1)
                        else:
                            act.wait_ge(weights_used, ff_slot(first, c) + 2)
                        act.activation(ff_silu[:, b, :], bank(4 + b, 0, T), ACT.Silu).then_inc(ffn_silu, 1)
                each_chunk(act, chunks_of(kind), visit)

            for n, kind in enumerate(plan):
                norm(n, 0)
                if kind.startswith("first"):
                    first_mixers(firsts.index(n))
                elif kind == "even":
                    even_mixers(n)
                else:
                    odd_mixers(n)
                norm(n, 1)
                if kind == "first1":
                    router(n)
                feed_forward(n, kind)
                if kind == "first1":
                    norm(n, 2)

        @block.tensor
        def _(pe):
            def mm(o, a, b, start=True, stop=True):
                return pe.matmul(o, lhsT=a, rhs=b, start=start, stop=stop, skip_group_check=True)

            def arrive(at, i=None):
                rounds = at // RING + 1
                pe.wait_ge(weights_here[at % RING], 16 * rounds if i is None else i * 16 + 16 * rounds)

            def product(at, to, src, token_major=False):
                arrive(at)
                w = slot_k(at)
                for t in range(2):
                    for k in range(KD):
                        a, b = w[:, k, t * P:t * P + P], src[:, k, :]
                        if token_major:
                            a, b = src[:, k, t * P:t * P + P], w[:, k, :]
                        last = mm(to[:, t * T:t * T + T], a, b, k == 0, k == KD - 1)
                last.then_inc(weights_used, 1)

            def project(n, slots, token_major=()):
                for s in slots:
                    if s >= 4:
                        pe.wait_ge(*proj_act.at("p", proj_before[n] + s - 4))
                    product(place[f"in{n}"] + s, bank(s % 4), hT, s in token_major)

            def modulate(m, count):
                a, b = mod_group(m)
                for _ in range(count):
                    s = mod_done[m] = mod_done.get(m, -1) + 1
                    if 2 * s >= b - a:
                        mod_done[m] -= 1
                        return
                    at = place[f"mod{m}"] + s
                    if s == 0:
                        if m:
                            pe.wait_ge(*mod_vec.at("mod", m - 1))
                        else:
                            pe.wait_ge(*cond_act.at("cond", 0))
                    arrive(at)
                    for t in range(2):
                        which = 0 if plan[(a + 2 * s + t) // MODS].startswith("first") else 1
                        for k in range(KD):
                            last = mm(bank(7, 2 * s + t, 2 * s + t + 1), slot_k(at)[:, k, t * P:t * P + P],
                                      cond[:, which, k:k + 1], k == 0, k == KD - 1)
                    last.then_inc(weights_used, 1)

            mod_done = {}

            def norm(n, which):
                u = norms.index((n, which))
                pe.wait_ge(*norm_act.at("squares", u))
                for k in range(KD):
                    last = mm(bank(4, 0, T), const("ones"), yT[:, k, :], k == 0, k == KD - 1)
                last.then_inc(*norm_pe.step("sum"))

            def normed(n, which):
                pe.wait_ge(*shift_act.at("h7", 2 * n + which))

            def la(l, m, between):
                n = firsts[l]
                key, q, qe = (gk, gq, gqe) if m == "g" else (hk, hq, hqe)
                slot = AV if m == "g" else HI
                pe.wait_ge(*(gla_vec if m == "g" else hgrn_vec).at("ku", l))
                if m == "h":
                    pe.wait_ge(*la_vec.at("ong", l))
                nf = 1 if m == "g" else 2
                for tt in range(NT):
                    for f in range(nf):
                        a = (tt * nf + f) * P
                        last = pe.transpose(bank(5, a, a + P), key[:, 1, f * T + tt * P:f * T + tt * P + P],
                                            const("ident"))
                last.then_inc(*la_pe.step("tr" + m))
                for tt, b in ((0, 4), (1, 6)):
                    if tt == 1 and m == "g":
                        pe.wait_ge(*sgu_vec.at("mix", l))
                    if m == "g":
                        last = mm(bank(b).rearrange("p (h t) -> p h t", h=4), key[:, 0, tt * P:tt * P + P],
                                  q[:, :, tt * P:tt * P + P])
                    else:
                        for f in range(2):
                            last = mm(bank(b, f * T, f * T + T).rearrange("p (h t) -> p h t", h=2),
                                      key[:, 0, f * T + tt * P:f * T + tt * P + P], q[:, f, :, tt * P:tt * P + P])
                    last.then_inc(*la_pe.step(("sa", "sb")[tt] + m))
                pe.wait_ge(*la_act.at("ku" + m, l))
                if m == "g":
                    pe.wait_ge(*proj_act.at("p", proj_before[n] + 11))
                for tt in range(NT):
                    pe.wait_ge(*v_pool.at(f"v{m}{tt}", l))
                    if tt == 1:
                        pe.wait_ge(*la_vec.at("st8" + m, l))
                    for b in range(4):
                        if m == "g":
                            last = mm(bank(b), ku_tok[:, tt * P:tt * P + P], v_chunks[:, b * 512:b * 512 + 512])
                        else:
                            f, half = b // 2, b % 2
                            v = v_chunks.rearrange("p (c v) -> p c v", c=8)[:, 4 * half:4 * half + 4, f * P:f * P + P]
                            last = mm(bank(b).rearrange("p (c v) -> p c v", c=4),
                                      ku_tok[:, (tt * 2 + f) * P:(tt * 2 + f) * P + P], v)
                    last.then_inc(*la_pe.step(f"u{tt}" + m))
                    between()
                pe.wait_ge(*la_vec.at("st15" + m, l))
                st = state.rearrange("p (c v) -> p c v", c=NCH)
                for half in range(2):
                    for vt in range(2):
                        h = 2 * vt + half
                        for tt in range(NT):
                            a = vt * T + tt * P
                            mm(bank(5, a, a + P)[64 * half:64 * half + 64, :], proj[:, slot, tt, h * 64:h * 64 + 64],
                               scores[:, tt, h * P:h * P + P], vt == 0 and tt == 0, False)
                        for c in range(1, NCH):
                            a = vt * T + c * LA
                            rq = qe[:, h, c * LA:c * LA + LA] if m == "g" else qe[:, vt, half, c * LA:c * LA + LA]
                            last = mm(bank(5, a, a + LA)[64 * half:64 * half + 64, :], st[:, c, h * 64:h * 64 + 64],
                                      rq, False, c == NCH - 1)
                last.then_inc(*la_pe.step("o" + m))
                between()
                pe.wait_ge(*la_act.at("osq" + m, l))
                mm(bank(4), const("half_ones"), osq).then_inc(*la_pe.step("ms" + m))

            def first_mixers(l):
                n = firsts[l]
                normed(n, 0)
                for k in range(KD):
                    last = mm(bank(4, 0, T)[0:16, :], param("w_glow", LAYER[plan[firsts[l]]], 2)[:, k * 16:k * 16 + 16], hT[:, k, :],
                              k == 0, k == KD - 1)
                last.then_inc(*glow_pe.step("glow"))
                project(n, [0], TOKEN_MAJOR)
                pe.wait_ge(*gla_act.at("glow", l))
                mm(bank(5, 0, T), param("gla_w_gate", LAYER[plan[firsts[l]]], 2)[0:16, :], glow[0:16, :]).then_inc(*glow_pe.step("z"))
                project(n, range(1, 12), TOKEN_MAJOR)
                pe.wait_ge(*sgu_vec.at("vn", l))
                pe.wait_ge(*sgu_pool.at("w", l))
                for half in range(2):
                    for vt in range(2):
                        h = 2 * vt + half
                        for tt in range(NT):
                            a = vt * T + tt * P
                            last = mm(bank(6, a, a + P)[64 * half:64 * half + 64, :], vn[:, tt, h * 64:h * 64 + 64],
                                      sgu_w[:, h, :])
                last.then_inc(*sgu_pe.step("mix"))
                modulate(n + 1, 2)
                la(l, "g", lambda: modulate(n + 1, 4))
                modulate(n + 1, 2)
                la(l, "h", lambda: modulate(n + 1, 4))
                modulate(n + 1, 24)
                pe.wait_ge(*conv_vec.at("y", l))
                pe.wait_ge(*sgu_vec.at("y", l))
                pe.wait_ge(*la_vec.at("yh", l))

            def even_mixers(n):
                normed(n, 0)
                for tt in range(NT):
                    for k in range(KD):
                        last = mm(bank(4, tt * 8, tt * 8 + 8), hT[:, k, tt * P:tt * P + P],
                                  param("w_ab")[:, k * 8:k * 8 + 8], k == 0, k == KD - 1)
                last.then_inc(*gdn_pe.step("ab"))
                project(n, range(2))
                pe.wait_ge(*gdn_vec.at("spread", 0))
                for tt in range(NT):
                    last = mm(bank(5, tt * 4, tt * 4 + 4), const("upto"), gdec[:, tt * 4:tt * 4 + 4])
                last.then_inc(*gdn_pe.step("gc"))
                for m in range(8):
                    last = mm(pair[:, m * P:m * P + P], spread[:, 0, m, :], const("upto"))
                last.then_inc(*gdn_pe.step("grows"))
                project(n, range(2, 10))
                pe.wait_ge(*proj_act.at("p", proj_before[n] + 9))
                pe.wait_ge(*gdn_act.at("sq", 0))
                for b in range(4):
                    last = mm(bank(b), const("ones"), l2[:, b * 512:b * 512 + 512])
                last.then_inc(*gdn_pe.step("l2"))
                pe.wait_ge(*gdn_vec.at("gcc", 0))
                for m in range(8):
                    a = m % 4 * P
                    last = mm(bank(4 + m // 4, a, a + P), spread[:, 1, m, :], const("ident"))
                last.then_inc(*gdn_pe.step("brows"))
                for tt in range(NT):
                    pe.wait_ge(*gdn_vec.at(f"kb{tt}", 0))
                    for h in range(HEADS):
                        kt, a = qkv[:, 4 + h, tt * P:tt * P + P], h * P
                        mm(bank(tt, a, a + P), kt, kb[:, tt, a:a + P])
                        last = mm(bank(2 + tt, a, a + P), kt, qkv[:, h, tt * P:tt * P + P])
                    last.then_inc(*gdn_pe.step(f"kk{tt}"))
                pe.wait_ge(*gdn_act.at("silu_v", 0))
                pe.wait_ge(*gdn_act.at("dec", 0))
                for m in range(8):
                    tt, h, a = m // 4, m % 4, m % 4 * P
                    pe.transpose(bank(4 + tt, a, a + P), qkv[:, 4 + h, tt * P:tt * P + P], const("ident"))
                    last = pe.transpose(pair[:, m * P:m * P + P], qkv[:, 8 + h, tt * P:tt * P + P], const("ident"))
                last.then_inc(*gdn_pe.step("tr"))
                pe.wait_ge(*gdn_pool.at("ident", 0))
                pe.wait_ge(*gdn_act.at("vb", 0))
                for l in range(LEVELS):
                    for t in range(NT):
                        pe.wait_ge(*gdn_vec.at(f"m{l}{t}", 0))
                        for h in range(HEADS):
                            a = h * P
                            last = mm(bank(t, a, a + P), MT[:, t, a:a + P], X[:, t, a:a + P])
                        last.then_inc(*gdn_pe.step(f"y{l}{t}"))
                    modulate(n + 1, 1)
                    for t in range(NT):
                        pe.wait_ge(*gdn_act.at(f"y{l}{t}", 0))
                        for h in range(HEADS):
                            a = h * P
                            mm(bank(2 + t, a, a + P), XT[:, t, a:a + P], Y[:, t, a:a + P])
                            last = mm(bank(4 + t, a, a + P), Y[:, t, a:a + P], XT[:, t, a:a + P])
                        last.then_inc(*gdn_pe.step(f"z{l}{t}"))
                    modulate(n + 1, 1)
                for t in range(NT):
                    pe.wait_ge(*gdn_vec.at(f"x6{t}", 0))
                for h in range(HEADS):
                    a = h * P
                    last = mm(bank(0, a, a + P), XT[:, 0, a:a + P], vb[:, a:a + P])
                last.then_inc(*gdn_pe.step("v0"))
                for h in range(HEADS):
                    a = h * P
                    last = mm(bank(1, a, a + P), kbe[:, a:a + P], XT[:, 1, a:a + P])
                last.then_inc(*gdn_pe.step("w"))
                modulate(n + 1, 2)
                pe.wait_ge(*gdn_act.at("vn0", 0))
                for h in range(HEADS):
                    a = h * P
                    last = mm(bank(2, a, a + P), kdec[:, a:a + P], vnew[:, 0, a:a + P])
                last.then_inc(*gdn_pe.step("s1"))
                modulate(n + 1, 2)
                pe.wait_ge(*gdn_act.at("S1", 0))
                for h in range(HEADS):
                    a = h * P
                    mm(bank(3, a, a + P), XT[:, 1, a:a + P], vb[:, 512 + a:512 + a + P], True, False)
                    last = mm(bank(3, a, a + P), wTn[:, a:a + P], S1[:, a:a + P], False, True)
                last.then_inc(*gdn_pe.step("v1"))
                modulate(n + 1, 24)
                pe.wait_ge(*gdn_act.at("vn1", 0))
                if mod_group(n + 1)[1] > mod_group(n + 1)[0]:
                    pe.wait_ge(*mod_vec.at("mod", n + 1))
                for h in range(HEADS):
                    a, o = h * P, h * T
                    mm(pair[:, o:o + P], vnew[:, 0, a:a + P], PT[:, 0, a:a + P])
                    mm(pair[:, o + P:o + T], vnew[:, 1, a:a + P], PT[:, 1, a:a + P], True, False)
                    last = mm(pair[:, o + P:o + T], S1[:, a:a + P], qg[:, a:a + P], False, True)
                last.then_inc(*gdn_pe.step("o"))
                pe.wait_ge(*gdn_act.at("osq", 0))
                mm(bank(4), const("ones"), gosq[:, 0:512])
                mm(bank(5), const("ones"), gosq[:, 512:1024]).then_inc(*gdn_pe.step("ms"))
                pe.wait_ge(*gdn_pool.at("less", 0))
                for g in range(4):
                    last = mm(bank(2 + g // 2, g % 2 * T, g % 2 * T + T), param("pool_w_2")[:, g * P:g * P + P],
                              poolb[g % 2][:, g, :])
                last.then_inc(*gdn_pe.step("pool"))
                pe.wait_ge(*gdn_vec.at("y", 0))
                pe.wait_ge(*gdn_act.at("pool", 0))

            def odd_mixers(n):
                first = place[f"in{n}"]

                def mean_square(q):
                    pe.wait_ge(*att_act["sq"].at("sq", q))
                    if q:
                        pe.wait_ge(*att_act["root"].at("root", q - 1))
                    mm(bank(2), const("ones"), qsq[:, q % 2, :]).then_inc(*att_pe["ms"].step("ms"))

                def scores_of(u):
                    hp, h, qt = u // 4, u // 2 % 2, u % 2
                    w = (qt + 1) * P
                    if u % 4 == 0:
                        pe.wait_ge(*att_vec["qk"].at("qk", 6 * hp + 5))
                    if u:
                        pe.wait_ge(*att_vec["logit"].at("logit", u - 1))
                    for g in range(ATT_GROUPS):
                        last = mm(pair[:, g * w:g * w + w], qk[:, hp % 2, 0, g, h, qt * P:qt * P + P],
                                  qk[:, hp % 2, 1, g, h, 0:w])
                    last.then_inc(*att_pe["scores"].step("scores"))

                def turn(u):
                    pe.wait_ge(*att_vec["prob"].at("prob", u))
                    if u:
                        pe.wait_ge(*att_act["turned"].at("turned", u - 1))
                    for b in range(ATT_GROUPS * (u % 2 + 1)):
                        last = pe.transpose(bank(4 + b // 4, b % 4 * P, b % 4 * P + P), prob[:, u % 2, b * P:b * P + P],
                                            const("ident"))
                    last.then_inc(*att_pe["turned"].step("turned"))

                def values_of(u):
                    hp, h, qt = u // 4, u // 2 % 2, u % 2
                    pe.wait_ge(*att_act["turned"].at("turned", u))
                    if u % 4 == 0:
                        pe.wait_ge(*att_act["v"].at("v", 3 * hp + 2))
                    if u:
                        pe.wait_ge(*att_act["out"].at("out", u - 1))
                    blocks = ATT_GROUPS * (qt + 1)
                    for b in range(blocks):
                        g, kt = b // (qt + 1), b % (qt + 1)
                        last = mm(bank(3, 0, P), vtok[:, hp % 2, g, kt, h * P:h * P + P], probT[:, u % 2, b, :],
                                  b == 0, b == blocks - 1)
                    last.then_inc(*att_pe["out"].step("out"))

                modulate(n + 1, 24)
                normed(n, 0)
                pe.wait_ge(*mod_vec.at("mod", n + 1))
                for hp in range(5):
                    for s in range(9):
                        if hp < 4:
                            at = hp * 9 + s
                            if at >= 2:
                                hb, sb_ = divmod(at - 2, 9)
                                if sb_ % 3 == 2:
                                    pe.wait_ge(*att_act["v"].at("v", hb * 3 + sb_ // 3))
                                else:
                                    pe.wait_ge(*att_act["sq"].at("sq", hb * 6 + sb_ // 3 * 2 + sb_ % 3))
                            product(first + at, bank(at % 2), hT, s % 3 == 2)
                        if hp >= 1:
                            u = 4 * (hp - 1)
                            if s % 2 == 0 and s >= 2:
                                values_of(u + s // 2 - 1)
                            if s < 8:
                                (scores_of if s % 2 == 0 else turn)(u + s // 2)
                        if hp < 4 and s % 3 < 2:
                            mean_square(hp * 6 + s // 3 * 2 + s % 3)
                for u in (14, 15):
                    pe.wait_ge(*att_act["out"].at("out", u))

            def out_product(n):
                for s in range(4):
                    product(place[f"out{n}"] + s, bank(s), yT)

            def router(n):
                normed(n, 1)
                for tt in range(NT):
                    for k in range(KD):
                        last = mm(bank(4, tt * 8, tt * 8 + 8), hT[:, k, tt * P:tt * P + P],
                                  param("moe_router")[:, k * 8:k * 8 + 8], k == 0, k == KD - 1)
                last.then_inc(*moe_pe.step("logits"))
                pe.wait_ge(*moe_vec.at("spread", 0))
                for e in range(EXPERTS):
                    for tt in range(NT):
                        a = e % 2 * T + tt * P
                        last = mm(bank(e // 2, a, a + P), comb_b[:, e, tt, :], const("ident"))
                last.then_inc(*moe_pe.step("rows"))

            def feed_forward(n, kind):
                chunks, first, base = chunks_of(kind), place[f"ffn{n}"], tiles_before[n]

                def up(c, i=None):
                    at = ff_slot(first, c)
                    for s in (at, at + 1):
                        arrive(s, i)
                    for j in range(2):
                        b = 4 + 2 * (c % 2) + j
                        if c >= 2:
                            t = base + 2 * c + j - 3
                            pe.wait_ge(ffn_hid, t if i is None else i * 4 + t)
                        for w in range(2):
                            for k in range(KD):
                                last = mm(bank(b, w * T, w * T + T), slot_k(at + w)[:, k, j * P:j * P + P], hT[:, k, :],
                                          k == 0, k == KD - 1)
                            if j == 1:
                                last.then_inc(weights_used, 1)
                        if j == 0:
                            last.then_inc(ffn_half, 1)

                def down(c, i=None, final=False):
                    at = ff_down(first, c, chunks) if final else first + 4 + 3 * c
                    arrive(at, i)
                    t = base + 2 * c + 2
                    pe.wait_ge(ffn_hid, t if i is None else i * 4 + t)
                    for j in range(2):
                        for d in range(KD):
                            last = mm(bank(d // 2, d % 2 * T, d % 2 * T + T), down_k(at)[:, j, d * P:d * P + P],
                                      ff_hid[:, 2 * (c % 2) + j, :],
                                      i is None and c == 0 and j == 0 and d % 2 == 0, final and j == 1)
                    last.then_inc(weights_used, 1)

                normed(n, 1)
                up(0)
                for c in range(2):
                    up(c + 1)
                    down(c)
                with pe.Fori(0, (chunks - 1) // 2 - 1) as i:
                    for c in (2, 3):
                        up(c + 1, i)
                        down(c, i)
                for c in range(2 * ((chunks - 1) // 2), chunks - 1):
                    up(c + 1)
                    down(c)
                down(chunks - 1, final=True)

            pe.wait_ge(consts_here, 16)
            pe.wait_ge(params_here, 16)
            modulate(0, 24)
            for n, kind in enumerate(plan):
                norm(n, 0)
                if kind.startswith("first"):
                    first_mixers(firsts.index(n))
                elif kind == "even":
                    even_mixers(n)
                else:
                    odd_mixers(n)
                out_product(n)
                norm(n, 1)
                if kind == "first1":
                    router(n)
                feed_forward(n, kind)
                if kind == "first1":
                    norm(n, 2)

        @block.vector
        def _(dve):
            def tt(o, a, b, op):
                return dve.tensor_tensor(o, a, b, op)

            def ts(o, a, s1, s2, op0, op1):
                return dve.tensor_scalar(o, a, s1, s2, op0, op1)

            def stt(o, a, s, b, op0, op1):
                return dve.scalar_tensor_tensor(o, a, s, b, op0, op1)

            def modulation(m):
                a, b = mod_group(m)
                if b <= a:
                    return
                dve.wait_ge(weights_used, place[f"mod{m}"] + (b - a) // 2)
                tt(mod[:, a:b], bank(7, 0, b - a), param("b_mod")[:, a:b], ALU.add).then_inc(*mod_vec.step("mod"))

            def norm(n, which):
                u = norms.index((n, which))
                if which < 2:
                    dve.wait_ge(*mod_vec.at("mod", n + which))
                    if u:
                        dve.wait_ge(*norm_vec.at("s7", u - 1))
                    last = stt(gain[:, :], mod_columns(n, 3 * which + 1), 1.0, norm_gain(n, which), ALU.add, ALU.mult)
                else:
                    dve.wait_ge(*norm_vec.at("s7", u - 1))
                    last = dve.tensor_copy(gain[:, :], norm_gain(n, which))
                last.then_inc(*norm_vec.step("gain"))
                dve.wait_ge(*norm_act.at("root", u))
                dve.reciprocal(rstd[:, :], rstd[:, :]).then_inc(*norm_vec.step("rstd"))
                dve.wait_ge(*norm_vec.at("rstd", u))
                for k in range(KD):
                    o = xT if which == 2 else yT
                    stt(o[:, k, :], xT[:, k, :], gain[:, k:k + 1], rstd[:, :], ALU.mult, ALU.mult)\
                        .then_inc(*norm_vec.step(f"s{k}"))

            def lower_bounds():
                raw = param("hgrn_lower_bounds").rearrange("p (l f) -> p l f", l=2)
                tt(lbw[:, 0, :], raw[:, 0, :], raw[:, 1, :], ALU.max).then_inc(*lb_vec.step("max"))
                dve.wait_ge(*lb_vec.at("max", 0))
                tt(lbw[:, 1, :], raw[:, 0, :], lbw[:, 0, :], ALU.subtract)
                tt(lbw[:, 2, :], raw[:, 1, :], lbw[:, 0, :], ALU.subtract).then_inc(*lb_vec.step("d"))
                dve.wait_ge(*lb_act.at("exp", 0))
                tt(lbw[:, 3, :], lbw[:, 1, :], lbw[:, 2, :], ALU.add).then_inc(*lb_vec.step("sum"))
                dve.wait_ge(*lb_vec.at("sum", 0))
                dve.reciprocal(lbw[:, 4, :], lbw[:, 3, :]).then_inc(*lb_vec.step("inv"))
                dve.wait_ge(*lb_vec.at("inv", 0))
                dve.memset(lbs[:, 0, 0, :], 0.0)
                dve.memset(lbs[:, 0, 1, :], 1.0)
                tt(lbs[:, 1, 0, :], lbw[:, 2, :], lbw[:, 4, :], ALU.mult).then_inc(*lb_vec.step("lb"))
                dve.wait_ge(*lb_vec.at("lb", 0))
                ts(lbs[:, 1, 1, :], lbs[:, 1, 0, :], -1.0, 1.0, ALU.mult, ALU.add).then_inc(*lb_vec.step("om"))
                dve.wait_ge(*lb_vec.at("om", 0))

            def running(vec, l, run, log, dist, w):
                dve.tensor_tensor_scan(run, const("restart")[:, 0:w], log, 0.0, ALU.mult, ALU.add)\
                   .then_inc(*vec.step("run"))
                dve.wait_ge(*vec.at("run", l))
                c = run.rearrange("p (c i) -> p c i", i=LA)
                d = [dist[:, a, :].rearrange("p (c i) -> p c i", i=LA) for a in range(2)]
                shape = [P, w // LA, LA]
                tt(d[0], c, c[:, :, LA // 2:LA // 2 + 1].to_broadcast(shape), ALU.subtract)
                tt(d[1], c[:, :, LA - 1:LA].to_broadcast(shape), c, ALU.subtract).then_inc(*vec.step("dist"))

            def la(l, m):
                n = firsts[l]
                mask = const("same_chunk").unsqueeze(1).to_broadcast([P, HEADS, P])
                for t, b in ((0, 4), (1, 6)):
                    s = ("sa", "sb")[t] + m
                    dve.wait_ge(*la_pe.at(s, l))
                    tt(scores[:, t, :].rearrange("p (h t) -> p h t", h=4), bank(b).rearrange("p (h t) -> p h t", h=4),
                       mask, ALU.mult).then_inc(*la_vec.step(s))
                st = state.rearrange("p (c v) -> p c v", c=NCH)
                for c in range(1, NCH):
                    t, cc = divmod(c - 1, 8)
                    if cc == 0:
                        dve.wait_ge(*la_pe.at(f"u{t}" + m, l))
                    if c > 1:
                        dve.wait_ge(*la_vec.at(f"st{c - 1}" + m, l))
                    for f in range(1 if m == "g" else 2):
                        if m == "g":
                            part, cols = bank(cc // 2, cc % 2 * T, cc % 2 * T + T), slice(0, T)
                            decay = gdecay[:, c - 1:c]
                        else:
                            part = bank(f * 2 + cc // 4, cc % 4 * P, cc % 4 * P + P)
                            cols, decay = slice(f * P, f * P + P), hdecay[:, f * NCH + c - 1:f * NCH + c]
                        if c == 1:
                            last = dve.tensor_copy(st[:, c, cols], part)
                        else:
                            last = stt(st[:, c, cols], st[:, c - 1, cols], decay, part, ALU.mult, ALU.add)
                    last.then_inc(*la_vec.step(f"st{c}" + m))
                dve.wait_ge(*la_act.at("root" + m, l))
                dve.reciprocal(orn, orn).then_inc(*la_vec.step("rn" + m))
                dve.wait_ge(*la_vec.at("rn" + m, l))
                tt(osq, bank(5), orn, ALU.mult).then_inc(*la_vec.step("on" + m))
                dve.wait_ge(*la_vec.at("on" + m, l))
                dve.wait_ge(*(gla_act if m == "g" else hgrn_act).at("gate", l))
                a = 4 if m == "g" else 6
                stt(yT[:, a:a + 2, :].rearrange("p a t -> p (a t)"), osq,
                    param("gla_norm_g" if m == "g" else "hgrn_norm_g", LAYER[plan[firsts[l]]], 2), gates[:, 0 if m == "g" else 1, :],
                    ALU.mult, ALU.mult).then_inc(*la_vec.step("y" + m))

            def first_mixers(l):
                n = firsts[l]

                def here(s):
                    dve.wait_ge(*proj_act.at("p", proj_before[n] + s))
                dve.wait_ge(*glow_pe.at("z", l))
                ts(gz, bank(5, 0, T), param("gla_b_gate", LAYER[plan[firsts[l]]], 2), None, ALU.add, ALU.bypass).then_inc(*gla_vec.step("z"))
                dve.wait_ge(*gla_vec.at("z", l))
                stt(gt, gz, -1.0, gz, ALU.mult, ALU.max).then_inc(*gla_vec.step("abs"))
                dve.wait_ge(*hgrn_act.at("e", l))
                ts(hz, hz, 1.0, None, ALU.add, ALU.bypass).then_inc(*hgrn_vec.step("add"))
                dve.wait_ge(*hgrn_vec.at("add", l))
                dve.reciprocal(hz, hz).then_inc(*hgrn_vec.step("sig"))
                dve.wait_ge(*hgrn_vec.at("sig", l))
                for f in range(2):
                    last = ts(hf[:, f * T:f * T + T], hz[:, f * T:f * T + T], lbs[:, LAYER[plan[firsts[l]]], 1, f:f + 1],
                              lbs[:, LAYER[plan[firsts[l]]], 0, f:f + 1], ALU.mult, ALU.add)
                last.then_inc(*hgrn_vec.step("f"))
                dve.wait_ge(*hgrn_vec.at("f", l))
                ts(hkey, hf, -1.0, 1.0, ALU.mult, ALU.add).then_inc(*hgrn_vec.step("key"))
                dve.wait_ge(*gla_act.at("ln", l))
                stt(gz, gz, 0.0, gt, ALU.min, ALU.subtract).then_inc(*gla_vec.step("min"))
                dve.wait_ge(*gla_vec.at("min", l))
                running(gla_vec, l, gb, gz, gd, T)
                dve.wait_ge(*hgrn_act.at("lnf", l))
                running(hgrn_vec, l, hb, hz, hd, 2 * T)
                dve.wait_ge(*zero_pool.at("zero", 0))
                here(AQK)
                dve.wait_ge(*gla_act.at("exps", l))
                for h in range(4):
                    r = slice(32 * h, 32 * h + 32)
                    for buf, e in ((gq, 0), (gqe, 3)):
                        stt(buf[r, h, :], proj[r, AQK, 0, :], float(32 ** -0.5), ge[r, e, :], ALU.mult, ALU.mult)
                tt(gk[:, 0, :], proj[:, AQK, 1, :], ge[:, 1, :], ALU.mult)
                tt(gk[:, 1, :], proj[:, AQK, 1, :], ge[:, 2, :], ALU.mult).then_inc(*gla_vec.step("ku"))
                dve.wait_ge(*hgrn_act.at("exps", l))
                for f in range(2):
                    for h in range(2):
                        r = slice(64 * h, 64 * h + 64)
                        for buf, e in ((hq, 0), (hqe, 3)):
                            tt(buf[r, f, h, :], proj[r, HQ, f, :], he[r, e, f * T:f * T + T], ALU.mult)
                tt(hk[:, 0, :], hkey, he[:, 1, :], ALU.mult)
                tt(hk[:, 1, :], hkey, he[:, 2, :], ALU.mult).then_inc(*hgrn_vec.step("ku"))
                here(SV)
                dve.tensor_reduce(sgu_s[:, 0:2], proj[:, SV, :, :], AX, ALU.add).then_inc(*sgu_vec.step("sum"))
                dve.wait_ge(*sgu_vec.at("sum", l))
                ts(sgu_s[:, 0:2], sgu_s[:, 0:2], 1.0 / T, None, ALU.mult, ALU.bypass).then_inc(*sgu_vec.step("mu"))
                dve.wait_ge(*sgu_vec.at("mu", l))
                for t in range(NT):
                    last = ts(vn[:, t, :], proj[:, SV, t, :], sgu_s[:, t:t + 1], None, ALU.subtract, ALU.bypass)
                last.then_inc(*sgu_vec.step("d"))
                dve.wait_ge(*sgu_act.at("root", l))
                dve.reciprocal(sgu_s[:, 6:8], sgu_s[:, 4:6]).then_inc(*sgu_vec.step("rs"))
                dve.wait_ge(*sgu_vec.at("rs", l))
                for t in range(NT):
                    last = stt(vn[:, t, :], vn[:, t, :], sgu_s[:, 6 + t:7 + t], param("sgu_norm_g", LAYER[plan[firsts[l]]], 2),
                               ALU.mult, ALU.mult)
                last.then_inc(*sgu_vec.step("vn"))
                here(CB)
                tt(cv, proj[:, CC, :, :], proj[:, CX, :, :], ALU.mult).then_inc(*conv_vec.step("cv"))
                dve.wait_ge(*conv_vec.at("cv", l))
                w = param("conv_w", LAYER[plan[firsts[l]]], 2).rearrange("p (f k) -> p f k", f=2)
                for f in range(2):
                    last = ts(cacc[:, f, :], cv[:, f, :], w[:, f, 2:3], None, ALU.mult, ALU.bypass)
                last.then_inc(*conv_vec.step("c0"))
                for back in (1, 2):
                    dve.wait_ge(*conv_vec.at(f"c{back - 1}", l))
                    for f in range(2):
                        last = stt(cacc[:, f, back:T], cv[:, f, 0:T - back], w[:, f, 2 - back:3 - back],
                                   cacc[:, f, back:T], ALU.mult, ALU.add)
                    last.then_inc(*conv_vec.step(f"c{back}"))
                dve.wait_ge(*conv_vec.at("c2", l))
                tt(yT[:, 0:2, :], cacc, proj[:, CB, :, :], ALU.mult).then_inc(*conv_vec.step("y"))
                dve.wait_ge(*sgu_pe.at("mix", l))
                bias = param("sgu_b", LAYER[plan[firsts[l]]], 2).rearrange("p (v t) -> p v t", v=2).unsqueeze(2).to_broadcast([P, 2, 2, P])
                tt(cv.rearrange("p v (t i) -> p v t i", t=2), bank(6).rearrange("p (v t i) -> p v t i", v=2, t=2),
                   bias, ALU.add).then_inc(*sgu_vec.step("mix"))
                dve.wait_ge(*sgu_vec.at("mix", l))
                tt(yT[:, 2:4, :], cv, proj[:, SU, :, :], ALU.mult).then_inc(*sgu_vec.step("y"))
                la(l, "g")
                la(l, "h")

            def router(n):
                dve.wait_ge(*moe_pe.at("logits", 0))
                dve.tensor_copy(logits, bank(4, 0, 16).rearrange("p (t e) -> p t e", t=NT))\
                   .then_inc(*moe_vec.step("copy"))
                dve.wait_ge(*moe_vec.at("copy", 0))
                dve.tensor_reduce(top, logits, AX, ALU.max).then_inc(*moe_vec.step("max"))
                dve.wait_ge(*moe_vec.at("max", 0))
                ts(top, top, -1.0, None, ALU.mult, ALU.bypass).then_inc(*moe_vec.step("neg"))
                lower = const("lower_expert").rearrange("p (a b) -> p a b", a=8)
                for t in range(NT):
                    mine = logits[:, t, :].unsqueeze(2).to_broadcast([P, 8, 8])
                    other = logits[:, t, :].unsqueeze(1).to_broadcast([P, 8, 8])
                    tt(rk_gt, other, mine, ALU.is_gt).then_inc(*moe_vec.step(f"gt{t}"))
                    tt(rk_eq, other, mine, ALU.is_equal).then_inc(*moe_vec.step(f"eq{t}"))
                    dve.wait_ge(*moe_vec.at(f"eq{t}", 0))
                    tt(rk_eq, rk_eq, lower, ALU.mult).then_inc(*moe_vec.step(f"low{t}"))
                    dve.wait_ge(*moe_vec.at(f"low{t}", 0))
                    tt(rk_gt, rk_gt, rk_eq, ALU.add).then_inc(*moe_vec.step(f"sum{t}"))
                    dve.wait_ge(*moe_vec.at(f"sum{t}", 0))
                    dve.tensor_reduce(rank[:, t, :], rk_gt, AX, ALU.add).then_inc(*moe_vec.step(f"rk{t}"))
                    dve.wait_ge(*moe_vec.at(f"rk{t}", 0))
                ts(rank, rank, 2.0, None, ALU.is_lt, ALU.bypass).then_inc(*moe_vec.step("sel"))
                dve.wait_ge(*moe_vec.at("sel", 0))
                dve.wait_ge(*moe_act.at("exp", 0))
                tt(comb, comb, rank, ALU.mult).then_inc(*moe_vec.step("pick"))
                dve.wait_ge(*moe_vec.at("pick", 0))
                dve.tensor_reduce(den, comb, AX, ALU.add).then_inc(*moe_vec.step("den"))
                dve.wait_ge(*moe_vec.at("den", 0))
                dve.reciprocal(den, den).then_inc(*moe_vec.step("inv"))
                dve.wait_ge(*moe_vec.at("inv", 0))
                tt(comb, comb, den.unsqueeze(2).to_broadcast([P, NT, 8]), ALU.mult).then_inc(*moe_vec.step("w"))
                dve.wait_ge(*moe_vec.at("w", 0))
                dve.tensor_copy(comb_b, comb.rearrange("p t e -> p e t").unsqueeze(3).to_broadcast([P, 8, NT, P]))\
                   .then_inc(*moe_vec.step("spread"))

            def even_mixers(n):
                v = gdn_vec
                hh = [P, NT, HEADS]

                def th(a):
                    return a.rearrange("p (t h) -> p t h", t=NT)

                def after(name):
                    dve.wait_ge(*v.at(name, 0))
                dve.wait_ge(*gdn_pe.at("ab", 0))
                dve.tensor_copy(ab, bank(4, 0, 16).rearrange("p (t e) -> p t e", t=NT)).then_inc(*v.step("ab"))
                after("ab")
                tt(abt[:, :, 4:8], ab[:, :, 4:8], param("gdn_dt_bias_2").unsqueeze(1).to_broadcast(hh), ALU.add)\
                    .then_inc(*v.step("adt"))
                after("adt")
                stt(abt[:, :, 0:4], abt[:, :, 4:8], -1.0, abt[:, :, 4:8], ALU.mult, ALU.max).then_inc(*v.step("aabs"))
                dve.wait_ge(*gdn_act.at("e", 0))
                ts(beta, beta, 1.0, None, ALU.add, ALU.bypass).then_inc(*v.step("b1"))
                after("b1")
                dve.reciprocal(beta, beta).then_inc(*v.step("b2"))
                dve.wait_ge(*gdn_act.at("ln", 0))
                stt(th(gdec), abt[:, :, 4:8], 0.0, abt[:, :, 0:4], ALU.max, ALU.add).then_inc(*v.step("sp"))
                after("sp")
                stt(th(gdec), th(gdec), -1.0, anex.unsqueeze(1).to_broadcast(hh), ALU.mult, ALU.mult)\
                    .then_inc(*v.step("g"))
                after("g")
                dve.tensor_copy(spread[:, 0, :, :], gdec.unsqueeze(2).to_broadcast([P, 8, P]))
                dve.tensor_copy(spread[:, 1, :, :], beta.unsqueeze(2).to_broadcast([P, 8, P]))\
                   .then_inc(*v.step("spread"))
                dve.wait_ge(*gdn_pe.at("gc", 0))
                dve.tensor_copy(gccol, bank(5, 0, 8)).then_inc(*v.step("gcc"))
                after("gcc")
                dve.wait_ge(*gdn_pe.at("grows", 0))
                for m in range(8):
                    ts(dec[:, m * P:m * P + P], pair[:, m * P:m * P + P], gccol[:, m:m + 1], 0.0, ALU.subtract, ALU.min)
                tt(kdf, pair[:, P - 1:8 * P:P], gccol, ALU.subtract).then_inc(*v.step("dd"))
                dve.wait_ge(*gdn_act.at("dec", 0))
                d3, s3 = (a.rearrange("p (m c) -> p m c", m=8) for a in (dec, decs))
                tt(s3, d3, const("before").unsqueeze(1).to_broadcast([P, 8, P]), ALU.mult)
                tt(bege, beta, egc, ALU.mult)
                tt(d3, d3, const("upto").unsqueeze(1).to_broadcast([P, 8, P]), ALU.mult).then_inc(*v.step("dm"))
                w = param("gdn_conv_w_2").rearrange("p (n k) -> p n k", n=12)
                for name, tiles in (("a", range(8)), ("b", range(8, 12))):
                    dve.wait_ge(*proj_act.at("p", proj_before[n] + tiles[-1] // 2))
                    for back in range(4):
                        at = back if name == "a" or back == 0 else back + 3
                        if back:
                            after(f"{name}{at - 1 if back > 1 or name == 'a' else 0}")
                        for j in tiles:
                            x = proj[:, j // 2, j % 2, :]
                            if back == 0:
                                last = ts(qkv[:, j, :], x, w[:, j, 3:4], None, ALU.mult, ALU.bypass)
                            else:
                                last = stt(qkv[:, j, back:T], x[:, 0:T - back], w[:, j, 3 - back:4 - back],
                                           qkv[:, j, back:T], ALU.mult, ALU.add)
                        last.then_inc(*v.step(f"{name}{at}"))
                dve.wait_ge(*gdn_act.at("l2root", 0))
                dve.reciprocal(l2, l2).then_inc(*v.step("l2i"))
                after("l2i")
                r8 = l2.rearrange("p (n t) -> p n t", n=8)
                stt(qkv[:, 0:4, :], qkv[:, 0:4, :], float(P ** -0.5), r8[:, 0:4, :], ALU.mult, ALU.mult)
                tt(qkv[:, 4:8, :], qkv[:, 4:8, :], r8[:, 4:8, :], ALU.mult).then_inc(*v.step("qkn"))
                after("qkn")
                dve.wait_ge(*gdn_pe.at("brows", 0))
                for t in range(NT):
                    tt(kb[:, t, :].rearrange("p (h c) -> p h c", h=4), bank(4 + t).rearrange("p (h c) -> p h c", h=4),
                       qkv[:, 4:8, t * P:t * P + P], ALU.mult).then_inc(*v.step(f"kb{t}"))
                tt(qg.rearrange("p (h c) -> p h c", h=4), qkv[:, 0:4, P:T],
                   egrow.rearrange("p (h c) -> p h c", h=4), ALU.mult).then_inc(*v.step("qg"))
                for t in range(NT):
                    dve.wait_ge(*gdn_pe.at(f"kk{t}", 0))
                    a = t * 512
                    tt(LT[:, t, :], bank(t), decs[:, a:a + 512], ALU.mult)
                    tt(PT[:, t, :], bank(2 + t), dec[:, a:a + 512], ALU.mult).then_inc(*v.step(f"lp{t}"))
                dve.wait_ge(*gdn_pe.at("tr", 0))
                for h in range(HEADS):
                    a = h * P
                    ts(kdec[:, a:a + P], bank(4, a, a + P), kdf[:, h:h + 1], None, ALU.mult, ALU.bypass)
                    last = ts(kbe[:, a:a + P], bank(5, a, a + P), bege[:, 4 + h:5 + h], None, ALU.mult, ALU.bypass)
                last.then_inc(*v.step("kt"))
                dve.wait_ge(*gdn_pool.at("ident", 0))
                levels = const("levels").rearrange("p (l c) -> p l c", l=LEVELS)
                for l in range(LEVELS):
                    for t in range(NT):
                        after("lp1")
                        tt(MT[:, t, :].rearrange("p (h c) -> p h c", h=4), LT[:, t, :].rearrange("p (h c) -> p h c", h=4),
                           levels[:, l, :].unsqueeze(1).to_broadcast([P, 4, P]), ALU.mult).then_inc(*v.step(f"m{l}{t}"))
                    for t in range(NT):
                        dve.wait_ge(*gdn_pe.at(f"z{l}{t}", 0))
                        if l:
                            after(f"x{l - 1}{t}")
                        tt(X[:, t, :], X[:, t, :], bank(2 + t), ALU.subtract)
                        tt(XT[:, t, :], XT[:, t, :], bank(4 + t), ALU.subtract).then_inc(*v.step(f"x{l}{t}"))
                modulation(n + 1)
                dve.wait_ge(*gdn_act.at("root", 0))
                dve.reciprocal(gorn, gorn).then_inc(*v.step("rn"))
                after("rn")
                tt(gosq, pair[:, :], gorn, ALU.mult).then_inc(*v.step("on"))
                after("on")
                dve.wait_ge(*gdn_act.at("zs", 0))
                stt(yT[:, 0:4, :].rearrange("p h t -> p (h t)"), gosq, param("gdn_norm_2"), zsilu, ALU.mult, ALU.mult)\
                    .then_inc(*v.step("y"))

            def odd_mixers(n):
                modulation(n + 1)
                ts(qgain, param("att_q_norm_2"), float(P ** -0.5), None, ALU.mult, ALU.bypass)\
                    .then_inc(*gain_vec.step("q"))
                dve.wait_ge(*gain_vec.at("q", 0))

                def normed_qk(q):
                    hp, g, j = q // 6, q % 6 // 2, q % 2
                    dve.wait_ge(*att_act["root"].at("root", q))
                    dve.reciprocal(qrn[:, q % 2, :], qrn[:, q % 2, :]).then_inc(*att_vec["rn"].step("rn"))
                    dve.wait_ge(*att_vec["rn"].at("rn", q))
                    if hp >= 2:
                        dve.wait_ge(*att_pe["scores"].at("scores", 4 * (hp - 1) - 1))
                    stt(qk[:, hp % 2, j, g, :, :].rearrange("p h t -> p (h t)"), qraw[:, q % 2, :],
                        (qgain, param("att_k_norm_2"))[j], qrn[:, q % 2, :], ALU.mult, ALU.mult)\
                        .then_inc(*att_vec["qk"].step("qk"))

                def softmax(u, part):
                    qt, w = u % 2, ATT_GROUPS * (u % 2 + 1) * P
                    slope = 2.0 ** (-8.0 * (u // 2 + 1) / ATT_HEADS)
                    if part == 0:
                        dist = const("distance")[:, 0:384] if qt == 0 else const("distance")[:, 384:1152]
                        dve.wait_ge(*att_pe["scores"].at("scores", u))
                        stt(logit[:, u % 2, 0:w], dist, slope, pair[:, 0:w], ALU.mult, ALU.add)\
                            .then_inc(*att_vec["logit"].step("logit"))
                        dve.wait_ge(*att_vec["logit"].at("logit", u))
                        dve.tensor_reduce(top_q[:, u:u + 1], logit[:, u % 2, 0:w], AX, ALU.max)\
                           .then_inc(*att_vec["top"].step("top"))
                        dve.wait_ge(*att_vec["top"].at("top", u))
                        ts(neg_q[:, u:u + 1], top_q[:, u:u + 1], -1.0, None, ALU.mult, ALU.bypass)\
                            .then_inc(*att_vec["neg"].step("neg"))
                    else:
                        dve.wait_ge(*att_act["exp"].at("exp", u))
                        dve.reciprocal(inv_q[:, u:u + 1], sum_q[:, u:u + 1]).then_inc(*att_vec["inv"].step("inv"))
                        dve.wait_ge(*att_vec["inv"].at("inv", u))
                        ts(prob[:, u % 2, 0:w], prob[:, u % 2, 0:w], inv_q[:, u:u + 1], None, ALU.mult, ALU.bypass)\
                            .then_inc(*att_vec["prob"].step("prob"))

                for hp in range(5):
                    for s in range(9):
                        if hp >= 1 and s % 2 == 0 and s < 8:
                            softmax(4 * (hp - 1) + s // 2, 0)
                            softmax(4 * (hp - 1) + s // 2, 1)
                        if hp < 4 and s % 3 < 2:
                            normed_qk(hp * 6 + s // 3 * 2 + s % 3)

            def out_update(n):
                g = mod_columns(n, 2)
                dve.wait_ge(*mod_vec.at("mod", n + 1))
                for s in range(4):
                    dve.wait_ge(weights_used, place[f"out{n}"] + s + 1)
                    for t in range(2):
                        d = 2 * s + t
                        last = stt(xT[:, d, :], bank(s, t * T, t * T + T), g[:, d:d + 1], xT[:, d, :],
                                   ALU.mult, ALU.add)
                last.then_inc(*x_vec.step("x"))

            def feed_forward(n, kind):
                base, first, chunks = tiles_before[n], place[f"ffn{n}"], chunks_of(kind)
                convolved = kind in ("even", "odd")

                def visit(c, odd):
                    late = not isinstance(c, int) or c >= 2

                    def up_here(j):
                        if j == 0:
                            dve.wait_ge(ffn_half, base // 2 + c + 1)
                        else:
                            dve.wait_ge(weights_used, ff_slot(first, c) + 2)
                    if convolved:
                        layer = LAYER[kind]
                        wa = param_at["ffn_conv_w_2"][0] + layer * FF_TILES * 3
                        ba = param_at["ffn_conv_b_2"][0] + layer * FF_TILES

                        def col(a, per, extra=0):
                            return params[:, bass.ds(c * (2 * per) + (a + extra), 1)]
                        for back in range(3):
                            if back:
                                dve.wait_ge(ffn_conv, conv_before[n] + 2 * c + back)
                            for j in range(2):
                                b = 2 * odd + j
                                if back == 0:
                                    up_here(j)
                                    if late:
                                        dve.wait_ge(ffn_silu, base + 2 * c + j - 3)
                                    last = ts(ff_mid[:, b, :], bank(4 + b, 0, T), col(wa, 3, 3 * j + 2),
                                              col(ba, 1, j), ALU.mult, ALU.add)
                                else:
                                    last = stt(ff_mid[:, b, back:T], bank(4 + b, 0, T - back),
                                               col(wa, 3, 3 * j + 2 - back), ff_mid[:, b, back:T], ALU.mult, ALU.add)
                                if back == 2:
                                    last.then_inc(ffn_mid, 1)
                            if back < 2:
                                last.then_inc(ffn_conv, 1)
                    if kind == "first1":
                        for j in range(2):
                            b = 2 * odd + j
                            dve.wait_ge(ffn_silu, base + 2 * c + j + 1)
                            tt(ff_mid[:, b, :], ff_silu[:, b, :], comb_row[:, c // EXPERT_CHUNKS, :], ALU.mult)\
                                .then_inc(ffn_mid, 1)
                    for j in range(2):
                        b = 2 * odd + j
                        dve.wait_ge(ffn_silu, base + 2 * c + j + 1)
                        if late:
                            dve.wait_ge(weights_used, first + 3 * c - 1)
                        factor = ff_silu[:, b, :]
                        if kind == "first1":
                            dve.wait_ge(ffn_mid, mid_before[n] + 2 * c + j + 1)
                            factor = ff_mid[:, b, :]
                        tt(ff_hid[:, b, :], bank(4 + b, T, 2 * T), factor, ALU.mult).then_inc(ffn_hid, 1)

                if kind == "first1":
                    dve.wait_ge(*moe_act.at("rows", 0))
                each_chunk(dve, chunks, visit)
                g = mod_columns(n, 5)
                dve.wait_ge(weights_used, first + 3 * chunks)
                for d in range(KD):
                    last = stt(xT[:, d, :], bank(d // 2, d % 2 * T, d % 2 * T + T), g[:, d:d + 1], xT[:, d, :],
                               ALU.mult, ALU.add)
                last.then_inc(*x_vec.step("x"))

            dve.wait_ge(params_here, 16)
            dve.wait_ge(consts_here, 16)
            lower_bounds()
            modulation(0)
            for n, kind in enumerate(plan):
                norm(n, 0)
                if kind.startswith("first"):
                    first_mixers(firsts.index(n))
                    modulation(n + 1)
                elif kind == "even":
                    even_mixers(n)
                else:
                    odd_mixers(n)
                out_update(n)
                norm(n, 1)
                if kind == "first1":
                    router(n)
                feed_forward(n, kind)
                if kind == "first1":
                    norm(n, 2)


def column_slots(w, first=0, last=None):
    w = w[:, first:last]
    return w.reshape(KD, P, w.shape[1] // COLS, COLS).transpose(2, 1, 0, 3).reshape(-1, P, SLOT)


def row_slots(w):
    return w.reshape(w.shape[0] // COLS, 2, P, D).transpose(0, 2, 1, 3).reshape(-1, P, SLOT)


def columns(v):
    return np.asarray(v).reshape(-1, P).T


def lay_stream(a, plan):
    place = stream_plan(plan)
    stream = np.empty((place["end"], P, SLOT), np.float32)

    def put(at, slots):
        stream[at:at + len(slots)] = slots
    mods = {"first0": ("w_ada", 0), "first1": ("w_ada", 1), "even": ("ada_w_2", 0), "odd": ("ada_w_2", 1)}
    at_mod = [np.asarray(a[mods[k][0]][mods[k][1]]) for k in plan]
    half = 2 * D
    put(place["mod0"], column_slots(at_mod[0], 0, half))
    for n, kind in enumerate(plan):
        put(place[f"mod{n + 1}"], column_slots(at_mod[n], half))
        if n + 1 < len(plan):
            put(place[f"mod{n + 1}"] + (6 * D - half) // COLS, column_slots(at_mod[n + 1], 0, half))
        at = place[f"in{n}"]
        layer = 1 if kind in ("first1", "odd") else 0
        if kind.startswith("first"):
            w = a["w_in"][layer]
            for s in range(12):
                put(at + s, column_slots(w, COLUMN_OF[s], COLUMN_OF[s] + COLS))
            put(place[f"out{n}"], column_slots(a["w_out"][layer]))
        elif kind == "even":
            w = a["ev_w_in_2"][0]
            put(at, column_slots(w, 0, 2048))
            put(at + 8, column_slots(w, 2056, 2568))
            put(place[f"out{n}"], column_slots(a["ev_w_out_2"][0]))
        else:
            w = a["od_w_in_2"][0]
            for hp in range(ATT_HEADS // 2):
                for s in range(9):
                    c = s * D + hp * COLS
                    put(at + hp * 9 + s, column_slots(w, c, c + COLS))
            put(place[f"out{n}"], column_slots(a["od_w_out_2"][0]))
        at = place[f"ffn{n}"]
        if kind == "first0":
            experts = [(a["ffn_w1"][0], a["ffn_w3"][0], a["ffn_w2"][0])]
        elif kind == "first1":
            experts = [(a["moe_w1"][0][e], a["moe_w3"][0][e], a["moe_w2"][0][e]) for e in range(EXPERTS)]
        else:
            up = a["ffn_w_up_2"][layer]
            experts = [(up[:, 0:D_FF], up[:, D_FF:], a["ffn_w_down_2"][layer])]
        chunks = sum(w1.shape[1] // COLS for w1, _, _ in experts)
        c = 0
        for w1, w3, w2 in experts:
            w1, w3, w2 = column_slots(w1), column_slots(w3), row_slots(w2)
            for i in range(len(w1)):
                up = at if c == 0 else at - 1 + 3 * c
                stream[up], stream[up + 1] = w1[i], w3[i]
                stream[at + 3 * chunks - 1 if c == chunks - 1 else at + 4 + 3 * c] = w2[i]
                c += 1
    return stream


def lay_params(a, plan):
    def rows(v):
        return np.broadcast_to(np.asarray(v).reshape(1, -1), (P, np.asarray(v).size))

    def padded(v):
        return np.concatenate([v, np.zeros((P - v.shape[0], v.shape[1]), v.dtype)])

    def per_k(w):
        return w.reshape(KD, P, -1).transpose(1, 0, 2).reshape(P, -1)
    both = range(2)
    mods = {"first0": ("b_ada", 0), "first1": ("b_ada", 1), "even": ("ada_b_2", 0), "odd": ("ada_b_2", 1)}
    b_mod = [columns(a[mods[k][0]][mods[k][1]]) for k in plan]
    b_mod += [np.zeros((P, MODS), np.float32)] * (4 - len(plan))
    out = {
        "c": columns(a["c"]), "c_2": columns(a["c_2"]), "b_mod": np.concatenate(b_mod, 1),
        "conv_w": np.concatenate([a["conv_w"][l].reshape(3, 2, P).transpose(2, 1, 0).reshape(P, 6) for l in both], 1),
        "sgu_norm_g": rows(a["sgu_norm_g"]),
        "sgu_w": np.concatenate([a["sgu_w"][l].transpose(2, 0, 1).reshape(P, 512) for l in both], 1),
        "sgu_b": np.concatenate([np.repeat(a["sgu_b"][l].reshape(2, 2, P).transpose(1, 0, 2), 64, axis=0)
                                 .reshape(P, 256) for l in both], 1),
        "w_glow": np.concatenate([per_k(a["w_in"][l][:, GLOW_COLUMN:GLOW_COLUMN + 16]) for l in both], 1),
        "gla_w_gate": np.concatenate([padded(a["gla_w_gate"][l]) for l in both], 1),
        "gla_norm_g": np.concatenate([a["gla_norm_g"].T] * 2), "hgrn_norm_g": np.concatenate([a["hgrn_norm_g"].T] * 2),
        "moe_router": per_k(a["moe_router"][0]), "w_ab": per_k(a["ev_w_in_2"][0][:, 2048:2056]),
        "gdn_conv_w_2": a["gdn_conv_w_2"][0].reshape(4, 12, P).transpose(2, 1, 0).reshape(P, 48),
        "gdn_a_log_2": rows(a["gdn_a_log_2"][0]), "gdn_dt_bias_2": rows(a["gdn_dt_bias_2"][0]),
        "pool_w_2": a["pool_w_2"][0].transpose(1, 0, 2).reshape(P, 512),
        "ffn_conv_w_2": np.concatenate([a["ffn_conv_w_2"][l].reshape(3, FF_TILES, P).transpose(2, 1, 0)
                                        .reshape(P, -1) for l in both], 1),
    }
    for name in PARAM_COLUMNS:
        if name not in out:
            out[name] = columns(a[name])
    assert {k: out[k].shape[1] for k in PARAM_COLUMNS} == PARAM_COLUMNS
    return np.ascontiguousarray(np.concatenate([out[k] for k in PARAM_COLUMNS], 1))


def lay_out(a, plan):
    return {
        "x_dram": np.ascontiguousarray(a["x"][0].reshape(T, KD, P).transpose(2, 1, 0)),
        "params_dram": lay_params(a, plan),
        "consts_dram": np.concatenate(list(constant_columns().values()), 1),
        "stream_dram": lay_stream(a, plan),
    }


def make(nc, arrays, plan):
    args = [nc.dram_tensor(k, v.shape, F32, kind="ExternalInput").ap() for k, v in arrays.items()]
    args.append(nc.dram_tensor("out_dram", (P, KD, T), F32, kind="ExternalOutput").ap())
    build_program(nc, *args, plan=plan)


def kernel(**inputs):
    import concourse.bacc as bacc
    from concourse.bass_utils import run_bass_kernel_spmd

    arrays = lay_out({k: np.asarray(v) for k, v in inputs.items()}, PLAN)
    nc = bacc.Bacc("TRN2", target_bir_lowering=False, num_devices=1)
    make(nc, arrays, PLAN)
    got = run_bass_kernel_spmd(nc, [arrays], core_ids=[0]).results[0]["out_dram"]
    return np.ascontiguousarray(got.transpose(2, 1, 0)).reshape(1, T, D)
```

```python
from contextlib import ExitStack

import concourse.bass as bass
import numpy as np
from concourse import mybir

F32 = mybir.dt.float32
F32R = mybir.dt.float32r
ALU = mybir.AluOpType
ACT = mybir.ActivationFunctionType
AX = mybir.AxisListType.X

P = 128
D = 1024
KD = D // P
T = 256
NT = T // P
EPS = 1e-6
SLOT = 2048
COLS = 256
RING = 6
MODS = 6 * KD
MOD_SLOTS = MODS * P // COLS
MOD_LEAD = 2 * KD * P // COLS
MOD_GROUP = 3
D_FF = 2816
D_FFE = 3584
EXPERTS = 8
DENSE_CHUNKS = D_FF // COLS
EXPERT_CHUNKS = D_FFE // COLS
MOE_CHUNKS = EXPERTS * EXPERT_CHUNKS
FF_TILES = D_FF // P
LA = 16
NCH = T // LA
HEADS = 4
ATT_HEADS = 8
ATT_GROUPS = 3
LEVELS = 7
NEG = -1e30

HF, HQ, HI, AQK, AV, SV, SU, CC, CX, CB, HG, AR = range(12)
TOKEN_MAJOR = (HI, AV, SV)
COLUMN_OF = {HF: 2320, HQ: 2064, HI: 2576, AQK: 1280, AV: 1536, SV: 1024, SU: 768, CC: 256, CX: 512, CB: 0,
             HG: 2832, AR: 1808}
GLOW_COLUMN = 1792
GDN_QKV, GDN_Z, GDN_POOL = 6, 2, 2
PLAN = ("first0", "first1", "even", "odd")
LAYER = {"first0": 0, "first1": 1, "even": 0, "odd": 1}


class Steps:

    def __init__(self, sem, names):
        self.sem, self.names, self.count = sem, names.split(), 0

    def step(self, name):
        assert self.names[self.count % len(self.names)] == name, (name, self.names[self.count % len(self.names)])
        self.count += 1
        return self.sem, 1

    def at(self, name, use):
        return self.sem, use * len(self.names) + self.names.index(name) + 1


def ffn_slots(first, chunks):
    def up(c):
        return first + 3 * c - 1

    def down(c):
        return first + 3 * c + 4
    return up, down, first, first + 3 * chunks - 1


def stream_plan(plan):
    at, place = 0, {}

    def put(name, n):
        nonlocal at
        place[name] = at
        at += n
    for n, kind in enumerate(plan):
        if kind.startswith("first"):
            put(f"in{n}", 12)
        elif kind == "even":
            put(f"in{n}", GDN_QKV + GDN_Z + GDN_POOL)
        else:
            put(f"in{n}", ATT_HEADS // 2 * ATT_GROUPS * 3)
        if n == 0:
            put("mod_rest", MOD_SLOTS - MOD_LEAD)
        put(f"out{n}", D // COLS)
        put(f"ffn{n}", 3 * (MOE_CHUNKS if kind == "first1" else DENSE_CHUNKS))
    place["end"] = at
    for n in range(len(plan)):
        put(f"mod{n}", MOD_SLOTS if n else MOD_LEAD)
    place["all"] = at
    return place


def constant_columns():
    r = np.arange(P)
    row, col = r[:, None], r[None, :]
    out = {
        "ident": (row == col), "ones": np.ones((P, P)), "half_ones": (row // 64 == col // 64),
        "upto": (row <= col), "before": (row < col),
        "same_chunk": (row // LA == col // LA) & (row <= col),
        "restart": np.tile((np.arange(2 * T) % LA != 0), (P, 1)),
        "chunk_of": (row // LA == np.arange(P // LA)[None, :]),
        "levels": np.concatenate([((col >> l) & 1 == 1) & (row >> l == (col >> l) - 1) for l in range(LEVELS)], 1),
    }
    rel = []
    for qt in range(NT):
        for dil in (1, 4, 16):
            d = (qt * P + row) - np.arange((qt + 1) * P)[None, :]
            ok = (d >= 0) & (d % dil == 0) & (d <= P * dil)
            rel.append(np.where(ok, -d.astype(np.float64), NEG))
    out["distance"] = np.concatenate(rel, 1)
    out["per_count"] = np.tile(np.concatenate([1.0 / np.minimum(np.arange(1, T + 1), w) for w in (2, 4, 8, 16)]), (P, 1))
    e = np.arange(EXPERTS)
    out["lower_expert"] = np.tile((e[None, :] < e[:, None]).reshape(-1), (P, 1))
    return {k: np.ascontiguousarray(v, np.float32) for k, v in out.items()}


PARAM_COLUMNS = {
    "c": KD, "c_2": KD, "norm_mix_g": 2 * KD, "norm_ffn_g": 2 * KD, "final_norm_g": KD, "b_mod": 4 * MODS,
    "norm_mix_2": 2 * KD, "norm_ffn_2": 2 * KD, "conv_w": 2 * 6, "sgu_norm_g": 2 * 256,
    "sgu_w": 2 * 512, "sgu_b": 2 * 256, "w_glow": 2 * KD * 16, "gla_w_gate": 2 * P, "gla_b_gate": 2,
    "gla_norm_g": 2, "hgrn_norm_g": 2, "hgrn_lower_bounds": 4, "moe_router": KD * EXPERTS,
    "w_ab": KD * 8, "gdn_conv_w_2": 12 * 4, "gdn_a_log_2": 4, "gdn_dt_bias_2": 4, "gdn_norm_2": 1,
    "pool_w_2": 4 * P, "pool_scale_2": 4, "ffn_conv_w_2": 2 * FF_TILES * 3, "ffn_conv_b_2": 2 * FF_TILES,
    "att_q_norm_2": 1, "att_k_norm_2": 1,
}


def columns_of(widths):
    at, out = 0, {}
    for name, n in widths.items():
        out[name] = (at, n)
        at += n
    return out, at



def build_program(nc, x_in, params_in, consts_in, stream_in, out, plan=PLAN):
    place = stream_plan(plan)
    total_slots = place["end"]
    const_at, const_n = columns_of({k: v.shape[1] for k, v in constant_columns().items()})
    param_at, param_n = columns_of(PARAM_COLUMNS)
    firsts = [n for n, kind in enumerate(plan) if kind.startswith("first")]

    with ExitStack() as ctx:
        def sb(name, shape):
            return ctx.enter_context(nc.sbuf_tensor(name, shape, F32))

        def sem(name):
            return ctx.enter_context(nc.semaphore(name))

        def steps(name, names):
            return Steps(sem(name), names)

        work_n = 16888
        shapes = {"ring": [P, RING, SLOT], "yT": [P, KD, T], "proj": [P, 12, 2, T], "ff_hid": [P, 4, T],
                  "work": [P, work_n]}
        rounded = {}
        with ExitStack() as same_place:
            for name, shape in shapes.items():
                rounded[name] = same_place.enter_context(nc.sbuf_tensor(name + "_rounded", shape, F32R))
        ring = sb("ring", shapes["ring"])
        yT = sb("yT", shapes["yT"])
        proj = sb("proj", shapes["proj"])
        ff_hid = sb("ff_hid", shapes["ff_hid"])
        work = sb("work", shapes["work"])
        ring_r, yT_r, ff_hid_r, work_r = (rounded[name] for name in ("ring", "yT", "ff_hid", "work"))
        pflat = proj[:, :, :, :].rearrange("p a b t -> p (a b t)")
        pflat_r = rounded["proj"][:, :, :, :].rearrange("p a b t -> p (a b t)")
        xT = sb("xT", [P, KD, T])
        hT = sb("hT", [P, KD, T])
        consts = sb("consts", [P, const_n])
        params = sb("params", [P, param_n])
        flag = ctx.enter_context(nc.sbuf_tensor("flag", [P, 1], mybir.dt.int32))
        mod = sb("mod", [P, 4 * MODS])
        cond = sb("cond", [P, 2, KD])
        rstd = sb("rstd", [P, T])
        gain = sb("gain", [P, KD])
        lbs = sb("lbs", [P, 2, 2, 2])
        lbw = sb("lbw", [P, 5, 2])
        ff_silu = sb("ff_silu", [P, 4, T])
        ff_mid = sb("ff_mid", [P, 4, T])

        banks = [ctx.enter_context(nc.psum_tensor(f"bank{i}", [P, 512], F32)) for i in range(6)]
        pair = ctx.enter_context(nc.psum_tensor("bank67", [P, 1024], F32))

        def bank(i, a=0, b=512):
            return banks[i][:, a:b] if i < 6 else pair[:, 512 * (i - 6) + a:512 * (i - 6) + b]

        def const(name):
            a, n = const_at[name]
            return consts[:, a:a + n]

        def param(name, layer=0, layers=1):
            a, n = param_at[name]
            n //= layers
            return params[:, a + layer * n:a + (layer + 1) * n]

        taken = [0]

        def take(n):
            taken[0] += n
            assert taken[0] <= work_n, taken[0]
            return work[:, taken[0] - n:taken[0]]

        gb = take(T)
        ge = take(4 * T).rearrange("p (a t) -> p a t", a=4)
        gz, gt = ge[:, 0, :], ge[:, 1, :]
        gk = take(2 * T).rearrange("p (a t) -> p a t", a=2)
        gdecay = take(NCH)
        gq = take(4 * T).rearrange("p (h t) -> p h t", h=4)
        gqe = take(4 * T).rearrange("p (h t) -> p h t", h=4)
        hb, hkey = take(2 * T), take(2 * T)
        he = take(4 * 2 * T).rearrange("p (a n) -> p a n", a=4)
        hz, hf = he[:, 0, :], he[:, 1, :]
        hk = take(4 * T).rearrange("p (a n) -> p a n", a=2)
        hdecay = take(2 * NCH)
        hq = take(4 * T).rearrange("p (f h t) -> p f h t", f=2, h=2)
        hqe = take(4 * T).rearrange("p (f h t) -> p f h t", f=2, h=2)
        v_chunks = hT[:, :, :].rearrange("p k t -> p (k t)")
        state = take(NCH * T)
        hd = state[:, 0:4 * T].rearrange("p (a n) -> p a n", a=2)
        gd = state[:, 4 * T:6 * T].rearrange("p (a t) -> p a t", a=2)
        ku_tok = take(2 * T)
        glow = ku_tok[:, 0:T]
        sgu_w = take(4 * P).rearrange("p (h t) -> p h t", h=HEADS)
        sgu_s = take(8)
        scores = ff_silu[:, :, :].rearrange("p a t -> p (a t)").rearrange("p (t n) -> p t n", t=NT)
        gates = ff_mid[:, :, :].rearrange("p a t -> p (a t)").rearrange("p (m n) -> p m n", m=2)
        osq = ff_hid[:, 0:2, :].rearrange("p a t -> p (a t)")
        orn = ff_hid[:, 2:4, :].rearrange("p a t -> p (a t)")
        vn = take(2 * T).rearrange("p (t d) -> p t d", t=NT)
        cv = take(2 * T).rearrange("p (f t) -> p f t", f=2)
        cacc = take(2 * T).rearrange("p (f t) -> p f t", f=2)
        used = [taken[0]]
        taken[0] = 0
        logits = take(NT * 8).rearrange("p (t e) -> p t e", t=NT)
        rk_gt = take(64).rearrange("p (a b) -> p a b", a=8)
        rk_eq = take(64).rearrange("p (a b) -> p a b", a=8)
        rank = take(NT * 8).rearrange("p (t e) -> p t e", t=NT)
        top = take(NT)
        den = take(NT)
        comb = take(NT * 8).rearrange("p (t e) -> p t e", t=NT)
        spot = take(NT * 8).rearrange("p (t e) -> p t e", t=NT)
        comb_row = take(EXPERTS * T).rearrange("p (e t) -> p e t", e=EXPERTS)
        spot_row = take(EXPERTS * T).rearrange("p (e t) -> p e t", e=EXPERTS)
        column, partition = take(P), take(1)
        most = take(1)
        moe_n = taken[0]
        comb_b = take(EXPERTS * NT * P).rearrange("p (e t m) -> p e t m", e=EXPERTS, t=NT)
        spot_b = take(EXPERTS * NT * P).rearrange("p (e t m) -> p e t m", e=EXPERTS, t=NT)
        h_tok = yT[:, :, :].rearrange("p k t -> p (k t)").rearrange("p (t d) -> p t d", t=NT)
        gathered_h = pflat[:, 0:KD * P].rearrange("p (k m) -> p k m", k=KD)
        expert_out = pflat[:, 1024:2048]
        pick = pflat[:, 2048:2048 + NT * P].rearrange("p (t m) -> p t m", t=NT)
        put_back = pflat[:, 2304:2304 + T]
        taken[0] = 0
        qkv = take(12 * T).rearrange("p (n t) -> p n t", n=12)
        l2 = take(8 * T)
        ab = take(NT * 8).rearrange("p (t e) -> p t e", t=NT)
        abt = take(NT * 8).rearrange("p (t e) -> p t e", t=NT)
        beta, gdec, anex, gccol, egc, kdf, bege = take(8), take(8), take(4), take(8), take(8), take(8), take(8)
        spread = take(2 * 8 * P).rearrange("p (a n m) -> p a n m", a=2, n=8)
        dec = take(8 * P)
        decs = take(8 * P)
        egrow = take(4 * P)
        qg = take(4 * P)
        kb = take(8 * P).rearrange("p (t n) -> p t n", t=NT)
        LT = take(8 * P).rearrange("p (t n) -> p t n", t=NT)
        PT = take(8 * P).rearrange("p (t n) -> p t n", t=NT)
        vb = take(8 * P)
        kbe, kdec = take(4 * P), take(4 * P)
        poolb = [ff_hid[:, :, :], pflat[:, 5120:6144].rearrange("p (n t) -> p n t", n=4)]
        X = pflat[:, 0:1024].rearrange("p (t n) -> p t n", t=NT)
        XT = pflat[:, 1024:2048].rearrange("p (t n) -> p t n", t=NT)
        Y = pflat[:, 2048:3072].rearrange("p (t n) -> p t n", t=NT)
        poolx = pflat[:, 4096:5120].rearrange("p (n t) -> p n t", n=4)
        MT = ff_silu[:, :, :].rearrange("p a t -> p (a t)").rearrange("p (t n) -> p t n", t=NT)
        vnew = l2[:, 0:1024].rearrange("p (t n) -> p t n", t=NT)
        wTn, S1 = l2[:, 1024:1536], l2[:, 1536:2048]
        zsilu = ff_mid[:, :, :].rearrange("p a t -> p (a t)")
        gosq = spread[:, 0, :, :].rearrange("p n m -> p (n m)")
        gorn = spread[:, 1, :, :].rearrange("p n m -> p (n m)")
        used.append(taken[0])
        taken[0] = 0
        qraw = take(2 * 512).rearrange("p (a n) -> p a n", a=2)
        qsq = take(2 * 512).rearrange("p (a n) -> p a n", a=2)
        qrn = take(2 * 512).rearrange("p (a n) -> p a n", a=2)
        qk = pflat[:, 0:6144].rearrange("p (b a g h t) -> p b a g h t", b=2, a=2, g=3, h=2)
        vtok = take(2 * 3 * 512).rearrange("p (b g t d) -> p b g t d", b=2, g=3, t=2)
        logit = take(2 * 768).rearrange("p (a n) -> p a n", a=2)
        prob = take(2 * 768).rearrange("p (a n) -> p a n", a=2)
        probT = take(2 * 768).rearrange("p (a n m) -> p a n m", a=2, n=6)
        top_q, neg_q, sum_q, inv_q = take(16), take(16), take(16), take(16)
        qgain = take(1)

        mod_at = work_n - MOD_SLOTS * COLS - MOD_GROUP * SLOT
        mod_ring = work[:, mod_at:mod_at + MOD_GROUP * SLOT].rearrange("p (s k n) -> p s k n", s=MOD_GROUP, k=KD)
        mod_acc = work[:, work_n - MOD_SLOTS * COLS:work_n].rearrange("p (s n) -> p s n", s=MOD_SLOTS)
        lead_ring = work[:, 0:MOD_LEAD * SLOT].rearrange("p (s k n) -> p s k n", s=MOD_LEAD, k=KD)
        lead_acc = pflat[:, 0:MOD_LEAD * COLS].rearrange("p (s n) -> p s n", s=MOD_LEAD)

        assert mod_at >= moe_n, (mod_at, moe_n)

        w_high = [work_r[:, 0:SLOT], work_r[:, SLOT:2 * SLOT], pflat_r[:, 0:SLOT]]
        h_high = yT_r
        h_low = pflat_r[:, SLOT:2 * SLOT].rearrange("p (k t) -> p k t", k=KD)
        hid_high = pflat_r[:, 2 * SLOT:2 * SLOT + 4 * T].rearrange("p (a t) -> p a t", a=4)
        assert mod_at >= 2 * SLOT

        weights_here = [sem(f"weights_here{i}") for i in range(RING)]
        weights_used = sem("weights_used")
        x_here, params_here, consts_here, stored = sem("x_here"), sem("params_here"), sem("consts_here"), sem("stored")
        cond_act = steps("cond_act", "cond")
        mod_here = sem("mod_here")
        lead_here = [sem(f"lead_here{i}") for i in range(MOD_LEAD // 2)]
        mod_part = sem("mod_part")
        mod_lead_pe, mod_rest_pe = steps("mod_lead_pe", "s"), steps("mod_rest_pe", "s")
        mod_lead, mod_rest = steps("mod_lead", "m"), steps("mod_rest", "m")
        x_vec = steps("x_vec", " ".join(f"x{k}" for k in range(KD)))
        norm_act = steps("norm_act", " ".join(f"q{k}" for k in range(KD)) + " root")
        ffn_out = sem("ffn_out")
        norm_pe = steps("norm_pe", "sum")
        norm_vec = steps("norm_vec", "gain rstd " + " ".join(f"s{k}" for k in range(KD)))
        shift_act = steps("shift_act", " ".join(f"h{k}" for k in range(KD)))
        proj_act = steps("proj_act", "p")
        ffn_half = sem("ffn_half")
        ffn_full = sem("ffn_full")
        high_act = steps("high_act", "h")
        low_pool = steps("low_pool", "h")
        split_high = sem("split_high")
        split_low = sem("split_low")
        ffn_mid = sem("ffn_mid")
        ffn_silu = sem("ffn_silu")
        ffn_hid = sem("ffn_hid")
        ffn_conv = sem("ffn_conv")
        zero_pool = steps("zero_pool", "zero")
        lb_vec = steps("lb_vec", "max d sum inv lb om")
        lb_act = steps("lb_act", "exp")
        glow_pe = steps("glow_pe", "glow z")
        gla_act = steps("gla_act", "glow t1 ln exps gate")
        gla_vec = steps("gla_vec", "z abs min run dist ku")
        hgrn_act = steps("hgrn_act", "e lnf exps gate")
        hgrn_vec = steps("hgrn_vec", "add sig f key run dist ku")
        v_pool = steps("v_pool", "vg0 vg1 vh0 vh1")
        la_pe = steps("la_pe", " ".join(f"{n}{m}" for m in "gh" for n in ("tr", "sa", "sb", "u0", "u1", "o", "ms")))
        la_act = steps("la_act", " ".join(f"{n}{m}" for m in "gh" for n in ("ku", "osq", "root")))
        la_vec = steps("la_vec", " ".join(f"{n}{m}" for m in "gh" for n in (
            ["sa", "sb"] + [f"st{c}" for c in range(1, NCH)] + ["rn", "on", "y"])))
        sgu_pool = steps("sgu_pool", "w")
        sgu_act = steps("sgu_act", "sq root")
        sgu_vec = steps("sgu_vec", "sum mu d rs vn mix y")
        sgu_pe = steps("sgu_pe", "mix")
        conv_vec = steps("conv_vec", "cv c0 c1 c2 y")
        moe_pe = steps("moe_pe", "logits turned spots rows")
        moe_act = steps("moe_act", "turned exp rows")
        moe_vec = steps("moe_vec", "copy max neg " + " ".join(f"gt{t} eq{t} low{t} sum{t} rk{t}" for t in range(NT)) +
                        " sel pick den inv w spots spot most flag spread")
        again_here = [sem(f"again_here{i}") for i in range(RING)]
        passes = []
        for r, (here, used) in enumerate(((weights_here, weights_used), (again_here, sem("again_used")))):
            passes.append(dict(
                here=here, used=used,
                lower=steps(f"moe_lower{r}", "s"),
                picks=sem(f"moe_picks{r}"),
                backs=sem(f"moe_backs{r}"),
                gathered=sem(f"moe_gathered{r}"),
                tokens=sem(f"moe_tokens{r}"),
                silu=sem(f"moe_silu{r}"),
                hid=sem(f"moe_hid{r}"),
                turned=sem(f"moe_turned{r}"),
                hid_t=sem(f"moe_hid_t{r}"),
                outs=sem(f"moe_outs{r}"),
                scattered=sem(f"moe_scattered{r}"),
                added=sem(f"moe_added{r}")))
        gdn_pe = steps("gdn_pe", "ab gc grows l2 brows kk0 kk1 tr " +
                       " ".join(f"{s}{l}{t}" for l in range(LEVELS) for s in "yz" for t in range(NT)) +
                       " v0 w s1 v1 o ms pool")
        gdn_act = steps("gdn_act", "e ln dec silu_qk sq silu_v l2root vb " +
                        " ".join(f"y{l}{t}" for l in range(LEVELS) for t in range(NT)) +
                        " vn0 w S1 vn1 osq root zs pool")
        gdn_vec = steps("gdn_vec", "ab adt aabs b1 b2 sp g spread gcc dd dm a0 a1 a2 a3 b0 b4 b5 b6 l2i qkn kb0 kb1 qg "
                        "lp0 lp1 kt " +
                        " ".join(f"{s}{l}{t}" for l in range(LEVELS) for s in "mx" for t in range(NT)) +
                        " rn on y")
        gdn_pool = steps("gdn_pool", "w2 w4 w8 w16 count less ident")
        att_pe = {s: steps(f"att_pe_{s}", s) for s in ("ms", "scores", "turned", "out")}
        att_act = {s: steps(f"att_act_{s}", s) for s in ("sq", "root", "v", "exp", "turned", "out")}
        att_vec = {s: steps(f"att_vec_{s}", s) for s in ("rn", "qk", "logit", "top", "neg", "inv", "prob")}
        gain_vec = steps("gain_vec", "q")

        def slot_k(n):
            return ring[:, n % RING, :].rearrange("p (k n) -> p k n", k=KD)

        def down_k(n):
            return ring[:, n % RING, :].rearrange("p (j n) -> p j n", j=2)

        def ff_slot(first, c):
            return first if isinstance(c, int) and c == 0 else first - 1 + 3 * c

        def ff_down(first, c, chunks):
            return first + 3 * chunks - 1 if isinstance(c, int) and c == chunks - 1 else first + 4 + 3 * c

        def f32(ap):
            return ap.bitcast(F32)

        SPLITS = 3 * DENSE_CHUNKS - 2
        dense_before = [sum(k != "first1" for k in plan[:n]) for n in range(len(plan))]

        def each_chunk(eng, chunks, visit):
            visit(0, 0)
            visit(1, 1)
            with eng.Fori(1, chunks // 2) as i:
                for u in range(2):
                    visit(2 * i + u, u)
            if chunks % 2:
                visit(chunks - 1, 0)

        def chunks_of(kind):
            return 0 if kind == "first1" else DENSE_CHUNKS

        tiles_before, total = [], 0
        for kind in plan:
            tiles_before.append(total)
            total += 2 * chunks_of(kind)
        mid_before, total = [], 0
        for kind in plan:
            mid_before.append(total)
            total += 2 * chunks_of(kind) if kind in ("even", "odd") else 0
        conv_before = [2 * DENSE_CHUNKS * sum(k in ("even", "odd") for k in plan[:n]) for n in range(len(plan))]
        proj_before = [sum({"first0": 12, "first1": 12, "even": 10, "odd": 0}[k] for k in plan[:n])
                       for n in range(len(plan))]

        def mod_columns(layer, what):
            a = layer * MODS + what * KD
            return mod[:, a:a + KD]

        def slots_before(m):
            return MOD_LEAD + (m - 1) * MOD_SLOTS if m else 0

        def cond_of(m):
            return cond[:, 0 if plan[m].startswith("first") else 1, :]

        norms = []
        for n, kind in enumerate(plan):
            norms += [(n, 0), (n, 1)] + ([(n, 2)] if kind == "first1" else [])

        def x_ready(u, k=KD - 1):
            if norms[u - 1][1] == 2:
                return norm_vec.at(f"s{k}", u - 1)
            return x_vec.at(f"x{k}", u - 1 - sum(which == 2 for _, which in norms[:u]))

        def norm_gain(n, which):
            kind, layer = plan[n], LAYER[plan[n]]
            if which == 2:
                return param("final_norm_g")
            if kind.startswith("first"):
                return param(("norm_mix_g", "norm_ffn_g")[which], layer, 2)
            return param(("norm_mix_2", "norm_ffn_2")[which], {"even": 0, "odd": 1}[kind], 2)

        moe_first = place[f"ffn{plan.index('first1')}"] if "first1" in plan else 0
        EXPERT_SLOTS = 3 * EXPERT_CHUNKS
        EXPERT_ROUNDS = EXPERT_SLOTS // RING

        def each_expert(eng, visit):
            visit(0)
            with eng.Fori(1, EXPERTS - 1) as e:
                visit(e)
            visit(EXPERTS - 1)

        def expert_chunks(eng, step):
            step(0, 0, 0)
            step(0, 1, 1)
            with eng.Fori(1, EXPERT_CHUNKS // 2 - 1) as i:
                step(i, 0, None)
                step(i, 1, None)
            step(EXPERT_CHUNKS // 2 - 1, 0, EXPERT_CHUNKS - 2)
            step(EXPERT_CHUNKS // 2 - 1, 1, EXPERT_CHUNKS - 1)

        def is_first(e, c=0):
            return isinstance(e, int) and e == 0 and c in (0, 1)

        def is_last(e, c=EXPERT_CHUNKS - 1):
            return isinstance(e, int) and e == EXPERTS - 1 and c == EXPERT_CHUNKS - 1

        def more_tokens(eng):
            eng.wait_ge(*moe_vec.at("flag", 0))
            return eng.value_load(flag[0:1, 0:1], min_val=0, max_val=1) > 0

        block = ctx.enter_context(nc.Block())

        @block.sync
        def _(sp):
            sp.wait_ge(lead_here[2], 32)

            def load(first, end):
                lo = min(end, -(-first // RING) * RING)
                lo = max(lo, min(RING, end))
                hi = max(lo, end // RING * RING)
                for n in list(range(first, lo)):
                    if n >= RING:
                        sp.wait_ge(weights_used, n - RING + 1)
                    sp.dma_start(ring[:, n % RING, :], stream_in[n]).then_inc(weights_here[n % RING], 16)
                if hi > lo:
                    with sp.Fori(lo // RING, hi // RING) as i:
                        for r in range(RING):
                            sp.wait_ge(weights_used, (i - 1) * RING + r + 1)
                            sp.dma_start(ring[:, r, :],
                                         stream_in[bass.ds(i * RING + r, 1)].rearrange("a p n -> p (a n)"))\
                              .then_inc(weights_here[r], 16)
                for n in range(hi, end):
                    sp.wait_ge(weights_used, n - RING + 1)
                    sp.dma_start(ring[:, n % RING, :], stream_in[n]).then_inc(weights_here[n % RING], 16)

            if "first1" in plan:
                moe_end = moe_first + 3 * MOE_CHUNKS
                load(0, moe_end)
                with sp.If(more_tokens(sp)):
                    sp.wait_ge(weights_used, moe_end)
                    for n in range(RING):
                        sp.dma_start(ring[:, (moe_first + n) % RING, :], stream_in[moe_first + n])\
                          .then_inc(again_here[(moe_first + n) % RING], 16)
                    with sp.Fori(1, 3 * MOE_CHUNKS // RING) as i:
                        for r in range(RING):
                            sp.wait_ge(passes[1]["used"], (i - 1) * RING + r + 1)
                            sp.dma_start(ring[:, (moe_first + r) % RING, :],
                                         stream_in[bass.ds(i * RING + (moe_first + r), 1)]
                                         .rearrange("a p n -> p (a n)"))\
                              .then_inc(again_here[(moe_first + r) % RING], 16)
                    sp.wait_ge(passes[1]["used"], 3 * MOE_CHUNKS)
                load(moe_end, total_slots)
            else:
                load(0, total_slots)
            sp.wait_ge(*x_ready(len(norms)))
            sp.dma_start(out, xT[:, :, :]).then_inc(stored, 16)
            sp.wait_ge(stored, 16)

        @block.gpsimd
        def _(pool):
            def first_mixers(l):
                n = firsts[l]
                if l == 0:
                    pool.wait_ge(consts_here, 16)
                    pool.wait_ge(params_here, 16)
                if n:
                    pool.wait_ge(*mod_rest.at("m", n))
                else:
                    pool.wait_ge(mod_part, MOD_LEAD * KD)
                for buf in (gq, gqe, hq, hqe):
                    last = pool.memset(buf, 0.0)
                last.then_inc(*zero_pool.step("zero"))
                pool.tensor_tensor(sgu_w, param("sgu_w", LAYER[plan[firsts[l]]], 2).rearrange("p (h t) -> p h t", h=HEADS),
                                   const("upto").unsqueeze(1).to_broadcast([P, HEADS, P]), ALU.mult)\
                    .then_inc(*sgu_pool.step("w"))
                for m, slot in (("g", AV), ("h", HI)):
                    if m == "g":
                        pool.wait_ge(*proj_act.at("p", proj_before[n] + 11))
                    for tt in range(NT):
                        if m == "g" and tt == 0:
                            pass
                        elif tt == 1:
                            pool.wait_ge(*la_pe.at("u0" + m, l))
                        else:
                            pool.wait_ge(*la_pe.at("u1g", l))
                        pool.tensor_tensor(
                            v_chunks.rearrange("p (c v) -> p c v", c=8),
                            proj[:, slot, tt, :].unsqueeze(1).to_broadcast([P, 8, T]),
                            const("chunk_of").unsqueeze(2).to_broadcast([P, 8, T]), ALU.mult)\
                            .then_inc(*v_pool.step(f"v{m}{tt}"))

            def even_mixers(n):
                pool.wait_ge(*proj_act.at("p", proj_before[n] + 9))
                src = poolx
                for j in range(4):
                    d, lag = poolb[j % 2], 2 ** j
                    if j:
                        pool.wait_ge(*gdn_pool.at(f"w{lag}", 0))
                    pool.tensor_copy(d[:, j:4, 0:lag], src[:, j:4, 0:lag])
                    pool.tensor_tensor(d[:, j:4, lag:T], src[:, j:4, lag:T], src[:, j:4, 0:T - lag], ALU.add)\
                        .then_inc(*gdn_pool.step(f"w{2 * lag}"))
                    src = d
                pool.wait_ge(*gdn_pool.at("w16", 0))
                counts = const("per_count").rearrange("p (g t) -> p g t", g=4)
                for g in range(4):
                    d = poolb[g % 2][:, g, :]
                    last = pool.tensor_tensor(d, d, counts[:, g, :], ALU.mult)
                last.then_inc(*gdn_pool.step("count"))
                pool.wait_ge(*gdn_pool.at("count", 0))
                for g in range(4):
                    d = poolb[g % 2][:, g, :]
                    last = pool.tensor_tensor(d, d, poolx[:, g, :], ALU.subtract)
                last.then_inc(*gdn_pool.step("less"))
                pool.wait_ge(*gdn_vec.at("b6", 0))
                for buf in (X, XT):
                    last = pool.tensor_copy(buf.rearrange("p t (h n) -> p (t h) n", h=HEADS),
                                            const("ident").unsqueeze(1).to_broadcast([P, 8, P]))
                last.then_inc(*gdn_pool.step("ident"))

            def feed_forward(n):
                first, before = place[f"ffn{n}"] + 2, dense_before[n] * SPLITS
                pool.wait_ge(*high_act.at("h", dense_before[n]))
                pool.tensor_tensor(h_low, hT[:, :, :], f32(h_high[:, :, :]), ALU.subtract)\
                    .then_inc(*low_pool.step("h"))

                def low(r, q):
                    w = ring[:, (first + r) % RING, :]
                    pool.wait_ge(split_high, q + (before + 1))
                    pool.tensor_tensor(ring_r[:, (first + r) % RING, :], w, f32(w_high[r % 3]), ALU.subtract).then_inc(split_low, 1)

                with pool.Fori(0, SPLITS // RING) as i:
                    for r in range(RING):
                        low(r, i * RING + r)
                for q in range(SPLITS // RING * RING, SPLITS):
                    low(q % RING, q)

            for n, kind in enumerate(plan):
                if kind.startswith("first"):
                    first_mixers(firsts.index(n))
                elif kind == "even":
                    even_mixers(n)
                if kind != "first1":
                    feed_forward(n)

        @block.scalar
        def _(act):
            act.dma_start(params[:, :], params_in).then_inc(params_here, 16)
            for s in range(MOD_LEAD):
                act.dma_start(lead_ring[:, s, :, :].rearrange("p k n -> p (k n)"), stream_in[place["mod0"] + s])\
                   .then_inc(lead_here[s // 2], 16)
            act.dma_start(xT[:, :, :], x_in).then_inc(x_here, 16)
            act.dma_start(consts[:, :], consts_in).then_inc(consts_here, 16)
            act.wait_ge(params_here, 16)
            act.activation(cond[:, 0, :], param("c"), ACT.Silu)
            act.activation(cond[:, 1, :], param("c_2"), ACT.Silu).then_inc(*cond_act.step("cond"))
            act.wait_ge(*lb_vec.at("d", 0))
            act.activation(lbw[:, 1:3, :], lbw[:, 1:3, :], ACT.Exp).then_inc(*lb_act.step("exp"))

            def norm(n, which):
                u = norms.index((n, which))
                if u == 0:
                    act.wait_ge(x_here, 16)
                for k in range(KD):
                    if u:
                        act.wait_ge(*x_ready(u, k))
                    act.activation(hT[:, k, :], xT[:, k, :], ACT.Square).then_inc(*norm_act.step(f"q{k}"))
                act.wait_ge(*norm_pe.at("sum", u))
                act.activation(rstd[:, :], bank(4, 0, T), ACT.Sqrt, bias=EPS, scale=1.0 / D)\
                   .then_inc(*norm_act.step("root"))
                if which == 2:
                    return
                shift = mod_columns(n, 3 * which)
                for k in range(KD):
                    act.wait_ge(*norm_vec.at(f"s{k}", u))
                    act.activation(hT[:, k, :], yT[:, k, :], ACT.Identity, bias=shift[:, k:k + 1])\
                       .then_inc(*shift_act.step(f"h{k}"))

            def load_modulation(m, group):
                act.wait_ge(mod_part, group * (MOD_GROUP * KD) + slots_before(m) * KD)
                for s in range(MOD_GROUP):
                    act.dma_start(mod_ring[:, s, :, :].rearrange("p k n -> p (k n)"),
                                  stream_in[bass.ds(group * MOD_GROUP + (place[f"mod{m}"] + s), 1)]
                                  .rearrange("a p n -> p (a n)")).then_inc(mod_here, 16)

            def evacuate(n, slots):
                for s in slots:
                    act.wait_ge(weights_used, place[f"in{n}"] + s + 1)
                    act.activation(proj[:, s, :, :], bank(s % 4).rearrange("p (a t) -> p a t", a=2), ACT.Copy)\
                       .then_inc(*proj_act.step("p"))

            def exps(l, steps_act, steps_vec, decay, dist, run, e, scale):
                act.wait_ge(*steps_vec.at("dist", l))
                act.activation(e[:, 0, :], dist[:, 0, :], ACT.Exp, scale=scale)
                act.activation(e[:, 1, :], dist[:, 0, :], ACT.Exp, scale=-scale)
                act.activation(e[:, 2, :], dist[:, 1, :], ACT.Exp, scale=scale)
                act.activation(e[:, 3, :], run, ACT.Exp, scale=scale)
                act.activation(decay, run.rearrange("p (c i) -> p c i", i=LA)[:, :, LA - 1], ACT.Exp, scale=scale)\
                   .then_inc(*steps_act.step("exps"))

            def first_mixers(l):
                n = firsts[l]
                act.wait_ge(*glow_pe.at("glow", l))
                act.activation(glow[0:16, :], bank(4, 0, T)[0:16, :], ACT.Copy).then_inc(*gla_act.step("glow"))
                evacuate(n, [HF])
                act.wait_ge(*gla_vec.at("abs", l))
                act.activation(gt, gt, ACT.Exp, scale=-1.0).then_inc(*gla_act.step("t1"))
                act.wait_ge(*proj_act.at("p", proj_before[n] + HF))
                act.activation(hz, proj[:, HF, :, :].rearrange("p a t -> p (a t)"), ACT.Exp, scale=-1.0)\
                   .then_inc(*hgrn_act.step("e"))
                act.wait_ge(*gla_act.at("t1", l))
                act.activation(gt, gt, ACT.Ln, bias=1.0).then_inc(*gla_act.step("ln"))
                exps(l, gla_act, gla_vec, gdecay, gd, gb, ge, 1.0 / 16.0)
                evacuate(n, [HQ])
                act.wait_ge(*hgrn_vec.at("key", l))
                act.activation(hz, hf, ACT.Ln).then_inc(*hgrn_act.step("lnf"))
                evacuate(n, [HI, AQK])
                exps(l, hgrn_act, hgrn_vec, hdecay, hd, hb, he, 1.0)
                evacuate(n, [AV, SV])
                act.wait_ge(*sgu_vec.at("d", l))
                for tt in range(NT):
                    last = act.activation(cacc[:, tt, :], vn[:, tt, :], ACT.Square, accum_out=sgu_s[:, 2 + tt:3 + tt])
                last.then_inc(*sgu_act.step("sq"))
                act.wait_ge(*sgu_act.at("sq", l))
                act.activation(sgu_s[:, 4:6], sgu_s[:, 2:4], ACT.Sqrt, bias=EPS, scale=1.0 / T)\
                   .then_inc(*sgu_act.step("root"))
                evacuate(n, [SU, CC, CX, CB, HG, AR])
                act.wait_ge(*proj_act.at("p", proj_before[n] + AR))
                act.activation(gates[:, 0, :], proj[:, AR, :, :].rearrange("p a t -> p (a t)"), ACT.Silu)\
                   .then_inc(*gla_act.step("gate"))
                act.activation(gates[:, 1, :], proj[:, HG, :, :].rearrange("p a t -> p (a t)"), ACT.Silu)\
                   .then_inc(*hgrn_act.step("gate"))
                for m in "gh":
                    w = 2 * P if m == "g" else 4 * P
                    act.wait_ge(*la_pe.at("tr" + m, l))
                    act.activation(ku_tok[:, 0:w], bank(5, 0, w), ACT.Copy).then_inc(*la_act.step("ku" + m))
                    act.wait_ge(*la_pe.at("o" + m, l))
                    act.activation(osq, bank(5), ACT.Square).then_inc(*la_act.step("osq" + m))
                    act.wait_ge(*la_pe.at("ms" + m, l))
                    act.activation(orn, bank(4), ACT.Sqrt, bias=EPS, scale=1.0 / 64)\
                       .then_inc(*la_act.step("root" + m))

            def router(n):
                act.wait_ge(*moe_pe.at("turned", 0))
                for b in range(4):
                    last = act.activation(h_tok[:, b // 2, b % 2 * 512:b % 2 * 512 + 512], bank(b), ACT.Copy)
                last.then_inc(*moe_act.step("turned"))
                act.wait_ge(*moe_vec.at("neg", 0))
                for tt in range(NT):
                    last = act.activation(comb[:, tt, :], logits[:, tt, :], ACT.Exp, bias=top[:, tt:tt + 1])
                last.then_inc(*moe_act.step("exp"))
                act.wait_ge(*moe_pe.at("rows", 0))
                for b in range(4):
                    act.activation(comb_row[:, 2 * b:2 * b + 2, :], bank(b).rearrange("p (e t) -> p e t", e=2),
                                   ACT.Copy)
                    last = act.activation(spot_row[:, 2 * b:2 * b + 2, :],
                                          bank(4 + b).rearrange("p (e t) -> p e t", e=2), ACT.Copy)
                last.then_inc(*moe_act.step("rows"))

            def experts(r):
                m, base, next_layer = passes[r], (moe_first, 0)[r], plan.index("first1") + 1

                def evacuate_tokens(e):
                    act.wait_ge(m["gathered"], e + 1)
                    for b in range(2):
                        last = act.activation(gathered_h[:, 4 * b:4 * b + 4, :],
                                              bank(6 + b).rearrange("p (k m) -> p k m", k=4), ACT.Copy)
                    last.then_inc(m["tokens"], 1)

                def silu(g, u, free, up_done):
                    act.wait_ge(m["used"], up_done)
                    if not free:
                        act.wait_ge(m["hid"], g - 1)
                    act.activation(ff_silu[:, u, :], bank(2 + u, 0, T), ACT.Silu).then_inc(m["silu"], 1)

                def visit(e):
                    def step(i, u, c):
                        g = e * EXPERT_CHUNKS + i * 2 + u
                        if c == 0 and r == 0 and next_layer < len(plan):
                            load_modulation(next_layer, e)
                        act.wait_ge(m["turned"], g + 1)
                        if not is_first(e, c):
                            act.wait_ge(m["used"], g * 3 + (base - 1))
                        act.activation(ff_hid[:, u, :], bank(4 + u, 0, T), ACT.Copy).then_inc(m["hid_t"], 1)
                        if not is_last(e, c):
                            silu(g + 1, 1 - u, is_first(e, c) and c == 0, g * 3 + (base + 4))
                        if c == EXPERT_CHUNKS - 2 and not is_last(e):
                            evacuate_tokens(e + 1)
                        if c == EXPERT_CHUNKS - 1:
                            act.wait_ge(m["used"], base + 3 * MOE_CHUNKS if is_last(e) else g * 3 + (base + 5))
                            if not is_first(e):
                                act.wait_ge(m["scattered"], 2 * e)
                            for b in range(2):
                                last = act.activation(expert_out[:, b * 512:b * 512 + 512], bank(b), ACT.Copy)
                            last.then_inc(m["outs"], 1)
                    expert_chunks(act, step)

                evacuate_tokens(0)
                silu(0, 0, True, base + 2)
                each_expert(act, visit)

            def even_mixers(n):
                act.wait_ge(*gdn_vec.at("aabs", 0))
                act.activation(beta.rearrange("p (t h) -> p t h", t=NT), ab[:, :, 0:4], ACT.Exp, scale=-1.0)
                act.activation(anex, param("gdn_a_log_2"), ACT.Exp)
                act.activation(abt[:, :, 0:4], abt[:, :, 0:4], ACT.Exp, scale=-1.0).then_inc(*gdn_act.step("e"))
                act.wait_ge(*gdn_act.at("e", 0))
                act.activation(abt[:, :, 0:4], abt[:, :, 0:4], ACT.Ln, bias=1.0).then_inc(*gdn_act.step("ln"))
                act.wait_ge(*gdn_vec.at("dd", 0))
                act.activation(dec, dec, ACT.Exp)
                act.activation(egrow, bank(7), ACT.Exp)
                act.activation(egc, gccol, ACT.Exp)
                act.activation(kdf, kdf, ACT.Exp).then_inc(*gdn_act.step("dec"))
                evacuate(n, range(6))
                act.wait_ge(*gdn_vec.at("a3", 0))
                act.activation(qkv[:, 0:8, :], qkv[:, 0:8, :], ACT.Silu).then_inc(*gdn_act.step("silu_qk"))
                evacuate(n, [6])
                act.wait_ge(*gdn_act.at("silu_qk", 0))
                act.activation(l2.rearrange("p (n t) -> p n t", n=8), qkv[:, 0:8, :], ACT.Square)\
                   .then_inc(*gdn_act.step("sq"))
                evacuate(n, [7])
                act.wait_ge(*gdn_vec.at("b6", 0))
                act.activation(qkv[:, 8:12, :], qkv[:, 8:12, :], ACT.Silu).then_inc(*gdn_act.step("silu_v"))
                evacuate(n, [8, 9])
                act.wait_ge(*gdn_pe.at("l2", 0))
                for b in range(4):
                    last = act.activation(l2[:, 512 * b:512 * b + 512], bank(b), ACT.Sqrt, bias=EPS)
                last.then_inc(*gdn_act.step("l2root"))
                act.wait_ge(*gdn_pe.at("tr", 0))
                for m in range(8):
                    last = act.activation(vb[:, m * P:m * P + P], pair[:, m * P:m * P + P], ACT.Copy,
                                          scale=beta[:, m:m + 1])
                last.then_inc(*gdn_act.step("vb"))
                for l in range(LEVELS):
                    for t in range(NT):
                        act.wait_ge(*gdn_pe.at(f"y{l}{t}", 0))
                        act.activation(Y[:, t, :], bank(t), ACT.Copy).then_inc(*gdn_act.step(f"y{l}{t}"))
                act.wait_ge(*gdn_pe.at("v0", 0))
                act.activation(vnew[:, 0, :], bank(0), ACT.Copy).then_inc(*gdn_act.step("vn0"))
                act.wait_ge(*gdn_pe.at("w", 0))
                act.activation(wTn, bank(1), ACT.Copy, scale=-1.0).then_inc(*gdn_act.step("w"))
                act.wait_ge(*gdn_pe.at("s1", 0))
                act.activation(S1, bank(2), ACT.Copy).then_inc(*gdn_act.step("S1"))
                act.wait_ge(*gdn_pe.at("v1", 0))
                act.activation(vnew[:, 1, :], bank(3), ACT.Copy).then_inc(*gdn_act.step("vn1"))
                act.wait_ge(*gdn_pe.at("o", 0))
                act.activation(gosq, pair[:, :], ACT.Square).then_inc(*gdn_act.step("osq"))
                act.wait_ge(*gdn_pe.at("ms", 0))
                act.activation(gorn[:, 0:512], bank(4), ACT.Sqrt, bias=EPS, scale=1.0 / P)
                act.activation(gorn[:, 512:1024], bank(5), ACT.Sqrt, bias=EPS, scale=1.0 / P)\
                   .then_inc(*gdn_act.step("root"))
                act.activation(zsilu, pflat[:, 3072:4096], ACT.Silu).then_inc(*gdn_act.step("zs"))
                act.wait_ge(*gdn_pe.at("pool", 0))
                for g in range(4):
                    last = act.activation(yT[:, 4 + g, :], bank(2 + g // 2, g % 2 * T, g % 2 * T + T), ACT.Copy,
                                          scale=param("pool_scale_2")[:, g:g + 1])
                last.then_inc(*gdn_act.step("pool"))

            def odd_mixers(n):
                def unit_exp(u):
                    w = ATT_GROUPS * (u % 2 + 1) * P
                    act.wait_ge(*att_vec["neg"].at("neg", u))
                    if u >= 2:
                        act.wait_ge(*att_pe["turned"].at("turned", u - 2))
                    act.activation(prob[:, u % 2, 0:w], logit[:, u % 2, 0:w], ACT.Exp, bias=neg_q[:, u:u + 1],
                                   accum_out=sum_q[:, u:u + 1]).then_inc(*att_act["exp"].step("exp"))

                def unit_turned(u):
                    blocks = ATT_GROUPS * (u % 2 + 1)
                    act.wait_ge(*att_pe["turned"].at("turned", u))
                    if u >= 2:
                        act.wait_ge(*att_pe["out"].at("out", u - 2))
                    a = min(blocks, 4)
                    last = act.activation(probT[:, u % 2, 0:a, :], bank(4, 0, a * P).rearrange("p (n m) -> p n m", n=a),
                                          ACT.Copy)
                    if blocks > 4:
                        last = act.activation(probT[:, u % 2, 4:6, :],
                                              bank(5, 0, 2 * P).rearrange("p (n m) -> p n m", n=2), ACT.Copy)
                    last.then_inc(*att_act["turned"].step("turned"))

                def unit_out(u):
                    act.wait_ge(*att_pe["out"].at("out", u))
                    act.activation(yT[:, u // 2, u % 2 * P:u % 2 * P + P], bank(3, 0, P), ACT.Copy)\
                       .then_inc(*att_act["out"].step("out"))

                for hp in range(5):
                    for s in range(9):
                        if hp < 4:
                            at, g, j = place[f"in{n}"] + hp * 9 + s, s // 3, s % 3
                            q = hp * 6 + g * 2 + j
                            act.wait_ge(weights_used, at + 1)
                            if j < 2:
                                if q >= 2:
                                    act.wait_ge(*att_vec["qk"].at("qk", q - 2))
                                act.activation(qraw[:, q % 2, :], bank((hp * 9 + s) % 2), ACT.Copy)
                                act.activation(qsq[:, q % 2, :], bank((hp * 9 + s) % 2), ACT.Square)\
                                   .then_inc(*att_act["sq"].step("sq"))
                            else:
                                if hp >= 2 and g == 0:
                                    act.wait_ge(*att_pe["out"].at("out", 4 * (hp - 1) - 1))
                                act.activation(vtok[:, hp % 2, g, :, :],
                                               bank((hp * 9 + s) % 2).rearrange("p (t d) -> p t d", t=2), ACT.Copy)\
                                   .then_inc(*att_act["v"].step("v"))
                        if hp >= 1 and s < 8:
                            u = 4 * (hp - 1) + s // 2
                            if s % 2 == 0:
                                unit_exp(u)
                            else:
                                unit_turned(u)
                        if hp >= 1 and s >= 2 and s % 2 == 0:
                            unit_out(4 * (hp - 1) + s // 2 - 1)
                        if hp < 4 and s % 3 < 2:
                            act.wait_ge(*att_pe["ms"].at("ms", q))
                            act.activation(qrn[:, q % 2, :], bank(2), ACT.Sqrt, bias=EPS, scale=1.0 / P)\
                               .then_inc(*att_act["root"].step("root"))

            def feed_forward(n, kind):
                base, first = tiles_before[n], place[f"ffn{n}"]

                def high(c, odd, r):
                    at = 3 * odd + r + 2
                    rounds = (first + at) // RING + 1
                    if isinstance(c, int):
                        act.wait_ge(weights_here[(first + at) % RING], 16 * (rounds + (c - odd) // 2))
                        if c:
                            act.wait_ge(weights_used, first + 3 * c + r)
                    else:
                        act.wait_ge(weights_here[(first + at) % RING], (c - odd) * 8 + 16 * rounds)
                        act.wait_ge(weights_used, c * 3 + (first + r))
                    act.activation(w_high[r], ring[:, (first + at) % RING, :], ACT.Copy).then_inc(split_high, 1)

                act.wait_ge(*shift_act.at("h7", 2 * n + 1))
                act.activation(h_high[:, :, :], hT[:, :, :], ACT.Copy).then_inc(*high_act.step("h"))

                def visit(c, odd):
                    if n + 1 < len(plan) and not isinstance(c, int):
                        load_modulation(n + 1, c - 2)
                    high(c, odd, 0)
                    if isinstance(c, int) and c == 0:
                        high(c, odd, 1)
                    tiles(c, odd)
                    if not (isinstance(c, int) and c in (0, DENSE_CHUNKS - 1)):
                        high(c, odd, 1)
                    if not (isinstance(c, int) and c == DENSE_CHUNKS - 1):
                        high(c, odd, 2)

                def tiles(c, odd):
                    for j in range(2):
                        t = base + 2 * c + j
                        b = 2 * odd + j
                        if not isinstance(c, int) or c >= 2:
                            act.wait_ge(ffn_hid, t - 3)
                        if kind in ("even", "odd"):
                            act.wait_ge(ffn_mid, mid_before[n] + 2 * c + j + 1)
                            act.activation(ff_silu[:, b, :], ff_mid[:, b, :], ACT.Silu).then_inc(ffn_silu, 1)
                            continue
                        if j == 0:
                            act.wait_ge(ffn_half, base // 2 + c + 1)
                        else:
                            act.wait_ge(weights_used, ff_slot(first, c) + 2)
                        act.activation(ff_silu[:, b, :], bank(4 + b, 0, T), ACT.Silu).then_inc(ffn_silu, 1)
                each_chunk(act, chunks_of(kind), visit)

            for n, kind in enumerate(plan):
                norm(n, 0)
                if kind.startswith("first"):
                    first_mixers(firsts.index(n))
                elif kind == "even":
                    even_mixers(n)
                else:
                    odd_mixers(n)
                norm(n, 1)
                if kind == "first1":
                    router(n)
                    experts(0)
                    with act.If(more_tokens(act)):
                        experts(1)
                    norm(n, 2)
                else:
                    feed_forward(n, kind)

        @block.tensor
        def _(pe):
            def mm(o, a, b, start=True, stop=True):
                return pe.matmul(o, lhsT=a, rhs=b, start=start, stop=stop, skip_group_check=True)

            def arrive(at, i=None):
                rounds = at // RING + 1
                pe.wait_ge(weights_here[at % RING], 16 * rounds if i is None else i * 16 + 16 * rounds)

            def product(at, to, src, token_major=False, ready=None):
                arrive(at)
                w = slot_k(at)
                for t in range(2):
                    for k in range(KD):
                        if ready and t == 0:
                            ready(k)
                        a, b = w[:, k, t * P:t * P + P], src[:, k, :]
                        if token_major:
                            a, b = src[:, k, t * P:t * P + P], w[:, k, :]
                        last = mm(to[:, t * T:t * T + T], a, b, k == 0, k == KD - 1)
                last.then_inc(weights_used, 1)

            def project(n, slots, token_major=()):
                for s in slots:
                    if s >= 4:
                        pe.wait_ge(*proj_act.at("p", proj_before[n] + s - 4))
                    product(place[f"in{n}"] + s, bank(s % 4), hT, s in token_major)

            def modulate(count):
                for _ in range(min(count, MOD_SLOTS - MOD_LEAD - mod_done[0])):
                    s = mod_done[0]
                    mod_done[0] += 1
                    at = place["mod_rest"] + s
                    arrive(at)
                    for t in range(2):
                        for k in range(KD):
                            last = mm(bank(7, 2 * s + t, 2 * s + t + 1), slot_k(at)[:, k, t * P:t * P + P],
                                      cond_of(0)[:, k:k + 1], k == 0, k == KD - 1)
                    last.then_inc(weights_used, 1)

            def sum_modulation(b, acc, first, end):
                for t in range(2 * first, 2 * end):
                    a = t - 2 * first
                    last = mm(bank(b, a, a + 1), acc[:, t // 2, t % 2 * P:t % 2 * P + P], const("ones")[:, 0:1])
                return last

            mod_done = [0]

            def norm(n, which):
                u = norms.index((n, which))
                for k in range(KD):
                    pe.wait_ge(*norm_act.at(f"q{k}", u))
                    last = mm(bank(4, 0, T), const("ones"), hT[:, k, :], k == 0, k == KD - 1)
                last.then_inc(*norm_pe.step("sum"))

            def normed(n, which, k):
                pe.wait_ge(*shift_act.at(f"h{k}", 2 * n + which))

            def la(l, m, between):
                n = firsts[l]
                key, q, qe = (gk, gq, gqe) if m == "g" else (hk, hq, hqe)
                slot = AV if m == "g" else HI
                pe.wait_ge(*(gla_vec if m == "g" else hgrn_vec).at("ku", l))
                if m == "h":
                    pe.wait_ge(*la_vec.at("ong", l))
                nf = 1 if m == "g" else 2
                for tt in range(NT):
                    for f in range(nf):
                        a = (tt * nf + f) * P
                        last = pe.transpose(bank(5, a, a + P), key[:, 1, f * T + tt * P:f * T + tt * P + P],
                                            const("ident"))
                last.then_inc(*la_pe.step("tr" + m))
                for tt, b in ((0, 4), (1, 6)):
                    if tt == 1 and m == "g":
                        pe.wait_ge(*sgu_vec.at("mix", l))
                    if m == "g":
                        last = mm(bank(b).rearrange("p (h t) -> p h t", h=4), key[:, 0, tt * P:tt * P + P],
                                  q[:, :, tt * P:tt * P + P])
                    else:
                        for f in range(2):
                            last = mm(bank(b, f * T, f * T + T).rearrange("p (h t) -> p h t", h=2),
                                      key[:, 0, f * T + tt * P:f * T + tt * P + P], q[:, f, :, tt * P:tt * P + P])
                    last.then_inc(*la_pe.step(("sa", "sb")[tt] + m))
                pe.wait_ge(*la_act.at("ku" + m, l))
                if m == "g":
                    pe.wait_ge(*proj_act.at("p", proj_before[n] + 11))
                for tt in range(NT):
                    pe.wait_ge(*v_pool.at(f"v{m}{tt}", l))
                    if tt == 1:
                        pe.wait_ge(*la_vec.at("st8" + m, l))
                    for b in range(4):
                        if m == "g":
                            last = mm(bank(b), ku_tok[:, tt * P:tt * P + P], v_chunks[:, b * 512:b * 512 + 512])
                        else:
                            f, half = b // 2, b % 2
                            v = v_chunks.rearrange("p (c v) -> p c v", c=8)[:, 4 * half:4 * half + 4, f * P:f * P + P]
                            last = mm(bank(b).rearrange("p (c v) -> p c v", c=4),
                                      ku_tok[:, (tt * 2 + f) * P:(tt * 2 + f) * P + P], v)
                    last.then_inc(*la_pe.step(f"u{tt}" + m))
                    between()
                pe.wait_ge(*la_vec.at("st15" + m, l))
                st = state.rearrange("p (c v) -> p c v", c=NCH)
                for half in range(2):
                    for vt in range(2):
                        h = 2 * vt + half
                        for tt in range(NT):
                            a = vt * T + tt * P
                            mm(bank(5, a, a + P)[64 * half:64 * half + 64, :], proj[:, slot, tt, h * 64:h * 64 + 64],
                               scores[:, tt, h * P:h * P + P], vt == 0 and tt == 0, False)
                        for c in range(1, NCH):
                            a = vt * T + c * LA
                            rq = qe[:, h, c * LA:c * LA + LA] if m == "g" else qe[:, vt, half, c * LA:c * LA + LA]
                            last = mm(bank(5, a, a + LA)[64 * half:64 * half + 64, :], st[:, c, h * 64:h * 64 + 64],
                                      rq, False, c == NCH - 1)
                last.then_inc(*la_pe.step("o" + m))
                between()
                pe.wait_ge(*la_act.at("osq" + m, l))
                mm(bank(4), const("half_ones"), osq).then_inc(*la_pe.step("ms" + m))

            def first_mixers(l):
                n = firsts[l]
                for k in range(KD):
                    normed(n, 0, k)
                    last = mm(bank(4, 0, T)[0:16, :], param("w_glow", LAYER[plan[firsts[l]]], 2)[:, k * 16:k * 16 + 16], hT[:, k, :],
                              k == 0, k == KD - 1)
                last.then_inc(*glow_pe.step("glow"))
                project(n, [0], TOKEN_MAJOR)
                pe.wait_ge(*gla_act.at("glow", l))
                mm(bank(5, 0, T), param("gla_w_gate", LAYER[plan[firsts[l]]], 2)[0:16, :], glow[0:16, :]).then_inc(*glow_pe.step("z"))
                project(n, range(1, 12), TOKEN_MAJOR)
                pe.wait_ge(*sgu_vec.at("vn", l))
                pe.wait_ge(*sgu_pool.at("w", l))
                for half in range(2):
                    for vt in range(2):
                        h = 2 * vt + half
                        for tt in range(NT):
                            a = vt * T + tt * P
                            last = mm(bank(6, a, a + P)[64 * half:64 * half + 64, :], vn[:, tt, h * 64:h * 64 + 64],
                                      sgu_w[:, h, :])
                last.then_inc(*sgu_pe.step("mix"))
                count = 0 if n else 1
                modulate(count * 2)
                la(l, "g", lambda: modulate(count * 2))
                modulate(count * 2)
                la(l, "h", lambda: modulate(count * 2))
                pe.wait_ge(*conv_vec.at("y", l))
                pe.wait_ge(*sgu_vec.at("y", l))
                pe.wait_ge(*la_vec.at("yh", l))

            def even_mixers(n):
                for tt in range(NT):
                    for k in range(KD):
                        if tt == 0:
                            normed(n, 0, k)
                        last = mm(bank(4, tt * 8, tt * 8 + 8), hT[:, k, tt * P:tt * P + P],
                                  param("w_ab")[:, k * 8:k * 8 + 8], k == 0, k == KD - 1)
                last.then_inc(*gdn_pe.step("ab"))
                project(n, range(2))
                pe.wait_ge(*mod_rest.at("m", n))
                pe.wait_ge(*gdn_vec.at("spread", 0))
                for tt in range(NT):
                    last = mm(bank(5, tt * 4, tt * 4 + 4), const("upto"), gdec[:, tt * 4:tt * 4 + 4])
                last.then_inc(*gdn_pe.step("gc"))
                for m in range(8):
                    last = mm(pair[:, m * P:m * P + P], spread[:, 0, m, :], const("upto"))
                last.then_inc(*gdn_pe.step("grows"))
                project(n, range(2, 10))
                pe.wait_ge(*proj_act.at("p", proj_before[n] + 9))
                pe.wait_ge(*gdn_act.at("sq", 0))
                for b in range(4):
                    last = mm(bank(b), const("ones"), l2[:, b * 512:b * 512 + 512])
                last.then_inc(*gdn_pe.step("l2"))
                pe.wait_ge(*gdn_vec.at("gcc", 0))
                for m in range(8):
                    a = m % 4 * P
                    last = mm(bank(4 + m // 4, a, a + P), spread[:, 1, m, :], const("ident"))
                last.then_inc(*gdn_pe.step("brows"))
                for tt in range(NT):
                    pe.wait_ge(*gdn_vec.at(f"kb{tt}", 0))
                    for h in range(HEADS):
                        kt, a = qkv[:, 4 + h, tt * P:tt * P + P], h * P
                        mm(bank(tt, a, a + P), kt, kb[:, tt, a:a + P])
                        last = mm(bank(2 + tt, a, a + P), kt, qkv[:, h, tt * P:tt * P + P])
                    last.then_inc(*gdn_pe.step(f"kk{tt}"))
                pe.wait_ge(*gdn_act.at("silu_v", 0))
                pe.wait_ge(*gdn_act.at("dec", 0))
                for m in range(8):
                    tt, h, a = m // 4, m % 4, m % 4 * P
                    pe.transpose(bank(4 + tt, a, a + P), qkv[:, 4 + h, tt * P:tt * P + P], const("ident"))
                    last = pe.transpose(pair[:, m * P:m * P + P], qkv[:, 8 + h, tt * P:tt * P + P], const("ident"))
                last.then_inc(*gdn_pe.step("tr"))
                pe.wait_ge(*gdn_pool.at("ident", 0))
                pe.wait_ge(*gdn_act.at("vb", 0))
                for l in range(LEVELS):
                    for t in range(NT):
                        pe.wait_ge(*gdn_vec.at(f"m{l}{t}", 0))
                        for h in range(HEADS):
                            a = h * P
                            last = mm(bank(t, a, a + P), MT[:, t, a:a + P], X[:, t, a:a + P])
                        last.then_inc(*gdn_pe.step(f"y{l}{t}"))
                    for t in range(NT):
                        pe.wait_ge(*gdn_act.at(f"y{l}{t}", 0))
                        for h in range(HEADS):
                            a = h * P
                            mm(bank(2 + t, a, a + P), XT[:, t, a:a + P], Y[:, t, a:a + P])
                            last = mm(bank(4 + t, a, a + P), Y[:, t, a:a + P], XT[:, t, a:a + P])
                        last.then_inc(*gdn_pe.step(f"z{l}{t}"))
                for t in range(NT):
                    pe.wait_ge(*gdn_vec.at(f"x6{t}", 0))
                for h in range(HEADS):
                    a = h * P
                    last = mm(bank(0, a, a + P), XT[:, 0, a:a + P], vb[:, a:a + P])
                last.then_inc(*gdn_pe.step("v0"))
                for h in range(HEADS):
                    a = h * P
                    last = mm(bank(1, a, a + P), kbe[:, a:a + P], XT[:, 1, a:a + P])
                last.then_inc(*gdn_pe.step("w"))
                pe.wait_ge(*gdn_act.at("vn0", 0))
                for h in range(HEADS):
                    a = h * P
                    last = mm(bank(2, a, a + P), kdec[:, a:a + P], vnew[:, 0, a:a + P])
                last.then_inc(*gdn_pe.step("s1"))
                pe.wait_ge(*gdn_act.at("S1", 0))
                for h in range(HEADS):
                    a = h * P
                    mm(bank(3, a, a + P), XT[:, 1, a:a + P], vb[:, 512 + a:512 + a + P], True, False)
                    last = mm(bank(3, a, a + P), wTn[:, a:a + P], S1[:, a:a + P], False, True)
                last.then_inc(*gdn_pe.step("v1"))
                pe.wait_ge(*gdn_act.at("vn1", 0))
                for h in range(HEADS):
                    a, o = h * P, h * T
                    mm(pair[:, o:o + P], vnew[:, 0, a:a + P], PT[:, 0, a:a + P])
                    mm(pair[:, o + P:o + T], vnew[:, 1, a:a + P], PT[:, 1, a:a + P], True, False)
                    last = mm(pair[:, o + P:o + T], S1[:, a:a + P], qg[:, a:a + P], False, True)
                last.then_inc(*gdn_pe.step("o"))
                pe.wait_ge(*gdn_act.at("osq", 0))
                mm(bank(4), const("ones"), gosq[:, 0:512])
                mm(bank(5), const("ones"), gosq[:, 512:1024]).then_inc(*gdn_pe.step("ms"))
                pe.wait_ge(*gdn_pool.at("less", 0))
                for g in range(4):
                    last = mm(bank(2 + g // 2, g % 2 * T, g % 2 * T + T), param("pool_w_2")[:, g * P:g * P + P],
                              poolb[g % 2][:, g, :])
                last.then_inc(*gdn_pe.step("pool"))
                pe.wait_ge(*gdn_vec.at("y", 0))
                pe.wait_ge(*gdn_act.at("pool", 0))

            def odd_mixers(n):
                first = place[f"in{n}"]

                def mean_square(q):
                    pe.wait_ge(*att_act["sq"].at("sq", q))
                    if q:
                        pe.wait_ge(*att_act["root"].at("root", q - 1))
                    mm(bank(2), const("ones"), qsq[:, q % 2, :]).then_inc(*att_pe["ms"].step("ms"))

                def scores_of(u):
                    hp, h, qt = u // 4, u // 2 % 2, u % 2
                    w = (qt + 1) * P
                    if u == 0:
                        pe.wait_ge(*mod_rest.at("m", n))
                    if u % 4 == 0:
                        pe.wait_ge(*att_vec["qk"].at("qk", 6 * hp + 5))
                    if u:
                        pe.wait_ge(*att_vec["logit"].at("logit", u - 1))
                    for g in range(ATT_GROUPS):
                        last = mm(pair[:, g * w:g * w + w], qk[:, hp % 2, 0, g, h, qt * P:qt * P + P],
                                  qk[:, hp % 2, 1, g, h, 0:w])
                    last.then_inc(*att_pe["scores"].step("scores"))

                def turn(u):
                    pe.wait_ge(*att_vec["prob"].at("prob", u))
                    if u:
                        pe.wait_ge(*att_act["turned"].at("turned", u - 1))
                    for b in range(ATT_GROUPS * (u % 2 + 1)):
                        last = pe.transpose(bank(4 + b // 4, b % 4 * P, b % 4 * P + P), prob[:, u % 2, b * P:b * P + P],
                                            const("ident"))
                    last.then_inc(*att_pe["turned"].step("turned"))

                def values_of(u):
                    hp, h, qt = u // 4, u // 2 % 2, u % 2
                    pe.wait_ge(*att_act["turned"].at("turned", u))
                    if u % 4 == 0:
                        pe.wait_ge(*att_act["v"].at("v", 3 * hp + 2))
                    if u:
                        pe.wait_ge(*att_act["out"].at("out", u - 1))
                    blocks = ATT_GROUPS * (qt + 1)
                    for b in range(blocks):
                        g, kt = b // (qt + 1), b % (qt + 1)
                        last = mm(bank(3, 0, P), vtok[:, hp % 2, g, kt, h * P:h * P + P], probT[:, u % 2, b, :],
                                  b == 0, b == blocks - 1)
                    last.then_inc(*att_pe["out"].step("out"))

                for hp in range(5):
                    for s in range(9):
                        if hp < 4:
                            at = hp * 9 + s
                            if at >= 2:
                                hb, sb_ = divmod(at - 2, 9)
                                if sb_ % 3 == 2:
                                    pe.wait_ge(*att_act["v"].at("v", hb * 3 + sb_ // 3))
                                else:
                                    pe.wait_ge(*att_act["sq"].at("sq", hb * 6 + sb_ // 3 * 2 + sb_ % 3))
                            product(first + at, bank(at % 2), hT, s % 3 == 2,
                                    (lambda k: normed(n, 0, k)) if at == 0 else None)
                        if hp >= 1:
                            u = 4 * (hp - 1)
                            if s % 2 == 0 and s >= 2:
                                values_of(u + s // 2 - 1)
                            if s < 8:
                                (scores_of if s % 2 == 0 else turn)(u + s // 2)
                        if hp < 4 and s % 3 < 2:
                            mean_square(hp * 6 + s // 3 * 2 + s % 3)
                for u in (14, 15):
                    pe.wait_ge(*att_act["out"].at("out", u))

            def out_product(n):
                for s in range(4):
                    product(place[f"out{n}"] + s, bank(s), yT)

            def router(n):
                for tt in range(NT):
                    for k in range(KD):
                        if tt == 0:
                            normed(n, 1, k)
                        last = mm(bank(4, tt * 8, tt * 8 + 8), hT[:, k, tt * P:tt * P + P],
                                  param("moe_router")[:, k * 8:k * 8 + 8], k == 0, k == KD - 1)
                last.then_inc(*moe_pe.step("logits"))
                for tt in range(NT):
                    for k in range(KD):
                        a = k % 4 * P
                        last = pe.transpose(bank(2 * tt + k // 4, a, a + P), hT[:, k, tt * P:tt * P + P],
                                            const("ident"))
                last.then_inc(*moe_pe.step("turned"))
                pe.wait_ge(*moe_vec.at("sel", 0))
                mm(bank(5, 0, 8), const("before"), rank[:, 0, :])
                mm(bank(5, P, 2 * P), const("ones"), const("before"))
                mm(bank(5, 24, 25), const("before"), const("ones")[:, 0:1])
                for a, first in ((8, "before"), (16, "ones")):
                    mm(bank(5, a, a + 8), const("ones"), rank[:, 0, :], True, False)
                    last = mm(bank(5, a, a + 8), const(first), rank[:, 1, :], False, True)
                last.then_inc(*moe_pe.step("spots"))
                pe.wait_ge(*moe_vec.at("spread", 0))
                pe.wait_ge(*moe_act.at("turned", 0))
                for e in range(EXPERTS):
                    for tt in range(NT):
                        a = e % 2 * T + tt * P
                        mm(bank(e // 2, a, a + P), comb_b[:, e, tt, :], const("ident"))
                        last = mm(bank(4 + e // 2, a, a + P), spot_b[:, e, tt, :], const("ident"))
                last.then_inc(*moe_pe.step("rows"))

            def experts(r):
                m, base = passes[r], (moe_first, 0)[r]

                def slot_here(s, e, i):
                    pe.wait_ge(m["here"][(moe_first + s) % RING],
                               e * (16 * EXPERT_ROUNDS) + i * 16 + 16 * ((base + s) // RING + 1))
                    return ring[:, (moe_first + s) % RING, :]

                def gather(e):
                    pe.wait_ge(m["picks"], e + 1)
                    if isinstance(e, int) and e == 0:
                        if r:
                            pe.wait_ge(passes[0]["added"], 2 * EXPERTS)
                        else:
                            pe.wait_ge(*moe_act.at("rows", 0))
                    elif not (isinstance(e, int) and e == 1):
                        pe.wait_ge(m["added"], 2 * e - 2)
                    for k in range(KD):
                        for tt in range(NT):
                            last = mm(pair[:, k * P:k * P + P], h_tok[:, tt, k * P:k * P + P], pick[:, tt, :],
                                      tt == 0, tt == 1)
                    last.then_inc(m["gathered"], 1)

                def up(half, s, e, i, u):
                    w = slot_here(s + half, e, i).rearrange("p (k n) -> p k n", k=4)
                    for k in range(4):
                        last = mm(bank(2 + u), gathered_h[:, 4 * half + k, :], w[:, k, :], half == 0 and k == 0,
                                  half == 1 and k == 3)
                    last.then_inc(m["used"], 1)

                def scatter(e, half):
                    if half == 0:
                        pe.wait_ge(m["outs"], e + 1)
                        pe.wait_ge(m["backs"], e + 1)
                        if not is_first(e):
                            pe.wait_ge(m["added"], 2 * e)
                    else:
                        pe.wait_ge(m["added"], 2 * e + 1)
                    for q in range(4):
                        d = 4 * half + q
                        last = mm(pair[:, q * T:q * T + T], expert_out[:, d * P:d * P + P], put_back)
                    last.then_inc(m["scattered"], 1)

                def visit(e):
                    def step(i, u, c):
                        g = e * EXPERT_CHUNKS + i * 2 + u
                        if c == EXPERT_CHUNKS - 2 and not is_last(e):
                            gather(e + 1)
                        if not is_last(e, c):
                            if c == EXPERT_CHUNKS - 1:
                                pe.wait_ge(m["tokens"], e + 2)
                            if not (is_first(e, c) and c == 0):
                                pe.wait_ge(m["hid"], g)
                            up(0, 3 * u + 2, e, i, 1 - u)
                        pe.wait_ge(m["hid"], g + 1)
                        if not is_first(e, c):
                            pe.wait_ge(m["hid_t"], g - 1)
                        for j in range(2):
                            last = pe.transpose(bank(4 + u, j * P, j * P + P), ff_mid[:, u, j * P:j * P + P],
                                                const("ident"))
                        last.then_inc(m["turned"], 1)
                        if not is_last(e, c):
                            up(1, 3 * u + 2, e, i, 1 - u)
                        w = slot_here(3 * u + (2 if is_last(e, c) else 4), e, i).rearrange("p (j n) -> p j n", j=2)
                        pe.wait_ge(m["hid_t"], g + 1)
                        if c == 0 and not is_first(e):
                            pe.wait_ge(m["outs"], e)
                        for j in range(2):
                            for b in range(2):
                                last = mm(bank(b), ff_hid[:, u, j * P:j * P + P], w[:, j, b * 512:b * 512 + 512],
                                          c == 0 and j == 0, c == EXPERT_CHUNKS - 1 and j == 1)
                        last.then_inc(m["used"], 1)
                        if c in (0, 1) and not is_first(e):
                            scatter(e - 1, c)
                    expert_chunks(pe, step)

                gather(0)
                pe.wait_ge(m["tokens"], 1)
                up(0, 0, 0, 0, 0)
                up(1, 0, 0, 0, 0)
                each_expert(pe, visit)
                scatter(EXPERTS - 1, 0)
                scatter(EXPERTS - 1, 1)

            def feed_forward(n, kind):
                chunks, first, base = chunks_of(kind), place[f"ffn{n}"], tiles_before[n]

                splits = dense_before[n] * SPLITS

                def split_here(q, i):
                    pe.wait_ge(split_low, splits + q + 1 if i is None else i * RING + (splits + q + 1))
                    return w_high[q % 3], ring_r[:, (first + 2 + q) % RING, :]

                def mm3(o, w, x, start, stop):
                    mm(o, w[0], x[0], start, False)
                    mm(o, w[0], x[1], False, False)
                    return mm(o, w[1], x[0], False, stop)

                def up(c, i=None):
                    at = ff_slot(first, c)
                    if c == 1:
                        pe.wait_ge(*low_pool.at("h", dense_before[n]))
                    for w in range(2):
                        if c == 0:
                            arrive(at + w)
                        else:
                            parts = [p.rearrange("p (k n) -> p k n", k=KD) for p in split_here(3 * (c - 1) + w, i)]
                        for j in range(2):
                            b = 4 + 2 * (c % 2) + j
                            if c >= 2 and w == 0:
                                t = base + 2 * c + j - 3
                                pe.wait_ge(ffn_hid, t if i is None else i * 4 + t)
                            o = bank(b, w * T, w * T + T)
                            for k in range(KD):
                                if c == 0:
                                    if j == 0 and w == 0:
                                        normed(n, 1, k)
                                    last = mm(o, slot_k(at + w)[:, k, j * P:j * P + P], hT[:, k, :], k == 0,
                                              k == KD - 1)
                                else:
                                    last = mm3(o, [p[:, k, j * P:j * P + P] for p in parts],
                                               (h_high[:, k, :], h_low[:, k, :]), k == 0, k == KD - 1)
                            if w == 1 and j == 0:
                                last.then_inc(ffn_half, 1)
                        last.then_inc(weights_used, 1)

                def down(c, i=None, final=False):
                    parts = [p.rearrange("p (j n) -> p j n", j=2) for p in split_here(3 * c + (0 if final else 2), i)]
                    t = base + 2 * c + 2
                    pe.wait_ge(ffn_hid, t if i is None else i * 4 + t)
                    for j in range(2):
                        b = 2 * (c % 2) + j
                        for d in range(KD):
                            last = mm3(bank(d // 2, d % 2 * T, d % 2 * T + T), [p[:, j, d * P:d * P + P] for p in parts],
                                       (hid_high[:, b, :], ff_hid_r[:, b, :]),
                                       i is None and c == 0 and j == 0 and d % 2 == 0, final and j == 1)
                            if final and j == 1 and d in (1, 3, 5):
                                last.then_inc(ffn_out, 1)
                    last.then_inc(weights_used, 1)

                up(0)
                for c in range(2):
                    up(c + 1)
                    down(c)
                with pe.Fori(0, (chunks - 1) // 2 - 1) as i:
                    for c in (2, 3):
                        up(c + 1, i)
                        down(c, i)
                for c in range(2 * ((chunks - 1) // 2), chunks - 1):
                    up(c + 1)
                    down(c)
                down(chunks - 1, final=True)

            pe.wait_ge(consts_here, 16)
            pe.wait_ge(params_here, 16)
            pe.wait_ge(mod_part, MOD_LEAD * KD)
            sum_modulation(5, lead_acc, 0, MOD_LEAD).then_inc(*mod_lead_pe.step("s"))
            for n, kind in enumerate(plan):
                if n:
                    pe.wait_ge(mod_part, slots_before(n + 1) * KD)
                    if plan[n - 1] == "first1":
                        pe.wait_ge(*x_ready(norms.index((n - 1, 2))))
                    sum_modulation(5, mod_acc, 0, MOD_LEAD).then_inc(*mod_lead_pe.step("s"))
                norm(n, 0)
                if n:
                    sum_modulation(7, mod_acc, MOD_LEAD, MOD_SLOTS).then_inc(*mod_rest_pe.step("s"))
                if kind.startswith("first"):
                    first_mixers(firsts.index(n))
                elif kind == "even":
                    even_mixers(n)
                else:
                    odd_mixers(n)
                out_product(n)
                norm(n, 1)
                if kind == "first1":
                    router(n)
                    experts(0)
                    with pe.If(more_tokens(pe)):
                        experts(1)
                    norm(n, 2)
                else:
                    feed_forward(n, kind)

        @block.vector
        def _(dve):
            def tt(o, a, b, op):
                return dve.tensor_tensor(o, a, b, op)

            def ts(o, a, s1, s2, op0, op1):
                return dve.tensor_scalar(o, a, s1, s2, op0, op1)

            def stt(o, a, s, b, op0, op1):
                return dve.scalar_tensor_tensor(o, a, s, b, op0, op1)

            def accumulate(m, slots, accs, ks, parts):
                for k in ks:
                    for s, (w, acc) in enumerate(zip(slots, accs)):
                        if k == 0:
                            last = ts(acc, w[:, 0, :], cond_of(m)[:, 0:1], None, ALU.mult, ALU.bypass)
                        else:
                            dve.wait_ge(mod_part, parts + ((k - 1) * len(slots) + s + 1))
                            last = stt(acc, w[:, k, :], cond_of(m)[:, k:k + 1], acc, ALU.mult, ALU.add)
                        last.then_inc(mod_part, 1)

            def mod_parts(m, group, ks):
                if ks[0] == 0:
                    dve.wait_ge(mod_here, group * (16 * MOD_GROUP) + 16 * (slots_before(m) - MOD_LEAD + MOD_GROUP))
                accumulate(m, [mod_ring[:, s, :, :] for s in range(MOD_GROUP)],
                           [mod_acc[:, bass.ds(group * MOD_GROUP + s, 1), :].rearrange("p a n -> p (a n)")
                            for s in range(MOD_GROUP)],
                           ks, group * (MOD_GROUP * KD) + slots_before(m) * KD)

            def modulation_lead(m):
                a = m * MODS
                dve.wait_ge(*mod_lead_pe.at("s", m))
                tt(mod[:, a:a + 2 * KD], bank(5, 0, 2 * KD), param("b_mod")[:, a:a + 2 * KD], ALU.add)\
                    .then_inc(*mod_lead.step("m"))

            def modulation_rest(m):
                a, b = m * MODS + 2 * KD, (m + 1) * MODS
                if m:
                    dve.wait_ge(*mod_rest_pe.at("s", m - 1))
                else:
                    dve.wait_ge(weights_used, place["mod_rest"] + MOD_SLOTS - MOD_LEAD)
                tt(mod[:, a:b], bank(7, 0, b - a), param("b_mod")[:, a:b], ALU.add).then_inc(*mod_rest.step("m"))

            def norm(n, which):
                u = norms.index((n, which))
                if which < 2:
                    dve.wait_ge(*(mod_rest if which else mod_lead).at("m", n))
                    if u:
                        dve.wait_ge(*norm_vec.at("s7", u - 1))
                    last = stt(gain[:, :], mod_columns(n, 3 * which + 1), 1.0, norm_gain(n, which), ALU.add, ALU.mult)
                else:
                    dve.wait_ge(*norm_vec.at("s7", u - 1))
                    last = dve.tensor_copy(gain[:, :], norm_gain(n, which))
                last.then_inc(*norm_vec.step("gain"))
                dve.wait_ge(*norm_act.at("root", u))
                dve.reciprocal(rstd[:, :], rstd[:, :]).then_inc(*norm_vec.step("rstd"))
                dve.wait_ge(*norm_vec.at("rstd", u))
                for k in range(KD):
                    o = xT if which == 2 else yT
                    stt(o[:, k, :], xT[:, k, :], gain[:, k:k + 1], rstd[:, :], ALU.mult, ALU.mult)\
                        .then_inc(*norm_vec.step(f"s{k}"))

            def lower_bounds():
                raw = param("hgrn_lower_bounds").rearrange("p (l f) -> p l f", l=2)
                tt(lbw[:, 0, :], raw[:, 0, :], raw[:, 1, :], ALU.max).then_inc(*lb_vec.step("max"))
                dve.wait_ge(*lb_vec.at("max", 0))
                tt(lbw[:, 1, :], raw[:, 0, :], lbw[:, 0, :], ALU.subtract)
                tt(lbw[:, 2, :], raw[:, 1, :], lbw[:, 0, :], ALU.subtract).then_inc(*lb_vec.step("d"))
                dve.wait_ge(*lb_act.at("exp", 0))
                tt(lbw[:, 3, :], lbw[:, 1, :], lbw[:, 2, :], ALU.add).then_inc(*lb_vec.step("sum"))
                dve.wait_ge(*lb_vec.at("sum", 0))
                dve.reciprocal(lbw[:, 4, :], lbw[:, 3, :]).then_inc(*lb_vec.step("inv"))
                dve.wait_ge(*lb_vec.at("inv", 0))
                dve.memset(lbs[:, 0, 0, :], 0.0)
                dve.memset(lbs[:, 0, 1, :], 1.0)
                tt(lbs[:, 1, 0, :], lbw[:, 2, :], lbw[:, 4, :], ALU.mult).then_inc(*lb_vec.step("lb"))
                dve.wait_ge(*lb_vec.at("lb", 0))
                ts(lbs[:, 1, 1, :], lbs[:, 1, 0, :], -1.0, 1.0, ALU.mult, ALU.add).then_inc(*lb_vec.step("om"))
                dve.wait_ge(*lb_vec.at("om", 0))

            def running(vec, l, run, log, dist, w):
                dve.tensor_tensor_scan(run, const("restart")[:, 0:w], log, 0.0, ALU.mult, ALU.add)\
                   .then_inc(*vec.step("run"))
                dve.wait_ge(*vec.at("run", l))
                c = run.rearrange("p (c i) -> p c i", i=LA)
                d = [dist[:, a, :].rearrange("p (c i) -> p c i", i=LA) for a in range(2)]
                shape = [P, w // LA, LA]
                tt(d[0], c, c[:, :, LA // 2:LA // 2 + 1].to_broadcast(shape), ALU.subtract)
                tt(d[1], c[:, :, LA - 1:LA].to_broadcast(shape), c, ALU.subtract).then_inc(*vec.step("dist"))

            def la(l, m):
                n = firsts[l]
                mask = const("same_chunk").unsqueeze(1).to_broadcast([P, HEADS, P])
                for t, b in ((0, 4), (1, 6)):
                    s = ("sa", "sb")[t] + m
                    dve.wait_ge(*la_pe.at(s, l))
                    tt(scores[:, t, :].rearrange("p (h t) -> p h t", h=4), bank(b).rearrange("p (h t) -> p h t", h=4),
                       mask, ALU.mult).then_inc(*la_vec.step(s))
                st = state.rearrange("p (c v) -> p c v", c=NCH)
                for c in range(1, NCH):
                    t, cc = divmod(c - 1, 8)
                    if cc == 0:
                        dve.wait_ge(*la_pe.at(f"u{t}" + m, l))
                    if c > 1:
                        dve.wait_ge(*la_vec.at(f"st{c - 1}" + m, l))
                    for f in range(1 if m == "g" else 2):
                        if m == "g":
                            part, cols = bank(cc // 2, cc % 2 * T, cc % 2 * T + T), slice(0, T)
                            decay = gdecay[:, c - 1:c]
                        else:
                            part = bank(f * 2 + cc // 4, cc % 4 * P, cc % 4 * P + P)
                            cols, decay = slice(f * P, f * P + P), hdecay[:, f * NCH + c - 1:f * NCH + c]
                        if c == 1:
                            last = dve.tensor_copy(st[:, c, cols], part)
                        else:
                            last = stt(st[:, c, cols], st[:, c - 1, cols], decay, part, ALU.mult, ALU.add)
                    last.then_inc(*la_vec.step(f"st{c}" + m))
                dve.wait_ge(*la_act.at("root" + m, l))
                dve.reciprocal(orn, orn).then_inc(*la_vec.step("rn" + m))
                dve.wait_ge(*la_vec.at("rn" + m, l))
                tt(osq, bank(5), orn, ALU.mult).then_inc(*la_vec.step("on" + m))
                dve.wait_ge(*la_vec.at("on" + m, l))
                dve.wait_ge(*(gla_act if m == "g" else hgrn_act).at("gate", l))
                a = 4 if m == "g" else 6
                stt(yT[:, a:a + 2, :].rearrange("p a t -> p (a t)"), osq,
                    param("gla_norm_g" if m == "g" else "hgrn_norm_g", LAYER[plan[firsts[l]]], 2), gates[:, 0 if m == "g" else 1, :],
                    ALU.mult, ALU.mult).then_inc(*la_vec.step("y" + m))

            def first_mixers(l):
                n = firsts[l]

                def here(s):
                    dve.wait_ge(*proj_act.at("p", proj_before[n] + s))
                dve.wait_ge(*glow_pe.at("z", l))
                ts(gz, bank(5, 0, T), param("gla_b_gate", LAYER[plan[firsts[l]]], 2), None, ALU.add, ALU.bypass).then_inc(*gla_vec.step("z"))
                dve.wait_ge(*gla_vec.at("z", l))
                stt(gt, gz, -1.0, gz, ALU.mult, ALU.max).then_inc(*gla_vec.step("abs"))
                dve.wait_ge(*hgrn_act.at("e", l))
                ts(hz, hz, 1.0, None, ALU.add, ALU.bypass).then_inc(*hgrn_vec.step("add"))
                dve.wait_ge(*hgrn_vec.at("add", l))
                dve.reciprocal(hz, hz).then_inc(*hgrn_vec.step("sig"))
                dve.wait_ge(*hgrn_vec.at("sig", l))
                for f in range(2):
                    last = ts(hf[:, f * T:f * T + T], hz[:, f * T:f * T + T], lbs[:, LAYER[plan[firsts[l]]], 1, f:f + 1],
                              lbs[:, LAYER[plan[firsts[l]]], 0, f:f + 1], ALU.mult, ALU.add)
                last.then_inc(*hgrn_vec.step("f"))
                dve.wait_ge(*hgrn_vec.at("f", l))
                ts(hkey, hf, -1.0, 1.0, ALU.mult, ALU.add).then_inc(*hgrn_vec.step("key"))
                dve.wait_ge(*gla_act.at("ln", l))
                stt(gz, gz, 0.0, gt, ALU.min, ALU.subtract).then_inc(*gla_vec.step("min"))
                dve.wait_ge(*gla_vec.at("min", l))
                running(gla_vec, l, gb, gz, gd, T)
                dve.wait_ge(*hgrn_act.at("lnf", l))
                running(hgrn_vec, l, hb, hz, hd, 2 * T)
                dve.wait_ge(*zero_pool.at("zero", l))
                here(AQK)
                dve.wait_ge(*gla_act.at("exps", l))
                for h in range(4):
                    r = slice(32 * h, 32 * h + 32)
                    for buf, e in ((gq, 0), (gqe, 3)):
                        stt(buf[r, h, :], proj[r, AQK, 0, :], float(32 ** -0.5), ge[r, e, :], ALU.mult, ALU.mult)
                tt(gk[:, 0, :], proj[:, AQK, 1, :], ge[:, 1, :], ALU.mult)
                tt(gk[:, 1, :], proj[:, AQK, 1, :], ge[:, 2, :], ALU.mult).then_inc(*gla_vec.step("ku"))
                dve.wait_ge(*hgrn_act.at("exps", l))
                for f in range(2):
                    for h in range(2):
                        r = slice(64 * h, 64 * h + 64)
                        for buf, e in ((hq, 0), (hqe, 3)):
                            tt(buf[r, f, h, :], proj[r, HQ, f, :], he[r, e, f * T:f * T + T], ALU.mult)
                tt(hk[:, 0, :], hkey, he[:, 1, :], ALU.mult)
                tt(hk[:, 1, :], hkey, he[:, 2, :], ALU.mult).then_inc(*hgrn_vec.step("ku"))
                here(SV)
                dve.tensor_reduce(sgu_s[:, 0:2], proj[:, SV, :, :], AX, ALU.add).then_inc(*sgu_vec.step("sum"))
                dve.wait_ge(*sgu_vec.at("sum", l))
                ts(sgu_s[:, 0:2], sgu_s[:, 0:2], 1.0 / T, None, ALU.mult, ALU.bypass).then_inc(*sgu_vec.step("mu"))
                dve.wait_ge(*sgu_vec.at("mu", l))
                for t in range(NT):
                    last = ts(vn[:, t, :], proj[:, SV, t, :], sgu_s[:, t:t + 1], None, ALU.subtract, ALU.bypass)
                last.then_inc(*sgu_vec.step("d"))
                dve.wait_ge(*sgu_act.at("root", l))
                dve.reciprocal(sgu_s[:, 6:8], sgu_s[:, 4:6]).then_inc(*sgu_vec.step("rs"))
                dve.wait_ge(*sgu_vec.at("rs", l))
                for t in range(NT):
                    last = stt(vn[:, t, :], vn[:, t, :], sgu_s[:, 6 + t:7 + t], param("sgu_norm_g", LAYER[plan[firsts[l]]], 2),
                               ALU.mult, ALU.mult)
                last.then_inc(*sgu_vec.step("vn"))
                here(CB)
                tt(cv, proj[:, CC, :, :], proj[:, CX, :, :], ALU.mult).then_inc(*conv_vec.step("cv"))
                dve.wait_ge(*conv_vec.at("cv", l))
                w = param("conv_w", LAYER[plan[firsts[l]]], 2).rearrange("p (f k) -> p f k", f=2)
                for f in range(2):
                    last = ts(cacc[:, f, :], cv[:, f, :], w[:, f, 2:3], None, ALU.mult, ALU.bypass)
                last.then_inc(*conv_vec.step("c0"))
                for back in (1, 2):
                    dve.wait_ge(*conv_vec.at(f"c{back - 1}", l))
                    for f in range(2):
                        last = stt(cacc[:, f, back:T], cv[:, f, 0:T - back], w[:, f, 2 - back:3 - back],
                                   cacc[:, f, back:T], ALU.mult, ALU.add)
                    last.then_inc(*conv_vec.step(f"c{back}"))
                dve.wait_ge(*conv_vec.at("c2", l))
                tt(yT[:, 0:2, :], cacc, proj[:, CB, :, :], ALU.mult).then_inc(*conv_vec.step("y"))
                dve.wait_ge(*sgu_pe.at("mix", l))
                bias = param("sgu_b", LAYER[plan[firsts[l]]], 2).rearrange("p (v t) -> p v t", v=2).unsqueeze(2).to_broadcast([P, 2, 2, P])
                tt(cv.rearrange("p v (t i) -> p v t i", t=2), bank(6).rearrange("p (v t i) -> p v t i", v=2, t=2),
                   bias, ALU.add).then_inc(*sgu_vec.step("mix"))
                dve.wait_ge(*sgu_vec.at("mix", l))
                tt(yT[:, 2:4, :], cv, proj[:, SU, :, :], ALU.mult).then_inc(*sgu_vec.step("y"))
                la(l, "g")
                la(l, "h")

            def router(n):
                dve.wait_ge(*moe_pe.at("logits", 0))
                dve.tensor_copy(logits, bank(4, 0, 16).rearrange("p (t e) -> p t e", t=NT))\
                   .then_inc(*moe_vec.step("copy"))
                dve.wait_ge(*moe_vec.at("copy", 0))
                dve.tensor_reduce(top, logits, AX, ALU.max).then_inc(*moe_vec.step("max"))
                dve.wait_ge(*moe_vec.at("max", 0))
                ts(top, top, -1.0, None, ALU.mult, ALU.bypass).then_inc(*moe_vec.step("neg"))
                lower = const("lower_expert").rearrange("p (a b) -> p a b", a=8)
                for t in range(NT):
                    mine = logits[:, t, :].unsqueeze(2).to_broadcast([P, 8, 8])
                    other = logits[:, t, :].unsqueeze(1).to_broadcast([P, 8, 8])
                    tt(rk_gt, other, mine, ALU.is_gt).then_inc(*moe_vec.step(f"gt{t}"))
                    tt(rk_eq, other, mine, ALU.is_equal).then_inc(*moe_vec.step(f"eq{t}"))
                    dve.wait_ge(*moe_vec.at(f"eq{t}", 0))
                    tt(rk_eq, rk_eq, lower, ALU.mult).then_inc(*moe_vec.step(f"low{t}"))
                    dve.wait_ge(*moe_vec.at(f"low{t}", 0))
                    tt(rk_gt, rk_gt, rk_eq, ALU.add).then_inc(*moe_vec.step(f"sum{t}"))
                    dve.wait_ge(*moe_vec.at(f"sum{t}", 0))
                    dve.tensor_reduce(rank[:, t, :], rk_gt, AX, ALU.add).then_inc(*moe_vec.step(f"rk{t}"))
                    dve.wait_ge(*moe_vec.at(f"rk{t}", 0))
                ts(rank, rank, 2.0, None, ALU.is_lt, ALU.bypass).then_inc(*moe_vec.step("sel"))
                dve.wait_ge(*moe_vec.at("sel", 0))
                dve.wait_ge(*moe_act.at("exp", 0))
                tt(comb, comb, rank, ALU.mult).then_inc(*moe_vec.step("pick"))
                dve.wait_ge(*moe_vec.at("pick", 0))
                dve.tensor_reduce(den, comb, AX, ALU.add).then_inc(*moe_vec.step("den"))
                dve.wait_ge(*moe_vec.at("den", 0))
                dve.reciprocal(den, den).then_inc(*moe_vec.step("inv"))
                dve.wait_ge(*moe_vec.at("inv", 0))
                tt(comb, comb, den.unsqueeze(2).to_broadcast([P, NT, 8]), ALU.mult).then_inc(*moe_vec.step("w"))
                dve.wait_ge(*moe_vec.at("w", 0))
                dve.wait_ge(*moe_pe.at("spots", 0))
                dve.tensor_copy(column, bank(5, P, 2 * P))
                dve.tensor_copy(partition, bank(5, 24, 25))
                stt(spot, bank(5, 0, 16).rearrange("p (t e) -> p t e", t=NT), 1.0, rank, ALU.add, ALU.mult)\
                    .then_inc(*moe_vec.step("spots"))
                dve.wait_ge(*moe_vec.at("spots", 0))
                ts(spot, spot, -1.0, None, ALU.add, ALU.bypass).then_inc(*moe_vec.step("spot"))
                dve.tensor_reduce(most, bank(5, 16, 24), AX, ALU.max).then_inc(*moe_vec.step("most"))
                dve.wait_ge(*moe_vec.at("most", 0))
                ts(flag[:, :], most, float(P), None, ALU.is_gt, ALU.bypass).then_inc(*moe_vec.step("flag"))
                dve.tensor_copy(spot_b, spot.rearrange("p t e -> p e t").unsqueeze(3).to_broadcast([P, 8, NT, P]))
                dve.tensor_copy(comb_b, comb.rearrange("p t e -> p e t").unsqueeze(3).to_broadcast([P, 8, NT, P]))\
                   .then_inc(*moe_vec.step("spread"))

            def experts(r):
                m, next_layer = passes[r], plan.index("first1") + 1
                gate = mod_columns(plan.index("first1"), 5)

                def one_hot(e):
                    if not (isinstance(e, int) and e == 0):
                        dve.wait_ge(m["gathered"], e)
                    for t in range(NT):
                        last = ts(pick[:, t, :], column, spot[:, t, bass.ds(e, 1)], None,
                                  ALU.is_equal, ALU.bypass)
                    last.then_inc(m["picks"], 1)

                def hidden(g, u, free):
                    dve.wait_ge(m["silu"], g + 1)
                    if not free:
                        dve.wait_ge(m["turned"], g - 1)
                    tt(ff_mid[:, u, :], bank(2 + u, T, 2 * T), ff_silu[:, u, :], ALU.mult).then_inc(m["hid"], 1)

                def add(e, half):
                    dve.wait_ge(m["scattered"], 2 * e + (1 + half))
                    for q in range(4):
                        d = 4 * half + q
                        last = stt(xT[:, d, :], pair[:, q * T:q * T + T], gate[:, d:d + 1], xT[:, d, :],
                                   ALU.mult, ALU.add)
                    last.then_inc(m["added"], 1)

                def visit(e):
                    def step(i, u, c):
                        g = e * EXPERT_CHUNKS + i * 2 + u
                        if not is_last(e, c):
                            hidden(g + 1, 1 - u, is_first(e, c) and c == 0)
                        if r == 0 and next_layer < len(plan):
                            if c == EXPERT_CHUNKS - 2:
                                mod_parts(next_layer, e, range(KD // 2))
                            if c == EXPERT_CHUNKS - 1:
                                mod_parts(next_layer, e, range(KD // 2, KD))
                        if c in (0, 1) and not is_first(e):
                            add(e - 1, c)
                        if c == 1:
                            if not is_last(e):
                                one_hot(e + 1)
                            stt(put_back, spot_row[:, bass.ds(e, 1), :].rearrange("p a t -> p (a t)"),
                                partition, comb_row[:, bass.ds(e, 1), :].rearrange("p a t -> p (a t)"),
                                ALU.is_equal, ALU.mult).then_inc(m["backs"], 1)
                    expert_chunks(dve, step)

                if r:
                    ts(spot, spot, -float(P), None, ALU.add, ALU.bypass)
                    ts(spot_row, spot_row, -float(P), None, ALU.add, ALU.bypass).then_inc(*m["lower"].step("s"))
                    dve.wait_ge(*m["lower"].at("s", 0))
                else:
                    dve.wait_ge(*moe_act.at("rows", 0))
                one_hot(0)
                hidden(0, 0, True)
                each_expert(dve, visit)
                add(EXPERTS - 1, 0)
                add(EXPERTS - 1, 1)

            def even_mixers(n):
                v = gdn_vec
                hh = [P, NT, HEADS]

                def th(a):
                    return a.rearrange("p (t h) -> p t h", t=NT)

                def after(name):
                    dve.wait_ge(*v.at(name, 0))
                dve.wait_ge(*gdn_pe.at("ab", 0))
                dve.tensor_copy(ab, bank(4, 0, 16).rearrange("p (t e) -> p t e", t=NT)).then_inc(*v.step("ab"))
                after("ab")
                tt(abt[:, :, 4:8], ab[:, :, 4:8], param("gdn_dt_bias_2").unsqueeze(1).to_broadcast(hh), ALU.add)\
                    .then_inc(*v.step("adt"))
                after("adt")
                stt(abt[:, :, 0:4], abt[:, :, 4:8], -1.0, abt[:, :, 4:8], ALU.mult, ALU.max).then_inc(*v.step("aabs"))
                dve.wait_ge(*gdn_act.at("e", 0))
                ts(beta, beta, 1.0, None, ALU.add, ALU.bypass).then_inc(*v.step("b1"))
                after("b1")
                dve.reciprocal(beta, beta).then_inc(*v.step("b2"))
                dve.wait_ge(*gdn_act.at("ln", 0))
                stt(th(gdec), abt[:, :, 4:8], 0.0, abt[:, :, 0:4], ALU.max, ALU.add).then_inc(*v.step("sp"))
                after("sp")
                stt(th(gdec), th(gdec), -1.0, anex.unsqueeze(1).to_broadcast(hh), ALU.mult, ALU.mult)\
                    .then_inc(*v.step("g"))
                after("g")
                dve.tensor_copy(spread[:, 0, :, :], gdec.unsqueeze(2).to_broadcast([P, 8, P]))
                dve.tensor_copy(spread[:, 1, :, :], beta.unsqueeze(2).to_broadcast([P, 8, P]))\
                   .then_inc(*v.step("spread"))
                dve.wait_ge(*gdn_pe.at("gc", 0))
                dve.tensor_copy(gccol, bank(5, 0, 8)).then_inc(*v.step("gcc"))
                after("gcc")
                dve.wait_ge(*gdn_pe.at("grows", 0))
                for m in range(8):
                    ts(dec[:, m * P:m * P + P], pair[:, m * P:m * P + P], gccol[:, m:m + 1], 0.0, ALU.subtract, ALU.min)
                tt(kdf, pair[:, P - 1:8 * P:P], gccol, ALU.subtract).then_inc(*v.step("dd"))
                dve.wait_ge(*gdn_act.at("dec", 0))
                d3, s3 = (a.rearrange("p (m c) -> p m c", m=8) for a in (dec, decs))
                tt(s3, d3, const("before").unsqueeze(1).to_broadcast([P, 8, P]), ALU.mult)
                tt(bege, beta, egc, ALU.mult)
                tt(d3, d3, const("upto").unsqueeze(1).to_broadcast([P, 8, P]), ALU.mult).then_inc(*v.step("dm"))
                w = param("gdn_conv_w_2").rearrange("p (n k) -> p n k", n=12)
                for name, tiles in (("a", range(8)), ("b", range(8, 12))):
                    dve.wait_ge(*proj_act.at("p", proj_before[n] + tiles[-1] // 2))
                    for back in range(4):
                        at = back if name == "a" or back == 0 else back + 3
                        if back:
                            after(f"{name}{at - 1 if back > 1 or name == 'a' else 0}")
                        for j in tiles:
                            x = proj[:, j // 2, j % 2, :]
                            if back == 0:
                                last = ts(qkv[:, j, :], x, w[:, j, 3:4], None, ALU.mult, ALU.bypass)
                            else:
                                last = stt(qkv[:, j, back:T], x[:, 0:T - back], w[:, j, 3 - back:4 - back],
                                           qkv[:, j, back:T], ALU.mult, ALU.add)
                        last.then_inc(*v.step(f"{name}{at}"))
                dve.wait_ge(*gdn_act.at("l2root", 0))
                dve.reciprocal(l2, l2).then_inc(*v.step("l2i"))
                after("l2i")
                r8 = l2.rearrange("p (n t) -> p n t", n=8)
                stt(qkv[:, 0:4, :], qkv[:, 0:4, :], float(P ** -0.5), r8[:, 0:4, :], ALU.mult, ALU.mult)
                tt(qkv[:, 4:8, :], qkv[:, 4:8, :], r8[:, 4:8, :], ALU.mult).then_inc(*v.step("qkn"))
                after("qkn")
                dve.wait_ge(*gdn_pe.at("brows", 0))
                for t in range(NT):
                    tt(kb[:, t, :].rearrange("p (h c) -> p h c", h=4), bank(4 + t).rearrange("p (h c) -> p h c", h=4),
                       qkv[:, 4:8, t * P:t * P + P], ALU.mult).then_inc(*v.step(f"kb{t}"))
                tt(qg.rearrange("p (h c) -> p h c", h=4), qkv[:, 0:4, P:T],
                   egrow.rearrange("p (h c) -> p h c", h=4), ALU.mult).then_inc(*v.step("qg"))
                for t in range(NT):
                    dve.wait_ge(*gdn_pe.at(f"kk{t}", 0))
                    a = t * 512
                    tt(LT[:, t, :], bank(t), decs[:, a:a + 512], ALU.mult)
                    tt(PT[:, t, :], bank(2 + t), dec[:, a:a + 512], ALU.mult).then_inc(*v.step(f"lp{t}"))
                dve.wait_ge(*gdn_pe.at("tr", 0))
                for h in range(HEADS):
                    a = h * P
                    ts(kdec[:, a:a + P], bank(4, a, a + P), kdf[:, h:h + 1], None, ALU.mult, ALU.bypass)
                    last = ts(kbe[:, a:a + P], bank(5, a, a + P), bege[:, 4 + h:5 + h], None, ALU.mult, ALU.bypass)
                last.then_inc(*v.step("kt"))
                dve.wait_ge(*gdn_pool.at("ident", 0))
                levels = const("levels").rearrange("p (l c) -> p l c", l=LEVELS)
                for l in range(LEVELS):
                    for t in range(NT):
                        after("lp1")
                        tt(MT[:, t, :].rearrange("p (h c) -> p h c", h=4), LT[:, t, :].rearrange("p (h c) -> p h c", h=4),
                           levels[:, l, :].unsqueeze(1).to_broadcast([P, 4, P]), ALU.mult).then_inc(*v.step(f"m{l}{t}"))
                    for t in range(NT):
                        dve.wait_ge(*gdn_pe.at(f"z{l}{t}", 0))
                        if l:
                            after(f"x{l - 1}{t}")
                        tt(X[:, t, :], X[:, t, :], bank(2 + t), ALU.subtract)
                        tt(XT[:, t, :], XT[:, t, :], bank(4 + t), ALU.subtract).then_inc(*v.step(f"x{l}{t}"))
                dve.wait_ge(*gdn_act.at("root", 0))
                dve.reciprocal(gorn, gorn).then_inc(*v.step("rn"))
                after("rn")
                tt(gosq, pair[:, :], gorn, ALU.mult).then_inc(*v.step("on"))
                after("on")
                dve.wait_ge(*gdn_act.at("zs", 0))
                stt(yT[:, 0:4, :].rearrange("p h t -> p (h t)"), gosq, param("gdn_norm_2"), zsilu, ALU.mult, ALU.mult)\
                    .then_inc(*v.step("y"))

            def odd_mixers(n):
                ts(qgain, param("att_q_norm_2"), float(P ** -0.5), None, ALU.mult, ALU.bypass)\
                    .then_inc(*gain_vec.step("q"))
                dve.wait_ge(*gain_vec.at("q", 0))

                def normed_qk(q):
                    hp, g, j = q // 6, q % 6 // 2, q % 2
                    dve.wait_ge(*att_act["root"].at("root", q))
                    dve.reciprocal(qrn[:, q % 2, :], qrn[:, q % 2, :]).then_inc(*att_vec["rn"].step("rn"))
                    dve.wait_ge(*att_vec["rn"].at("rn", q))
                    if hp >= 2:
                        dve.wait_ge(*att_pe["scores"].at("scores", 4 * (hp - 1) - 1))
                    stt(qk[:, hp % 2, j, g, :, :].rearrange("p h t -> p (h t)"), qraw[:, q % 2, :],
                        (qgain, param("att_k_norm_2"))[j], qrn[:, q % 2, :], ALU.mult, ALU.mult)\
                        .then_inc(*att_vec["qk"].step("qk"))

                def softmax(u, part):
                    qt, w = u % 2, ATT_GROUPS * (u % 2 + 1) * P
                    slope = 2.0 ** (-8.0 * (u // 2 + 1) / ATT_HEADS)
                    if part == 0:
                        dist = const("distance")[:, 0:384] if qt == 0 else const("distance")[:, 384:1152]
                        dve.wait_ge(*att_pe["scores"].at("scores", u))
                        stt(logit[:, u % 2, 0:w], dist, slope, pair[:, 0:w], ALU.mult, ALU.add)\
                            .then_inc(*att_vec["logit"].step("logit"))
                        dve.wait_ge(*att_vec["logit"].at("logit", u))
                        dve.tensor_reduce(top_q[:, u:u + 1], logit[:, u % 2, 0:w], AX, ALU.max)\
                           .then_inc(*att_vec["top"].step("top"))
                        dve.wait_ge(*att_vec["top"].at("top", u))
                        ts(neg_q[:, u:u + 1], top_q[:, u:u + 1], -1.0, None, ALU.mult, ALU.bypass)\
                            .then_inc(*att_vec["neg"].step("neg"))
                    else:
                        dve.wait_ge(*att_act["exp"].at("exp", u))
                        dve.reciprocal(inv_q[:, u:u + 1], sum_q[:, u:u + 1]).then_inc(*att_vec["inv"].step("inv"))
                        dve.wait_ge(*att_vec["inv"].at("inv", u))
                        ts(prob[:, u % 2, 0:w], prob[:, u % 2, 0:w], inv_q[:, u:u + 1], None, ALU.mult, ALU.bypass)\
                            .then_inc(*att_vec["prob"].step("prob"))

                for hp in range(5):
                    for s in range(9):
                        if hp >= 1 and s % 2 == 0 and s < 8:
                            softmax(4 * (hp - 1) + s // 2, 0)
                            softmax(4 * (hp - 1) + s // 2, 1)
                        if hp < 4 and s % 3 < 2:
                            normed_qk(hp * 6 + s // 3 * 2 + s % 3)

            def out_update(n):
                g = mod_columns(n, 2)
                dve.wait_ge(*mod_rest.at("m", n))
                for s in range(4):
                    dve.wait_ge(weights_used, place[f"out{n}"] + s + 1)
                    for t in range(2):
                        d = 2 * s + t
                        stt(xT[:, d, :], bank(s, t * T, t * T + T), g[:, d:d + 1], xT[:, d, :],
                            ALU.mult, ALU.add).then_inc(*x_vec.step(f"x{d}"))

            def feed_forward(n, kind):
                base, first, chunks = tiles_before[n], place[f"ffn{n}"], chunks_of(kind)
                convolved = kind in ("even", "odd")

                def visit(c, odd):
                    late = not isinstance(c, int) or c >= 2

                    def up_here(j):
                        if j == 0:
                            dve.wait_ge(ffn_half, base // 2 + c + 1)
                        else:
                            dve.wait_ge(weights_used, ff_slot(first, c) + 2)
                    if convolved:
                        layer = LAYER[kind]
                        wa = param_at["ffn_conv_w_2"][0] + layer * FF_TILES * 3
                        ba = param_at["ffn_conv_b_2"][0] + layer * FF_TILES

                        def col(a, per, extra=0):
                            return params[:, bass.ds(c * (2 * per) + (a + extra), 1)]
                        for back in range(3):
                            if back:
                                dve.wait_ge(ffn_conv, conv_before[n] + 2 * c + back)
                            for j in range(2):
                                b = 2 * odd + j
                                if back == 0:
                                    up_here(j)
                                    if late:
                                        dve.wait_ge(ffn_silu, base + 2 * c + j - 3)
                                    last = ts(ff_mid[:, b, :], bank(4 + b, 0, T), col(wa, 3, 3 * j + 2),
                                              col(ba, 1, j), ALU.mult, ALU.add)
                                else:
                                    last = stt(ff_mid[:, b, back:T], bank(4 + b, 0, T - back),
                                               col(wa, 3, 3 * j + 2 - back), ff_mid[:, b, back:T], ALU.mult, ALU.add)
                                if back == 2:
                                    last.then_inc(ffn_mid, 1)
                            if back < 2:
                                last.then_inc(ffn_conv, 1)
                    for j in range(2):
                        b = 2 * odd + j
                        dve.wait_ge(ffn_silu, base + 2 * c + j + 1)
                        if late:
                            dve.wait_ge(weights_used, first + 3 * c - 1)
                        tt(ff_hid[:, b, :], bank(4 + b, T, 2 * T), ff_silu[:, b, :], ALU.mult)
                        tt(hid_high[:, b, :], bank(4 + b, T, 2 * T), ff_silu[:, b, :], ALU.mult)\
                            .then_inc(ffn_full, 1)
                    for j in range(2):
                        b = 2 * odd + j
                        dve.wait_ge(ffn_full, base + 2 * c + j + 1)
                        tt(ff_hid_r[:, b, :], ff_hid[:, b, :], f32(hid_high[:, b, :]), ALU.subtract).then_inc(ffn_hid, 1)
                    if n + 1 < len(plan) and not isinstance(c, int):
                        mod_parts(n + 1, c - 2, range(KD))

                each_chunk(dve, chunks, visit)
                g = mod_columns(n, 5)
                for d in range(KD):
                    if d < 6:
                        dve.wait_ge(ffn_out, 3 * sum(k != "first1" for k in plan[:n]) + d // 2 + 1)
                    else:
                        dve.wait_ge(weights_used, first + 3 * chunks)
                    stt(xT[:, d, :], bank(d // 2, d % 2 * T, d % 2 * T + T), g[:, d:d + 1], xT[:, d, :],
                        ALU.mult, ALU.add).then_inc(*x_vec.step(f"x{d}"))

            dve.wait_ge(params_here, 16)
            lower_bounds()
            dve.wait_ge(*cond_act.at("cond", 0))
            for start in range(0, MOD_LEAD, 2):
                group = range(start, start + 2)
                dve.wait_ge(lead_here[start // 2], 32)
                accumulate(0, [lead_ring[:, s, :, :] for s in group], [lead_acc[:, s, :] for s in group], range(KD),
                           group[0] * KD)
            for n, kind in enumerate(plan):
                modulation_lead(n)
                norm(n, 0)
                if n == 0:
                    dve.wait_ge(consts_here, 16)
                if n:
                    modulation_rest(n)
                if kind.startswith("first"):
                    first_mixers(firsts.index(n))
                    if n == 0:
                        modulation_rest(0)
                elif kind == "even":
                    even_mixers(n)
                else:
                    odd_mixers(n)
                out_update(n)
                norm(n, 1)
                if kind == "first1":
                    router(n)
                    experts(0)
                    with dve.If(more_tokens(dve)):
                        experts(1)
                    dve.wait_ge(passes[0]["added"], 2 * EXPERTS)
                    dve.tensor_copy(den, top).then_inc(x_vec.sem, KD)
                    x_vec.count += KD
                    norm(n, 2)
                else:
                    feed_forward(n, kind)


def column_slots(w, first=0, last=None):
    w = w[:, first:last]
    return w.reshape(KD, P, w.shape[1] // COLS, COLS).transpose(2, 1, 0, 3).reshape(-1, P, SLOT)


def row_slots(w):
    return w.reshape(w.shape[0] // COLS, 2, P, D).transpose(0, 2, 1, 3).reshape(-1, P, SLOT)


def columns(v):
    return np.asarray(v).reshape(-1, P).T


def lay_stream(a, plan):
    place = stream_plan(plan)
    stream = np.empty((place["all"], P, SLOT), np.float32)

    def put(at, slots):
        stream[at:at + len(slots)] = slots
    mods = {"first0": ("w_ada", 0), "first1": ("w_ada", 1), "even": ("ada_w_2", 0), "odd": ("ada_w_2", 1)}
    at_mod = [np.asarray(a[mods[k][0]][mods[k][1]]) for k in plan]
    lead = column_slots(at_mod[0])
    put(place["mod0"], lead[:MOD_LEAD])
    put(place["mod_rest"], lead[MOD_LEAD:])
    for n, kind in enumerate(plan):
        if n:
            put(place[f"mod{n}"], column_slots(at_mod[n]))
        at = place[f"in{n}"]
        layer = 1 if kind in ("first1", "odd") else 0
        if kind.startswith("first"):
            w = a["w_in"][layer]
            for s in range(12):
                put(at + s, column_slots(w, COLUMN_OF[s], COLUMN_OF[s] + COLS))
            put(place[f"out{n}"], column_slots(a["w_out"][layer]))
        elif kind == "even":
            w = a["ev_w_in_2"][0]
            put(at, column_slots(w, 0, 2048))
            put(at + 8, column_slots(w, 2056, 2568))
            put(place[f"out{n}"], column_slots(a["ev_w_out_2"][0]))
        else:
            w = a["od_w_in_2"][0]
            for hp in range(ATT_HEADS // 2):
                for s in range(9):
                    c = s * D + hp * COLS
                    put(at + hp * 9 + s, column_slots(w, c, c + COLS))
            put(place[f"out{n}"], column_slots(a["od_w_out_2"][0]))
        at = place[f"ffn{n}"]
        if kind == "first0":
            experts = [(a["ffn_w1"][0], a["ffn_w3"][0], a["ffn_w2"][0])]
        elif kind == "first1":
            experts = [(a["moe_w1"][0][e], a["moe_w3"][0][e], a["moe_w2"][0][e]) for e in range(EXPERTS)]
        else:
            up = a["ffn_w_up_2"][layer]
            experts = [(up[:, 0:D_FF], up[:, D_FF:], a["ffn_w_down_2"][layer])]
        chunks = sum(w1.shape[1] // COLS for w1, _, _ in experts)
        c = 0
        for w1, w3, w2 in experts:
            w1, w3, w2 = column_slots(w1), column_slots(w3), row_slots(w2)
            for i in range(len(w1)):
                up = at if c == 0 else at - 1 + 3 * c
                if kind == "first1":
                    both = np.concatenate([w.reshape(P, KD, COLS) for w in (w1[i], w3[i])], 2)
                    stream[up:up + 2] = both.reshape(P, 2, SLOT).transpose(1, 0, 2)
                else:
                    stream[up], stream[up + 1] = w1[i], w3[i]
                stream[at + 3 * chunks - 1 if c == chunks - 1 else at + 4 + 3 * c] = w2[i]
                c += 1
    return stream


def lay_params(a, plan):
    def rows(v):
        return np.broadcast_to(np.asarray(v).reshape(1, -1), (P, np.asarray(v).size))

    def padded(v):
        return np.concatenate([v, np.zeros((P - v.shape[0], v.shape[1]), v.dtype)])

    def per_k(w):
        return w.reshape(KD, P, -1).transpose(1, 0, 2).reshape(P, -1)
    both = range(2)
    mods = {"first0": ("b_ada", 0), "first1": ("b_ada", 1), "even": ("ada_b_2", 0), "odd": ("ada_b_2", 1)}
    b_mod = [columns(a[mods[k][0]][mods[k][1]]) for k in plan]
    b_mod += [np.zeros((P, MODS), np.float32)] * (4 - len(plan))
    out = {
        "c": columns(a["c"]), "c_2": columns(a["c_2"]), "b_mod": np.concatenate(b_mod, 1),
        "conv_w": np.concatenate([a["conv_w"][l].reshape(3, 2, P).transpose(2, 1, 0).reshape(P, 6) for l in both], 1),
        "sgu_norm_g": rows(a["sgu_norm_g"]),
        "sgu_w": np.concatenate([a["sgu_w"][l].transpose(2, 0, 1).reshape(P, 512) for l in both], 1),
        "sgu_b": np.concatenate([np.repeat(a["sgu_b"][l].reshape(2, 2, P).transpose(1, 0, 2), 64, axis=0)
                                 .reshape(P, 256) for l in both], 1),
        "w_glow": np.concatenate([per_k(a["w_in"][l][:, GLOW_COLUMN:GLOW_COLUMN + 16]) for l in both], 1),
        "gla_w_gate": np.concatenate([padded(a["gla_w_gate"][l]) for l in both], 1),
        "gla_norm_g": np.concatenate([a["gla_norm_g"].T] * 2), "hgrn_norm_g": np.concatenate([a["hgrn_norm_g"].T] * 2),
        "moe_router": per_k(a["moe_router"][0]), "w_ab": per_k(a["ev_w_in_2"][0][:, 2048:2056]),
        "gdn_conv_w_2": a["gdn_conv_w_2"][0].reshape(4, 12, P).transpose(2, 1, 0).reshape(P, 48),
        "gdn_a_log_2": rows(a["gdn_a_log_2"][0]), "gdn_dt_bias_2": rows(a["gdn_dt_bias_2"][0]),
        "pool_w_2": a["pool_w_2"][0].transpose(1, 0, 2).reshape(P, 512),
        "ffn_conv_w_2": np.concatenate([a["ffn_conv_w_2"][l].reshape(3, FF_TILES, P).transpose(2, 1, 0)
                                        .reshape(P, -1) for l in both], 1),
    }
    for name in PARAM_COLUMNS:
        if name not in out:
            out[name] = columns(a[name])
    assert {k: out[k].shape[1] for k in PARAM_COLUMNS} == PARAM_COLUMNS
    return np.ascontiguousarray(np.concatenate([out[k] for k in PARAM_COLUMNS], 1))


def lay_out(a, plan):
    return {
        "x_dram": np.ascontiguousarray(a["x"][0].reshape(T, KD, P).transpose(2, 1, 0)),
        "params_dram": lay_params(a, plan),
        "consts_dram": np.concatenate(list(constant_columns().values()), 1),
        "stream_dram": lay_stream(a, plan),
    }


def make(nc, arrays, plan):
    args = [nc.dram_tensor(k, v.shape, F32, kind="ExternalInput").ap() for k, v in arrays.items()]
    args.append(nc.dram_tensor("out_dram", (P, KD, T), F32, kind="ExternalOutput").ap())
    build_program(nc, *args, plan=plan)


def kernel(**inputs):
    import concourse.bacc as bacc
    from concourse.bass_utils import run_bass_kernel_spmd

    arrays = lay_out({k: np.asarray(v) for k, v in inputs.items()}, PLAN)
    nc = bacc.Bacc("TRN2", target_bir_lowering=False, num_devices=1)
    make(nc, arrays, PLAN)
    got = run_bass_kernel_spmd(nc, [arrays], core_ids=[0]).results[0]["out_dram"]
    return np.ascontiguousarray(got.transpose(2, 1, 0)).reshape(1, T, D)
```
